# Optimizing a Trainium2 kernel written in Bass

```python
import math
import jax, jax.numpy as jnp
from jax import lax
import numpy as np
import jax
import jax.numpy as jnp

D_MODEL = 1024
BATCH = 1
SEQ = 256
DEPTH = 2

N_MIXERS = 3
BLOCK = 128
EPS = 1e-6
NEG = -1e30

SB_HEADS = 16
SB_HEAD_DIM = 64

DIL_GROUPS = ((128, 1), (512, 4), (2048, 16))
DIL_HEADS = 8
DIL_HEAD_DIM = 64
N_BUCKETS = 32
BUCKET_MAX_DIST = 2048

MLA_HEADS = 16
MLA_Q_RANK = 384
MLA_KV_RANK = 256
MLA_NOPE = 64
MLA_ROPE = 32
MLA_V = 64
ROPE_THETA = 10000.0

D_FF = 2816
CONV_W = 3


def rms_norm(x, g):
    xf = x.astype(jnp.float32)
    y = xf * lax.rsqrt(jnp.mean(xf * xf, axis=-1, keepdims=True) + EPS)
    return (y * g.astype(jnp.float32)).astype(x.dtype)

def t5_bucket(dist):
    dist = jnp.maximum(dist, 0)
    max_exact = N_BUCKETS // 2
    d = jnp.maximum(dist.astype(jnp.float32), 1.0)
    large = max_exact + (jnp.log(d / max_exact) / math.log(BUCKET_MAX_DIST / max_exact)
                         * (N_BUCKETS - max_exact)).astype(jnp.int32)
    large = jnp.minimum(large, N_BUCKETS - 1)
    return jnp.where(dist < max_exact, dist, large)

def stick_breaking_attention(xn, w_qkv, w_o):
    B, S, _ = xn.shape
    H, dh = SB_HEADS, SB_HEAD_DIM
    qkv = (xn @ w_qkv).reshape(B, S, 3, H, dh)
    q, k, v = qkv[:, :, 0], qkv[:, :, 1], qkv[:, :, 2]
    nb = S // BLOCK
    qb = q.reshape(B, nb, BLOCK, H, dh).transpose(1, 0, 3, 2, 4)
    kt = k.transpose(0, 2, 1, 3)
    vt = v.transpose(0, 2, 1, 3)
    key_pos = jnp.arange(S)
    scale = dh ** -0.5

    def one_block(args):
        q_blk, n = args
        z = jnp.einsum('bhqd,bhkd->bhqk', q_blk, kt).astype(jnp.float32) * scale
        q_pos = n * BLOCK + jnp.arange(BLOCK)
        mask = key_pos[None, :] < q_pos[:, None]
        log_not = jnp.where(mask, jax.nn.log_sigmoid(-z), 0.0)
        between = lax.cumsum(log_not, axis=3, reverse=True) - log_not
        a = jnp.where(mask, jnp.exp(jax.nn.log_sigmoid(z) + between), 0.0)
        return jnp.einsum('bhqk,bhkd->bhqd', a.astype(vt.dtype), vt)

    o = lax.map(one_block, (qb, jnp.arange(nb)))
    o = o.transpose(1, 0, 3, 2, 4).reshape(B, S, H * dh)
    return o @ w_o

def strided_window_attention(q, k, v, dilation, n_back, bias_g):
    B, S, Hg, dh = q.shape
    r, W = dilation, n_back
    L = S // r

    def to_sub(a):
        return a.reshape(B, L, r, Hg, dh).transpose(0, 2, 3, 1, 4)

    qs, ks, vs = to_sub(q), to_sub(k), to_sub(v)
    Lp = -(-L // W) * W
    nb = Lp // W
    pad = Lp - L
    qs = jnp.pad(qs, ((0, 0), (0, 0), (0, 0), (0, pad), (0, 0)))
    kp = jnp.pad(ks, ((0, 0), (0, 0), (0, 0), (W, pad), (0, 0)))
    vp = jnp.pad(vs, ((0, 0), (0, 0), (0, 0), (W, pad), (0, 0)))
    q_blk = qs.reshape(B, r, Hg, nb, W, dh)
    k_blk = jnp.concatenate([kp[:, :, :, :Lp].reshape(B, r, Hg, nb, W, dh),
                             kp[:, :, :, W:].reshape(B, r, Hg, nb, W, dh)], axis=4)
    v_blk = jnp.concatenate([vp[:, :, :, :Lp].reshape(B, r, Hg, nb, W, dh),
                             vp[:, :, :, W:].reshape(B, r, Hg, nb, W, dh)], axis=4)
    i = jnp.arange(W)[:, None]
    j = jnp.arange(2 * W)[None, :]
    m = i + W - j
    key_abs = jnp.arange(nb)[:, None, None] * W - W + j[None]
    mask = (m >= 0)[None] & (m <= n_back)[None] & (key_abs >= 0)
    bias = bias_g[t5_bucket(m * r)].astype(jnp.float32).transpose(2, 0, 1)
    s = jnp.einsum('brhnqd,brhnkd->brhnqk', q_blk, k_blk).astype(jnp.float32) * (dh ** -0.5)
    s = jnp.where(mask[None, None, None], s + bias[None, None, :, None], NEG)
    lse = jax.nn.logsumexp(s, axis=-1)
    p = jnp.exp(s - lse[..., None])
    o = jnp.einsum('brhnqk,brhnkd->brhnqd', p.astype(v_blk.dtype), v_blk)
    o = o.reshape(B, r, Hg, Lp, dh)[:, :, :, :L].transpose(0, 3, 1, 2, 4).reshape(B, S, Hg, dh)
    lse = lse.reshape(B, r, Hg, Lp)[:, :, :, :L].transpose(0, 3, 1, 2).reshape(B, S, Hg)
    return o, lse

def dilated_attention(xn, w_qkv, w_o, rel_bias):
    B, S, _ = xn.shape
    G, Hg, dh = len(DIL_GROUPS), DIL_HEADS, DIL_HEAD_DIM
    qkv = (xn @ w_qkv).reshape(B, S, 3, G, Hg, dh)
    outs, lses = [], []
    for g, (window, dilation) in enumerate(DIL_GROUPS):
        o, lse = strided_window_attention(qkv[:, :, 0, g], qkv[:, :, 1, g], qkv[:, :, 2, g],
                                          dilation, window // dilation,
                                          rel_bias[:, g * Hg:(g + 1) * Hg])
        outs.append(o)
        lses.append(lse)
    outs = jnp.stack(outs)
    wts = jax.nn.softmax(jnp.stack(lses), axis=0)
    o = jnp.einsum('gbshd,gbsh->bshd', outs, wts.astype(outs.dtype)).reshape(B, S, Hg * dh)
    return o @ w_o

def apply_rope(x, positions):
    half = x.shape[-1] // 2
    freqs = ROPE_THETA ** (-jnp.arange(half, dtype=jnp.float32) / half)
    ang = positions.astype(jnp.float32)[:, :, None, None] * freqs
    cos, sin = jnp.cos(ang).astype(x.dtype), jnp.sin(ang).astype(x.dtype)
    x1, x2 = x[..., :half], x[..., half:]
    return jnp.concatenate([x1 * cos - x2 * sin, x2 * cos + x1 * sin], axis=-1)

def causal_softmax_blocks(q, k, v, scale):
    B, S, H, dq = q.shape
    nb = S // BLOCK
    qb = q.reshape(B, nb, BLOCK, H, dq).transpose(1, 0, 3, 2, 4)
    kt = k.transpose(0, 2, 1, 3)
    vt = v.transpose(0, 2, 1, 3)
    key_pos = jnp.arange(S)

    def one_block(args):
        q_blk, n = args
        s = jnp.einsum('bhqd,bhkd->bhqk', q_blk, kt).astype(jnp.float32) * scale
        q_pos = n * BLOCK + jnp.arange(BLOCK)
        s = jnp.where(key_pos[None, :] <= q_pos[:, None], s, NEG)
        p = jax.nn.softmax(s, axis=-1)
        return jnp.einsum('bhqk,bhkd->bhqd', p.astype(vt.dtype), vt)

    o = lax.map(one_block, (qb, jnp.arange(nb)))
    return o.transpose(1, 0, 3, 2, 4).reshape(B, S, H, v.shape[-1])

def latent_attention(xn, positions, w_in, q_norm, w_qb, kv_norm, w_kvb, w_o):
    B, S, _ = xn.shape
    H = MLA_HEADS
    h = xn @ w_in
    c_q = h[..., :MLA_Q_RANK]
    c_kv = h[..., MLA_Q_RANK:MLA_Q_RANK + MLA_KV_RANK]
    k_rope = h[..., MLA_Q_RANK + MLA_KV_RANK:][:, :, None, :]
    q = (rms_norm(c_q, q_norm) @ w_qb).reshape(B, S, H, MLA_NOPE + MLA_ROPE)
    kv = (rms_norm(c_kv, kv_norm) @ w_kvb).reshape(B, S, H, MLA_NOPE + MLA_V)
    q_rope = apply_rope(q[..., MLA_NOPE:], positions)
    k_rope = apply_rope(k_rope, positions)
    q_full = jnp.concatenate([q[..., :MLA_NOPE], q_rope], axis=-1)
    k_full = jnp.concatenate([kv[..., :MLA_NOPE],
                              jnp.broadcast_to(k_rope, (B, S, H, MLA_ROPE))], axis=-1)
    o = causal_softmax_blocks(q_full, k_full, kv[..., MLA_NOPE:], (MLA_NOPE + MLA_ROPE) ** -0.5)
    return o.reshape(B, S, H * MLA_V) @ w_o

def conv_ffn(xn, w_up, conv_w, conv_b, w_down):
    h = xn @ w_up
    C = h.shape[-1]
    h = lax.conv_general_dilated(h, conv_w[:, None, :], window_strides=(1,),
                                 padding=[(CONV_W - 1, 0)],
                                 dimension_numbers=('NWC', 'WIO', 'NWC'),
                                 feature_group_count=C) + conv_b
    g, u = h[..., :D_FF], h[..., D_FF:]
    return (jax.nn.silu(g) * u) @ w_down

def first_inputs(seed: int = 0) -> dict:
    key = jax.random.key(seed)
    ks = iter(jax.random.split(key, 32))
    n_a = len(range(0, DEPTH, N_MIXERS))
    n_b = len(range(1, DEPTH, N_MIXERS))
    n_c = len(range(2, DEPTH, N_MIXERS))
    G = len(DIL_GROUPS)

    def w(shape, fan_in):
        return jax.random.normal(next(ks), shape, jnp.float32) * fan_in ** -0.5

    def gain(shape):
        return 1.0 + 0.05 * jax.random.normal(next(ks), shape, jnp.float32)

    return {
        'x': jax.random.normal(next(ks), (BATCH, SEQ, D_MODEL), jnp.float32),
        'positions': jnp.broadcast_to(jnp.arange(SEQ, dtype=jnp.int32), (BATCH, SEQ)),
        'rel_bias': 0.5 * jax.random.normal(next(ks), (N_BUCKETS, G * DIL_HEADS), jnp.float32),
        'norm_gains': gain((DEPTH, 4, D_MODEL)),
        'sb_w_qkv': w((n_a, D_MODEL, 3 * SB_HEADS * SB_HEAD_DIM), D_MODEL),
        'sb_w_o': w((n_a, SB_HEADS * SB_HEAD_DIM, D_MODEL), SB_HEADS * SB_HEAD_DIM),
        'dil_w_qkv': w((n_b, D_MODEL, 3 * G * DIL_HEADS * DIL_HEAD_DIM), D_MODEL),
        'dil_w_o': w((n_b, DIL_HEADS * DIL_HEAD_DIM, D_MODEL), DIL_HEADS * DIL_HEAD_DIM),
        'mla_w_in': w((n_c, D_MODEL, MLA_Q_RANK + MLA_KV_RANK + MLA_ROPE), D_MODEL),
        'mla_q_norm': gain((n_c, MLA_Q_RANK)),
        'mla_w_qb': w((n_c, MLA_Q_RANK, MLA_HEADS * (MLA_NOPE + MLA_ROPE)), MLA_Q_RANK),
        'mla_kv_norm': gain((n_c, MLA_KV_RANK)),
        'mla_w_kvb': w((n_c, MLA_KV_RANK, MLA_HEADS * (MLA_NOPE + MLA_V)), MLA_KV_RANK),
        'mla_w_o': w((n_c, MLA_HEADS * MLA_V, D_MODEL), MLA_HEADS * MLA_V),
        'ffn_w_up': w((DEPTH, D_MODEL, 2 * D_FF), D_MODEL),
        'ffn_conv_w': w((DEPTH, CONV_W, 2 * D_FF), CONV_W),
        'ffn_conv_b': 0.02 * jax.random.normal(next(ks), (DEPTH, 2 * D_FF), jnp.float32),
        'ffn_w_down': w((DEPTH, D_FF, D_MODEL), D_FF),
    }

def first_block(x, positions, rel_bias, norm_gains, sb_w_qkv, sb_w_o, dil_w_qkv, dil_w_o,
              mla_w_in, mla_q_norm, mla_w_qb, mla_kv_norm, mla_w_kvb, mla_w_o,
              ffn_w_up, ffn_conv_w, ffn_conv_b, ffn_w_down):
    for i in range(DEPTH):
        kind, j = i % N_MIXERS, i // N_MIXERS
        hn = rms_norm(x, norm_gains[i, 0])
        if kind == 0:
            m = stick_breaking_attention(hn, sb_w_qkv[j], sb_w_o[j])
        elif kind == 1:
            m = dilated_attention(hn, dil_w_qkv[j], dil_w_o[j], rel_bias)
        else:
            m = latent_attention(hn, positions, mla_w_in[j], mla_q_norm[j], mla_w_qb[j],
                                 mla_kv_norm[j], mla_w_kvb[j], mla_w_o[j])
        x = x + rms_norm(m, norm_gains[i, 1])
        f = conv_ffn(rms_norm(x, norm_gains[i, 2]), ffn_w_up[i], ffn_conv_w[i],
                     ffn_conv_b[i], ffn_w_down[i])
        x = x + rms_norm(f, norm_gains[i, 3])
    return x


GRID_W = 64
CTX_LEN = 256
BRANCH_W = 512
NA_HEADS = 8
NA_DH = BRANCH_W // NA_HEADS
NA_WIN_R = 8
NA_WIN_C = 16
DA_HEADS = 4
DA_DH = 64
DA_VD = 2 * DA_DH
DA_QK = DA_HEADS * 2 * DA_DH
GM_GROUPS = 4
GM_CHUNK = 128
GM_GW = BRANCH_W // GM_GROUPS
N_BRANCH = 3
N_EXPERTS = 16
EC_CAPACITY = 2
EXPERT_FF = 1024
Q_BLOCK = 128
ROPE_AXIS = DA_DH // 2
N_MOD = 6
KV_SIZES = (BRANCH_W, BRANCH_W, DA_QK, DA_HEADS * DA_VD)
Q_SIZES = (BRANCH_W, DA_QK, BRANCH_W, BRANCH_W, N_BRANCH * D_MODEL)
KV_COLS = sum(KV_SIZES)
PROJ_COLS = KV_COLS + sum(Q_SIZES)


def _split(z, sizes):
    offs = np.cumsum(sizes)[:-1].tolist()
    return jnp.split(z, offs, axis=-1)

def rmsnorm(x, g):
    xf = x.astype(jnp.float32)
    y = xf * lax.rsqrt(jnp.mean(xf * xf, axis=-1, keepdims=True) + EPS)
    return y.astype(x.dtype) * g

def layernorm(x, g, b):
    xf = x.astype(jnp.float32)
    mu = jnp.mean(xf, axis=-1, keepdims=True)
    var = jnp.mean(jnp.square(xf - mu), axis=-1, keepdims=True)
    return ((xf - mu) * lax.rsqrt(var + EPS)).astype(x.dtype) * g + b

def modulate(h, shift, scale):
    return h * (1 + scale) + shift

def rope_tables(n):
    t = jnp.arange(n)
    inv = ROPE_THETA ** (-jnp.arange(0, ROPE_AXIS, 2, dtype=jnp.float32) / ROPE_AXIS)
    ang_r = (t // GRID_W).astype(jnp.float32)[:, None] * inv
    ang_c = (t % GRID_W).astype(jnp.float32)[:, None] * inv
    return (jnp.cos(ang_r), jnp.sin(ang_r), jnp.cos(ang_c), jnp.sin(ang_c))

def _rot(x, cos, sin):
    x1, x2 = jnp.split(x, 2, axis=-1)
    return jnp.concatenate([x1 * cos - x2 * sin, x1 * sin + x2 * cos], axis=-1)

def rope_2d(x, tabs):
    cr, sr, cc, sc = [t.astype(x.dtype)[None, :, None, None, :] for t in tabs]
    xr, xcol = jnp.split(x, 2, axis=-1)
    return jnp.concatenate([_rot(xr, cr, sr), _rot(xcol, cc, sc)], axis=-1)

def dense_attn(q, k, v):
    B, n, H, dh = q.shape
    s = jnp.einsum('bqhd,bkhd->bhqk', q, k) * (dh ** -0.5)
    p = jax.nn.softmax(s.astype(jnp.float32), axis=-1).astype(v.dtype)
    return jnp.einsum('bhqk,bkhd->bqhd', p, v).reshape(B, n, H * dh)

def neighbourhood_attn(q, k, v, kc, vc, rpb):
    B, L, H, dh = q.shape
    Lc = kc.shape[1]
    rows = L // GRID_W
    wr = min(NA_WIN_R, rows)
    scale = dh ** -0.5
    kg = k.reshape(B, rows, GRID_W, H, dh)
    vg = v.reshape(B, rows, GRID_W, H, dh)
    qg = jnp.moveaxis(q.reshape(B, rows, GRID_W, H, dh), 1, 0)
    col = jnp.arange(GRID_W)
    col_start = jnp.clip(col - NA_WIN_C // 2, 0, GRID_W - NA_WIN_C)
    col_idx = col_start[:, None] + jnp.arange(NA_WIN_C)[None, :]
    dc = col_idx - col[:, None] + (NA_WIN_C - 1)

    def row_block(args):
        r, qr = args
        r0 = jnp.clip(r - wr // 2, 0, rows - wr)
        kw = lax.dynamic_slice_in_dim(kg, r0, wr, axis=1)[:, :, col_idx]
        vw = lax.dynamic_slice_in_dim(vg, r0, wr, axis=1)[:, :, col_idx]
        dr = r0 + jnp.arange(wr) - r + (NA_WIN_R - 1)
        bias = jnp.transpose(rpb[:, dr[:, None, None], dc[None]], (0, 2, 1, 3))
        s_loc = jnp.einsum('bqhd,brqjhd->bhqrj', qr, kw) * scale + bias[None]
        s_ctx = jnp.einsum('bqhd,bchd->bhqc', qr, kc) * scale
        s = jnp.concatenate([s_ctx, s_loc.reshape(B, H, GRID_W, wr * NA_WIN_C)], axis=-1)
        p = jax.nn.softmax(s.astype(jnp.float32), axis=-1).astype(v.dtype)
        p_loc = p[..., Lc:].reshape(B, H, GRID_W, wr, NA_WIN_C)
        return (jnp.einsum('bhqc,bchd->bqhd', p[..., :Lc], vc)
                + jnp.einsum('bhqrj,brqjhd->bqhd', p_loc, vw))

    out = lax.map(row_block, (jnp.arange(rows), qg))
    return jnp.moveaxis(out, 0, 1).reshape(B, L, H * dh)

def diff_attend(q, k, v, lam):
    s = jnp.einsum('bqhcd,bkhcd->bhcqk', q, k) * (q.shape[-1] ** -0.5)
    p = jax.nn.softmax(s.astype(jnp.float32), axis=-1)
    a = (p[:, :, 0] - lam * p[:, :, 1]).astype(v.dtype)
    return jnp.einsum('bhqk,bkhd->bqhd', a, v)

def diff_attn_blocks(q, k, v, lam):
    B, L, H, _, dh = q.shape
    nb = L // Q_BLOCK
    qblk = jnp.moveaxis(q.reshape(B, nb, Q_BLOCK, H, 2, dh), 1, 0)
    out = lax.map(lambda qb: diff_attend(qb, k, v, lam), qblk)
    return jnp.moveaxis(out, 0, 1).reshape(B, L, H, v.shape[-1])

def diff_head_norm(o, g, lam_init):
    B, n = o.shape[:2]
    return (rmsnorm(o, g) * (1.0 - lam_init)).reshape(B, n, -1)

def gmlp_gate(u, v, ln_g, ln_b, w_s, b_s):
    B, n, _ = u.shape
    vn = layernorm(v, ln_g, ln_b).reshape(B, n // GM_CHUNK, GM_CHUNK, GM_GROUPS, GM_GW)
    mixed = jnp.einsum('gpq,bnqgc->bnpgc', w_s, vn) + jnp.swapaxes(b_s, 0, 1)[:, :, None]
    return u * mixed.reshape(B, n, BRANCH_W)

def branch_merge(ya, yb, yc, gates, w_branch, w_out):
    ga, gb, gc = jnp.split(jax.nn.sigmoid(gates), N_BRANCH, axis=-1)
    m = ga * (ya @ w_branch[0]) + gb * (yb @ w_branch[1]) + gc * (yc @ w_branch[2])
    return m @ w_out

def ec_moe(h, w_r, w1, w3, w2):
    B, n, D = h.shape
    cap = max(1, EC_CAPACITY * n // N_EXPERTS)
    aff = jax.nn.softmax((h @ w_r).astype(jnp.float32), axis=-1)
    gate, idx = lax.top_k(jnp.swapaxes(aff, 1, 2), cap)
    xin = jax.vmap(lambda hb, ib: hb[ib])(h, idx)
    hid = jax.nn.silu(jnp.einsum('becd,edf->becf', xin, w1)) * jnp.einsum('becd,edf->becf', xin, w3)
    ye = jnp.einsum('becf,efd->becd', hid, w2) * gate[..., None].astype(h.dtype)
    return jax.vmap(lambda yb, ib: jnp.zeros((n, D), h.dtype).at[ib.reshape(-1)].add(yb.reshape(-1, D)))(ye, idx)

def _na_heads(t):
    return t.reshape(t.shape[0], t.shape[1], NA_HEADS, NA_DH)

def _da_qk(t):
    return t.reshape(t.shape[0], t.shape[1], DA_HEADS, 2, DA_DH)

def _da_v(t):
    return t.reshape(t.shape[0], t.shape[1], DA_HEADS, DA_VD)

def second_inputs(seed: int = 0) -> dict:
    key = jax.random.key(seed)
    ks = jax.random.split(key, 32)
    f32 = jnp.float32

    def nrm(k, shape, scale):
        return jax.random.normal(k, shape, f32) * scale

    D = D_MODEL
    return {
        "x": nrm(ks[0], (BATCH, SEQ, D), 1.0),
        "c": nrm(ks[1], (BATCH, D), 1.0),
        "ctx": nrm(ks[2], (BATCH, CTX_LEN, D), 1.0),
        "c_ctx": nrm(ks[3], (D,), 1.0),
        "w_ada": nrm(ks[4], (DEPTH, D, N_MOD * D), 0.5 * D ** -0.5),
        "b_ada": nrm(ks[5], (DEPTH, N_MOD * D), 0.02),
        "g_norm1": 1.0 + nrm(ks[6], (DEPTH, D), 0.05),
        "g_norm2": 1.0 + nrm(ks[7], (DEPTH, D), 0.05),
        "w_in": nrm(ks[8], (DEPTH, D, PROJ_COLS), D ** -0.5),
        "na_rpb": nrm(ks[9], (DEPTH, NA_HEADS, 2 * NA_WIN_R - 1, 2 * NA_WIN_C - 1), 0.1),
        "da_lam_q1": nrm(ks[10], (DEPTH, DA_DH), 0.1),
        "da_lam_k1": nrm(ks[11], (DEPTH, DA_DH), 0.1),
        "da_lam_q2": nrm(ks[12], (DEPTH, DA_DH), 0.1),
        "da_lam_k2": nrm(ks[13], (DEPTH, DA_DH), 0.1),
        "da_subln_g": 1.0 + nrm(ks[14], (DEPTH, DA_VD), 0.05),
        "gm_ln_g": 1.0 + nrm(ks[15], (DEPTH, BRANCH_W), 0.05),
        "gm_ln_b": nrm(ks[16], (DEPTH, BRANCH_W), 0.02),
        "gm_w_s": nrm(ks[17], (DEPTH, GM_GROUPS, GM_CHUNK, GM_CHUNK), GM_CHUNK ** -0.5),
        "gm_b_s": 1.0 + nrm(ks[18], (DEPTH, GM_GROUPS, GM_CHUNK), 0.1),
        "w_branch": nrm(ks[19], (DEPTH, N_BRANCH, BRANCH_W, D), BRANCH_W ** -0.5),
        "w_out": nrm(ks[20], (DEPTH, D, D), D ** -0.5),
        "w_router": nrm(ks[21], (DEPTH, D, N_EXPERTS), D ** -0.5),
        "w_e1": nrm(ks[22], (DEPTH, N_EXPERTS, D, EXPERT_FF), D ** -0.5),
        "w_e3": nrm(ks[23], (DEPTH, N_EXPERTS, D, EXPERT_FF), D ** -0.5),
        "w_e2": nrm(ks[24], (DEPTH, N_EXPERTS, EXPERT_FF, D), EXPERT_FF ** -0.5),
        "g_final": 1.0 + nrm(ks[25], (D,), 0.05),
    }

def second_block(x, c, ctx, c_ctx, w_ada, b_ada, g_norm1, g_norm2, w_in, na_rpb,
              da_lam_q1, da_lam_k1, da_lam_q2, da_lam_k2, da_subln_g,
              gm_ln_g, gm_ln_b, gm_w_s, gm_b_s, w_branch, w_out,
              w_router, w_e1, w_e3, w_e2, g_final):
    L = x.shape[1]
    tabs = rope_tables(L)
    xc = ctx
    for i in range(DEPTH):
        last = i == DEPTH - 1
        mod = jax.nn.silu(c) @ w_ada[i] + b_ada[i]
        sh1, sc1, gt1, sh2, sc2, gt2 = jnp.split(mod[:, None, :], N_MOD, axis=-1)
        modc = jax.nn.silu(c_ctx) @ w_ada[i] + b_ada[i]
        sh1c, sc1c, gt1c, sh2c, sc2c, gt2c = jnp.split(modc, N_MOD, axis=-1)
        lam_init = 0.8 - 0.6 * math.exp(-0.3 * i)
        lam = (jnp.exp(jnp.sum(da_lam_q1[i].astype(jnp.float32) * da_lam_k1[i].astype(jnp.float32)))
               - jnp.exp(jnp.sum(da_lam_q2[i].astype(jnp.float32) * da_lam_k2[i].astype(jnp.float32)))
               + lam_init)

        h = modulate(rmsnorm(x, g_norm1[i]), sh1, sc1)
        hc = modulate(rmsnorm(xc, g_norm1[i]), sh1c, sc1c)
        ka, va, kb, vb, qa, qb, u, v, gates = _split(h @ w_in[i], KV_SIZES + Q_SIZES)
        if last:
            kac, vac, kbc, vbc = _split(hc @ w_in[i][:, :KV_COLS], KV_SIZES)
        else:
            kac, vac, kbc, vbc, qac, qbc, uc, vcc, gatesc = _split(hc @ w_in[i], KV_SIZES + Q_SIZES)

        ya = neighbourhood_attn(_na_heads(qa), _na_heads(ka), _na_heads(va),
                                _na_heads(kac), _na_heads(vac), na_rpb[i])
        kb_all = jnp.concatenate([_da_qk(kbc), rope_2d(_da_qk(kb), tabs)], axis=1)
        vb_all = jnp.concatenate([_da_v(vbc), _da_v(vb)], axis=1)
        yb = diff_head_norm(diff_attn_blocks(rope_2d(_da_qk(qb), tabs), kb_all, vb_all, lam),
                            da_subln_g[i], lam_init)
        yc = gmlp_gate(jax.nn.gelu(u), jax.nn.gelu(v), gm_ln_g[i], gm_ln_b[i], gm_w_s[i], gm_b_s[i])
        x = x + gt1 * branch_merge(ya, yb, yc, gates, w_branch[i], w_out[i])
        if not last:
            yac = dense_attn(_na_heads(qac), _na_heads(kac), _na_heads(vac))
            ybc = diff_head_norm(diff_attend(_da_qk(qbc), _da_qk(kbc), _da_v(vbc), lam),
                                 da_subln_g[i], lam_init)
            ycc = gmlp_gate(jax.nn.gelu(uc), jax.nn.gelu(vcc), gm_ln_g[i], gm_ln_b[i], gm_w_s[i], gm_b_s[i])
            xc = xc + gt1c * branch_merge(yac, ybc, ycc, gatesc, w_branch[i], w_out[i])

        h2 = modulate(rmsnorm(x, g_norm2[i]), sh2, sc2)
        x = x + gt2 * ec_moe(h2, w_router[i], w_e1[i], w_e3[i], w_e2[i])
        if not last:
            h2c = modulate(rmsnorm(xc, g_norm2[i]), sh2c, sc2c)
            xc = xc + gt2c * ec_moe(h2c, w_router[i], w_e1[i], w_e3[i], w_e2[i])
    return rmsnorm(x, g_final)


def setup_inputs(seed=0):
    out = dict(first_inputs(seed))
    for name, value in second_inputs(seed + 1).items():
        if name != "x":
            out[name + "_2"] = value
    return out


def reference(
    x, positions, rel_bias, norm_gains, sb_w_qkv, sb_w_o, dil_w_qkv, dil_w_o, mla_w_in,
    mla_q_norm, mla_w_qb, mla_kv_norm, mla_w_kvb, mla_w_o, ffn_w_up, ffn_conv_w, ffn_conv_b,
    ffn_w_down, c_2, ctx_2, c_ctx_2, w_ada_2, b_ada_2, g_norm1_2, g_norm2_2, w_in_2, na_rpb_2,
    da_lam_q1_2, da_lam_k1_2, da_lam_q2_2, da_lam_k2_2, da_subln_g_2, gm_ln_g_2, gm_ln_b_2,
    gm_w_s_2, gm_b_s_2, w_branch_2, w_out_2, w_router_2, w_e1_2, w_e3_2, w_e2_2, g_final_2,
):
    x = first_block(
        x, positions, rel_bias, norm_gains, sb_w_qkv, sb_w_o, dil_w_qkv, dil_w_o, mla_w_in,
        mla_q_norm, mla_w_qb, mla_kv_norm, mla_w_kvb, mla_w_o, ffn_w_up, ffn_conv_w, ffn_conv_b,
        ffn_w_down,
    )
    return second_block(
        x, c_2, ctx_2, c_ctx_2, w_ada_2, b_ada_2, g_norm1_2, g_norm2_2, w_in_2, na_rpb_2,
        da_lam_q1_2, da_lam_k1_2, da_lam_q2_2, da_lam_k2_2, da_subln_g_2, gm_ln_g_2, gm_ln_b_2,
        gm_w_s_2, gm_b_s_2, w_branch_2, w_out_2, w_router_2, w_e1_2, w_e3_2, w_e2_2, g_final_2,
    )


_drawn_inputs = setup_inputs


def setup_inputs(seed=0):
    import zlib

    import numpy as np

    out = dict(_drawn_inputs(seed))
    spreads = {}
    factors = {'b_ada_2': 4.487,
     'g_norm1_2': 6.529,
     'g_norm2_2': 8.0,
     'na_rpb_2': 8.0,
     'da_lam_q1_2': 8.0,
     'da_lam_k1_2': 8.0,
     'da_lam_q2_2': 8.0,
     'da_lam_k2_2': 8.0,
     'da_subln_g_2': 8.0,
     'gm_ln_g_2': 8.0,
     'gm_ln_b_2': 8.0,
     'gm_b_s_2': 7.076}
    for name, (base, spread) in spreads.items():
        noise = np.random.default_rng([zlib.crc32(name.encode()), seed]).standard_normal(out[name].shape)
        drawn = base * np.exp(spread * noise) if base else spread * noise
        out[name] = jnp.asarray(drawn.astype(out[name].dtype))
    for name, factor in factors.items():
        out[name] = (out[name] * factor).astype(out[name].dtype)
    return out
```

```python
import math

import numpy as np
import concourse.bass as bass
from concourse import mybir
from concourse.alu_op_type import AluOpType as ALU

ACT = mybir.ActivationFunctionType
AX = mybir.AxisListType
F32 = mybir.dt.float32

P = 128
D = 1024
KT = D // P
S = 256
ST = S // P
DEPTH = 2
DH = 64
SCALE = DH ** -0.5
EPS = 1e-6
NEG = -1e30
SB_HEADS = 16
DIL = ((128, 1), (512, 4), (2048, 16))
DIL_HEADS = 8
N_BUCKETS, BUCKET_MAX_DIST = 32, 2048
D_FF = 2816
FT = D_FF // P
CONV_W = 3
GRID_W = 64
NA_HEADS, NA_WIN_R, NA_WIN_C = 8, 8, 16
NA_DR = 6
DA_HEADS = 4
BRANCH = 512
BT = BRANCH // P
GM_GROUPS = 4
N_EXPERTS, CAP = 16, 32
PROJ = 7168
N_MOD = 6
SLOT = 4 * BRANCH
NSLOT = 8
NBANK = 8

C_AT, C_N = {}, 0
for _name, _w in (("ident", P), ("mean", P), ("mean_head", P), ("ones", P), ("suffix", P), ("rot", P),
                  ("cos", S), ("sin", S), ("sb_keep", 384), ("sb_neg", 384), ("iota", CAP), ("col_neg", GRID_W)):
    C_AT[_name] = (C_N, C_N + _w)
    C_N += _w

ROWS = (("norm_gains", DEPTH * 4 * KT, 0, 0), ("c_2", KT, 0, 64), ("c_ctx_2", KT, 0, 72), ("g_final_2", KT, 0, 80),
        ("g_norm1_2", DEPTH * KT, 0, 88), ("g_norm2_2", DEPTH * KT, 0, 104), ("da_subln_g_2", DEPTH, 0, 120),
        ("ffn_conv_w", P, 1, 0), ("ffn_conv_w", P, 2, 0), ("ffn_conv_w", 8, 3, 0),
        ("ffn_conv_b", DEPTH * 2 * FT, 3, 8), ("b_ada_2", DEPTH * N_MOD * KT, 4, 0))
ROW_BLOCKS = (122, 128, 128, 96, 96)


def constant_table():
    t = np.zeros((P, C_N), np.float32)

    def put(name, v):
        t[:, slice(*C_AT[name])] = v

    k = np.arange(P)
    put("ident", np.eye(P))
    put("mean", 1.0 / D)
    put("mean_head", 1.0 / P)
    put("ones", 1.0)
    put("suffix", k[:, None] >= k[None, :])
    rot = np.zeros((P, P))
    for m in range(P):
        if m % 32 < 16:
            rot[m + 16, m] = -1.0
        else:
            rot[m - 16, m] = 1.0
    put("rot", rot)
    inv = 10000.0 ** (-np.arange(0, 32, 2, dtype=np.float32) / 32)
    tok = np.arange(S)
    at = np.where((k % 64 < 32)[:, None], (tok // GRID_W)[None], (tok % GRID_W)[None]).astype(np.float32)
    ang = at * inv.astype(np.float32)[k % 16][:, None]
    put("cos", np.cos(ang))
    put("sin", np.sin(ang))
    tri = (k[:, None] < k[None, :]).astype(np.float32)
    keep = np.concatenate([tri, np.ones((P, P)), tri], 1)
    put("sb_keep", -keep)
    put("sb_neg", np.where(keep > 0, 0.0, NEG))
    put("iota", np.arange(CAP)[None])
    col = np.arange(GRID_W)
    first = np.clip(col - NA_WIN_C // 2, 0, GRID_W - NA_WIN_C)
    inside = (col[None] >= first[:, None]) & (col[None] < first[:, None] + NA_WIN_C)
    put("col_neg", np.tile(np.where(inside, 0.0, NEG), (2, 1)))
    return t


def bucket_table():
    t = np.zeros((N_BUCKETS + 1, 3 * 384), np.float32)
    exact = N_BUCKETS // 2
    for g, (window, r) in enumerate(DIL):
        for i in range(383):
            d = 255 - i
            if d < 0 or d % r or d // r > window // r:
                t[N_BUCKETS, g * 384 + i] = NEG
                continue
            x = np.float32(max(d, 1))
            large = exact + int(np.float32(np.log(x / np.float32(exact)) / np.float32(math.log(BUCKET_MAX_DIST / exact))
                                           * np.float32(N_BUCKETS - exact)))
            t[d if d < exact else min(large, N_BUCKETS - 1), g * 384 + i] = 1.0
    return t


class Signal:

    def __init__(self, sem):
        self.sem, self.made, self.taken = sem, 0, {}

    def up(self):
        self.made += 1
        return 1

    def nth(self, who):
        self.taken[who] = self.taken.get(who, 0) + 1
        return self.taken[who]


class Banks:

    def __init__(self, ps, filled, freed):
        self.ps, self.filled, self.freed = ps, filled, freed
        self.uses, self.at, self.frees, self.due = [], {}, {}, None

    def open(self, *readers):
        u = len(self.uses)
        last = self.uses[u - NBANK][-1] if u >= NBANK else None
        self.due = last and (self.freed[last], sum(r[-1] == last for r in self.uses[:u - NBANK + 1]))
        self.uses.append(readers)
        return self.ps[:, u % NBANK, :]

    def take(self, who):
        u = self.at.get(who, 0)
        while who not in self.uses[u]:
            u += 1
        self.at[who] = u + 1
        return self.ps[:, u % NBANK, :]

    def free(self, who):
        self.frees[who] = self.frees.get(who, 0) + 1
        return 1


def weight_chunks(a):
    out = []

    def cols(w, k0, c0):
        out.append([(w[k0:k0 + 4 * P, c0:c0 + BRANCH].rearrange("(k p) n -> p k n", p=P), 0, 4, BRANCH, 0)])

    def panel(w, c0, rows=D):
        for k0 in range(0, rows, 4 * P):
            cols(w, k0, c0)

    def ffn(i):
        up, down = a["ffn_w_up"][i], a["ffn_w_down"][i]
        for j in range(FT // 2):
            for k0 in (0, 4 * P):
                out.append([(up[k0:k0 + 4 * P, half * D_FF + j * S:half * D_FF + (j + 1) * S]
                             .rearrange("(k p) n -> p k n", p=P), half * S, 4, S, 0) for half in (0, 1)])
        for j in range(FT // 2):
            out.append([(down[j * S:(j + 1) * S, :].rearrange("(k p) n -> p k n", p=P), 0, 2, D, 1)])

    for i in range(2):
        w = a["sb_w_qkv"][0] if i == 0 else a["dil_w_qkv"][0]
        for c0 in range(0, w.shape[1], BRANCH):
            panel(w, c0)
        w = a["sb_w_o"][0] if i == 0 else a["dil_w_o"][0]
        for c0 in range(0, D, BRANCH):
            panel(w, c0, w.shape[0])
        ffn(i)
    for i in range(DEPTH):
        for c0 in range(0, N_MOD * D, BRANCH):
            panel(a["w_ada_2"][i], c0)
        w = a["w_in_2"][i]
        for c0 in (6, 7, 0, 1, 4, 2, 3, 5):
            panel(w, c0 * BRANCH)
        for b in range(3):
            for half in range(2):
                panel(w, 8 * BRANCH + b * D + half * BRANCH)
                panel(a["w_branch_2"][i][b], half * BRANCH, BRANCH)
        for half in range(2):
            panel(a["w_out_2"][i], half * BRANCH)
        for e in range(N_EXPERTS):
            for w in ("w_e1_2", "w_e3_2", "w_e2_2"):
                for half in range(2):
                    panel(a[w][i][e], half * BRANCH)
    return out


def build(nc, a, out, dump=None, stop=None):
    from contextlib import ExitStack
    ctx = ExitStack()
    with ctx:
        def sb(name, words):
            return ctx.enter_context(nc.sbuf_tensor(name, [P, words], F32))

        ring = sb("ring", NSLOT * SLOT)
        Xb = sb("residual", KT * 2 * S)
        Hb = sb("normed", KT * 2 * S)
        Cb = sb("constants", C_N)
        colsb = sb("param_cols", 5 * P)
        small = sb("small", 1024)
        ARENA = 24500
        arena = sb("arena", ARENA)
        ps = ctx.enter_context(nc.psum_tensor("ps", [P, NBANK, 512], F32))

        X = Xb[:, :].rearrange("p (k t) -> p k t", k=KT)
        H = Hb[:, :].rearrange("p (k t) -> p k t", k=KT)

        def cst(name):
            return Cb[:, slice(*C_AT[name])]

        ident, mean, mean_head, ones, suffix, rot = (cst(n) for n in ("ident", "mean", "mean_head", "ones", "suffix", "rot"))

        def view(off, *dims):
            n = int(np.prod(dims))
            assert off + n <= ARENA
            v = arena[:, off:off + n]
            if len(dims) == 2:
                v = v.rearrange("p (a b) -> p a b", b=dims[1])
            if len(dims) == 3:
                v = v.rearrange("p (a b c) -> p a b c", b=dims[1], c=dims[2])
            if len(dims) == 4:
                v = v.rearrange("p (a b c d) -> p a b c d", b=dims[1], c=dims[2], d=dims[3])
            return v

        def tiny(off, n):
            return small[:, off:off + n]

        gains = colsb[:, 0:64]
        col_c = colsb[:, 64:80]
        g_final = colsb[:, 80:88]
        g_norm = (colsb[:, 88:104], colsb[:, 104:120])
        subln = colsb[:, 120:122]
        conv_w = colsb[:, P:P + DEPTH * CONV_W * 2 * FT]
        conv_b = colsb[:, 3 * P + 8:3 * P + 8 + DEPTH * 2 * FT]
        b_ada = colsb[:, 4 * P:4 * P + DEPTH * N_MOD * KT]

        rstd = small[:, 0:512]
        mod = small[:, 512:608].rearrange("p (t s) -> p t s", s=2)
        ampl = small[:, 608:624].rearrange("p (k s) -> p k s", s=2)
        silu_c = small[:, 624:640].rearrange("p (k s) -> p k s", s=2)
        nmax, ssum, rsum = (small[:, 640 + 8 * i:648 + 8 * i].rearrange("p (b c) -> p b c", b=2) for i in range(3))
        neg_lam = small[:, 664:665]
        lam2 = small[:, 665:667]
        g_head = small[:, 667:668]
        eps = small[:, 668:669]
        sc16 = small[:, 670:686].rearrange("p (k s) -> p k s", s=2)
        stat = small[:, 686:698].rearrange("p (a b) -> p a b", b=4)
        rden = small[:, 698:702]
        top8 = small[:, 704:712]
        aff = small[:, 712:776].rearrange("p (j q e) -> p j q e", j=ST, q=2)
        pos = small[:, 776:840].rearrange("p (j r) -> p j r", j=ST)
        den4 = small[:, 840:844]
        mx4 = small[:, 844:848]

        bias_scratch = nc.dram_tensor("dil_bias_scratch", [3 * DIL_HEADS, 384], F32, kind="Internal").ap()
        rpb_scratch = nc.dram_tensor("na_bias_scratch", [NA_HEADS, 15, P], F32, kind="Internal").ap()

        bias_shear = nc.dram_tensor("dil_bias_shear", [3 * DIL_HEADS, P * 386], F32, kind="Internal").ap()
        rpb_shear = nc.dram_tensor("na_bias_shear", [NA_HEADS, NA_DR + 1, GRID_W * 130], F32, kind="Internal").ap()

        def sem(name):
            return ctx.enter_context(nc.semaphore(name))

        def sig(name):
            return Signal(sem(name))

        banks = Banks(ps, sem("psum_filled"), {"v": sem("psum_freed_by_vector"), "a": sem("psum_freed_by_scalar")})
        slot_loaded = [sem(f"slot_loaded{i}") for i in range(NSLOT)]
        chunk_used = sem("chunk_used")
        loads = {n: sem(f"load_{n}") for n in ("consts", "rows", "x", "ctx", "bucket", "router", "out", "relb", "gm",
                                               "lam", "bias_out", "bias_shear", "bias_in", "rpb_out", "rpb_shear", "rpb_in")}
        load_count = {n: 0 for n in loads}
        consts_ready, cols_ready, x_ready, zero_ready = sig("consts_ready"), sig("cols_ready"), sig("x_ready"), sig("zero_ready")
        sq_ready, rstd_ready, h_ready = sig("squares_ready"), sig("rstd_ready"), sig("normed_ready")
        src_ready = sig("norm_source_ready")
        v_step, a_step = sig("vector_step"), sig("scalar_step")
        qkv_ready = sig("qkv_ready")
        z_copied, z_abs, l_ready, L_ready, t_ready, sb_p_ready, o_ready = (
            sig(n) for n in ("z_copied", "neg_abs_ready", "log1p_ready", "lognot_ready", "stick_arg_ready",
                             "stick_probs_ready", "attn_out_ready"))
        gate_ready, gate_exp, hidden_ready = sig("gate_ready"), sig("gate_exp_ready"), sig("hidden_ready")
        max_ready, exp_ready, p_ready, pt_ready = (sig(n) for n in ("row_max_ready", "exp_ready", "probs_ready", "probsT_ready"))
        bias_rows, bias_tile = sig("bias_rows_ready"), sig("bias_tile_ready")
        sc_ready = sig("silu_c_ready")
        dma_free = sig("arena_free_for_loads")
        rope_ready = sig("rope_ready")
        ln_ready, ln_rstd = sig("ln_var_ready"), sig("ln_rstd_ready")
        y_ready = sig("branch_out_ready")
        merged_ready = sig("merged_ready")
        tok_ready, aff_ready, pos_ready, P_ready, G_ready = (
            sig(n) for n in ("token_major_ready", "affinity_ready", "slot_pos_ready", "select_ready", "gated_select_ready"))
        xin_ready, pgt_ready, ye_ready = sig("expert_in_ready"), sig("scatter_ready"), sig("expert_out_ready")
        affT_ready = sig("affinityT_ready")
        lam_ready, lam_exp = sig("lambda_dot_ready"), sig("lambda_exp_ready")
        wst_ready, final_ready, mod_ready = sig("spatialT_ready"), sig("final_ready"), sig("mod_ready")
        gate_used = sig("gate_used")

        chunks = weight_chunks(a)
        freed_at = []
        state = {"chunk": 0}

        X_STAGE, C_STAGE, ROW_STAGE, RELB, BUCKET, DROW = 0, 2048, 4096, 4800, 4832, 20480
        SQT, SKT, SV, SOT = view(0, 8, S), view(2048, 8, S), view(4096, ST, D), view(6144, 8, S)
        SM = view(22000, 8, S)
        SBUFS = [view(8192 + 1536 * i, 4, 384) for i in range(8)]
        DQT, DKT, DV = view(0, 12, S), view(3072, 12, S), view(6144, ST, 1536)
        DB = view(9216, 24, S)
        DOT = view(15360, 4, S)
        DS = [view(16384 + 768 * i, 3, S) for i in range(2)]
        DPT = [view(17920 + 768 * i, 6, P) for i in range(2)]
        HID = view(0, FT, S)
        GU = [view(5632 + 1024 * i, 4, S) for i in range(2)]
        GE = [view(7680 + 512 * i, 2, S) for i in range(2)]
        KT2, QT2, V2 = view(0, 4, 512), view(2048, 4, 512), view(4096, 4, 512)
        Y2 = [view(6144 + 2048 * i, 4, 512) for i in range(3)]
        BN = view(12288, NA_HEADS, NA_DR, GRID_W)
        S2 = [view(15360 + 1024 * i, 2, 512) for i in range(2)]
        PT2 = [view(17408 + 512 * i, 4, P) for i in range(2)]
        WST = view(18432, 4, P)
        GMR = view(18944, 3, 512)
        LAMV = view(20480, 4, DH)
        WS_RAW = view(20736, 4, P)
        ROPE_T = view(21248, S)
        O2 = view(21504, 4, 512)
        UT, VG, TG = view(0, 4, 512), view(2048, 4, 512), view(4096, 4, 512)
        YCU = Y2[2]
        MB = view(0, 8, 512)
        GS = [view(15360 + 2048 * i, 4, 512) for i in range(2)]
        HT = view(0, 4, D)
        SEL = view(4096, ST, 2 * N_EXPERTS, CAP)
        GSEL = view(6144, ST, 2 * N_EXPERTS, CAP)
        XIN = view(8192, KT, N_EXPERTS, 2 * CAP)
        PGT = view(16384, 2, 4, S)
        HE = [view(18432 + 512 * i, 8, 2 * CAP) for i in range(2)]
        AT = view(20480, 2, S)[0:2 * N_EXPERTS]
        AW = view(20992, S)[0:2 * N_EXPERTS]
        WR = small[:, 848:976].rearrange("p (k e) -> p k e", k=KT)
        YE = (Hb[:, :].rearrange("p (k d) -> p k d", k=4), arena[:, 0:4096].rearrange("p (k d) -> p k d", k=4))
        OUTT = view(0, ST, D)

        block = ctx.enter_context(nc.Block())

        @block.tensor
        def _(pe):
            mm = nc.tensor.matmul

            def chunk(n):
                return (ring[:, (n % NSLOT) * SLOT:(n % NSLOT + 1) * SLOT], slot_loaded[n % NSLOT],
                        16 * sum(len(chunks[m]) for m in range(n % NSLOT, n + 1, NSLOT)))

            def next_chunks(k):
                state["chunk"] += k
                return [chunk(n) for n in range(state["chunk"] - k, state["chunk"])]

            used = [0]

            def chunks_done(k, banked=False):
                for _ in range(k):
                    freed_at.append(len(banks.uses))

            def gemm_T(panels, src, n, kts=KT, readers=("v",)):
                for _ in range(panels):
                    slots = []
                    for slot, loaded, count in next_chunks(kts // 4):
                        pe.wait_ge(loaded, count)
                        slots.append(slot.rearrange("p (k n) -> p k n", k=4))
                    for f in range(4):
                        o = banks.open(*readers)
                        if banks.due:
                            pe.wait_ge(*banks.due)
                        for k in range(kts):
                            ins = mm(o[:, 0:n], slots[k // 4][:, k % 4, f * P:(f + 1) * P], src[:, k, 0:n],
                                     start=k == 0, stop=k == kts - 1)
                        ins.then_inc(banks.filled, 1)
                    chunks_done(kts // 4)

            def gemm_N(panels, src, tiles):
                for _ in range(panels):
                    slots = []
                    for slot, loaded, count in next_chunks(2):
                        pe.wait_ge(loaded, count)
                        slots.append(slot.rearrange("p (k n) -> p k n", k=4))
                    for t in range(tiles):
                        o = banks.open("v")
                        if banks.due:
                            pe.wait_ge(*banks.due)
                        for k in range(KT):
                            ins = mm(o, src[:, k, t * P:(t + 1) * P], slots[k // 4][:, k % 4, :],
                                     start=k == 0, stop=k == KT - 1)
                        ins.then_inc(banks.filled, 1)
                    chunks_done(2)

            def mean_square(src, n, tiles, m):
                pe.wait_ge(sq_ready.sem, sq_ready.nth("pe"))
                o = banks.open("a")
                if banks.due:
                    pe.wait_ge(*banks.due)
                for k in range(tiles):
                    ins = mm(o[:, 0:n], m, src[:, k, 0:n], start=k == 0, stop=k == tiles - 1)
                ins.then_inc(banks.filled, 1)

            pe.wait_ge(loads["consts"], 16)
            pe.wait_ge(loads["rows"], 16 * len(ROWS))
            for b, r in enumerate(ROW_BLOCKS):
                o = banks.open("v")
                if banks.due:
                    pe.wait_ge(*banks.due)
                nc.tensor.transpose(o[:, 0:r], view(ROW_STAGE, 5, P)[0:r, b, :], ident[0:r, 0:r]).then_inc(banks.filled, 1)
            pe.wait_ge(loads["x"], 16)
            pe.wait_ge(loads["ctx"], 16)
            for k in range(KT):
                o = banks.open("v")
                if banks.due:
                    pe.wait_ge(*banks.due)
                for t in range(4):
                    src = view((X_STAGE, C_STAGE)[t // 2], ST, D)
                    ins = nc.tensor.transpose(o[:, t * P:(t + 1) * P], src[:, t % 2, k * P:(k + 1) * P], ident)
                ins.then_inc(banks.filled, 1)
            pe.wait_ge(loads["relb"], 16)
            pe.wait_ge(loads["bucket"], 16)
            pe.wait_ge(zero_ready.sem, zero_ready.nth("pe"))
            for g in range(3):
                o = banks.open("v")
                if banks.due:
                    pe.wait_ge(*banks.due)
                mm(o[0:DIL_HEADS, 0:384], arena[0:33, RELB + g * DIL_HEADS:RELB + (g + 1) * DIL_HEADS],
                               arena[0:33, BUCKET + g * 384:BUCKET + (g + 1) * 384], start=True, stop=True).then_inc(banks.filled, 1)

            def ffn():
                mean_square(H, S, KT, mean)
                pe.wait_ge(h_ready.sem, h_ready.nth("pe"))
                gemm_T(FT // 2, H, S)
                outs = []
                for _ in range(8):
                    outs.append(banks.open("v"))
                    pe.wait_ge(*banks.due)
                for j in range(FT // 2):
                    pe.wait_ge(hidden_ready.sem, hidden_ready.nth("pe"))
                    (slot, loaded, count), = next_chunks(1)
                    pe.wait_ge(loaded, count)
                    slot = slot.rearrange("p (k n) -> p k n", k=2)
                    for f in range(8):
                        for k in range(2):
                            ins = mm(outs[f][:, 0:S], slot[:, k, f * P:(f + 1) * P], HID[:, 2 * j + k, :],
                                     start=j == 0 and k == 0, stop=j == FT // 2 - 1 and k == 1)
                        if j == FT // 2 - 1:
                            ins.then_inc(banks.filled, 1)
                    if j < FT // 2 - 1:
                        ins.then_inc(chunk_used, 1)
                        used[0] += 1
                        freed_at.append(-used[0])
                    else:
                        chunks_done(1)
                mean_square(H, S, KT, mean)

            mean_square(H, S, KT, mean)
            pe.wait_ge(h_ready.sem, h_ready.nth("pe"))
            gemm_T(4, H, S)
            gemm_N(2, H, ST)
            pe.wait_ge(qkv_ready.sem, qkv_ready.nth("pe"))

            def sb_scores(b):
                for h in range(4 * b, 4 * b + 4):
                    r, t = DH * (h % 2), h // 2
                    o = banks.open("a")
                    if banks.due:
                        pe.wait_ge(*banks.due)
                    mm(o[:, 0:S], SKT[r:r + DH, t, 0:P], SQT[r:r + DH, t, :], start=True, stop=True)
                    mm(o[:, S:384], SKT[r:r + DH, t, P:S], SQT[r:r + DH, t, P:S], start=True, stop=True).then_inc(banks.filled, 1)

            def sb_sums(b):
                L = SBUFS[4 * (b % 2) + 2]
                pe.wait_ge(L_ready.sem, L_ready.nth("pe"))
                for j in range(4):
                    o = banks.open("v")
                    if banks.due:
                        pe.wait_ge(*banks.due)
                    mm(o[:, 0:384], suffix, L[:, j, :], start=True, stop=False)
                    mm(o[:, P:S], ones, L[:, j, S:384], start=False, stop=True).then_inc(banks.filled, 1)

            def sb_out(b):
                Pr = SBUFS[4 * (b % 2) + 3]
                pe.wait_ge(sb_p_ready.sem, sb_p_ready.nth("pe"))
                for j in range(0, 4, 2):
                    o = banks.open("v")
                    if banks.due:
                        pe.wait_ge(*banks.due)
                    for i in range(2):
                        h = 4 * b + j + i
                        v0 = SV[:, 0, h * DH:(h + 1) * DH]
                        v1 = SV[:, 1, h * DH:(h + 1) * DH]
                        dst = o[DH * i:DH * (i + 1)]
                        mm(dst[:, 0:S], v0, Pr[:, j + i, 0:S], start=True, stop=False)
                        ins = mm(dst[:, P:S], v1, Pr[:, j + i, S:384], start=False, stop=True)
                    ins.then_inc(banks.filled, 1)

            sb_scores(0)
            for b in range(SB_HEADS // 4):
                if b + 1 < SB_HEADS // 4:
                    sb_scores(b + 1)
                sb_sums(b)
                sb_out(b)
            pe.wait_ge(o_ready.sem, o_ready.nth("pe"))
            gemm_T(2, SOT, S)
            mean_square(H, S, KT, mean)
            ffn()

            mean_square(H, S, KT, mean)
            pe.wait_ge(h_ready.sem, h_ready.nth("pe"))
            gemm_T(6, H, S)
            gemm_N(3, H, ST)
            pe.wait_ge(qkv_ready.sem, qkv_ready.nth("pe"))
            items = [(h, t) for h in range(DIL_HEADS) for t in range(ST)]

            def dil_scores(i):
                h, t = items[i]
                r = DH * (h % 2)
                for g in range(3):
                    o = banks.open("v")
                    if banks.due:
                        pe.wait_ge(*banks.due)
                    c = g * 4 + h // 2
                    mm(o[:, 0:(t + 1) * P], DQT[r:r + DH, c, t * P:(t + 1) * P],
                                   DKT[r:r + DH, c, 0:(t + 1) * P], start=True, stop=True).then_inc(banks.filled, 1)

            def dil_out(i):
                h, t = items[i]
                pe.wait_ge(p_ready.sem, p_ready.nth("pe"))
                tiles = [(g, k) for g in range(3) for k in range(t + 1)]
                for n0 in range(0, len(tiles), 4):
                    o = banks.open("a")
                    if banks.due:
                        pe.wait_ge(*banks.due)
                    for n, (g, k) in enumerate(tiles[n0:n0 + 4]):
                        ins = nc.tensor.transpose(o[:, n * P:(n + 1) * P], DS[i % 2][:, g, k * P:(k + 1) * P], ident)
                    ins.then_inc(banks.filled, 1)
                pe.wait_ge(pt_ready.sem, pt_ready.nth("pe"))
                o = banks.open("v")
                if banks.due:
                    pe.wait_ge(*banks.due)
                r = DH * (h % 2)
                for n, (g, k) in enumerate(tiles):
                    ins = mm(o[r:r + DH, 0:P], DV[:, k, g * BRANCH + h * DH:g * BRANCH + (h + 1) * DH],
                             DPT[i % 2][:, n, :], start=n == 0, stop=n == len(tiles) - 1)
                ins.then_inc(banks.filled, 1)

            def skewed(n, first, second):
                first(0)
                for i in range(n):
                    if i + 1 < n:
                        first(i + 1)
                    second(i)

            skewed(len(items), dil_scores, dil_out)
            pe.wait_ge(o_ready.sem, o_ready.nth("pe"))
            gemm_T(2, DOT, S, 4)
            mean_square(H, S, KT, mean)
            ffn()

            pe.wait_ge(sc_ready.sem, sc_ready.nth("pe"))
            for i in range(DEPTH):
                last = i == DEPTH - 1
                qtok, qtiles = (S, ST) if last else (2 * S, 2 * ST)
                for _ in range(N_MOD * D // BRANCH):
                    slots = []
                    for slot, loaded, count in next_chunks(2):
                        pe.wait_ge(loaded, count)
                        slots.append(slot.rearrange("p (k n) -> p k n", k=4))
                    o = banks.open("v")
                    if banks.due:
                        pe.wait_ge(*banks.due)
                    for f in range(4):
                        for k in range(KT):
                            ins = mm(o[:, 2 * f:2 * f + 2], slots[k // 4][:, k % 4, f * P:(f + 1) * P], silu_c[:, k, :],
                                     start=k == 0, stop=k == KT - 1)
                    ins.then_inc(banks.filled, 1)
                    chunks_done(2)
                mean_square(H, 2 * S, KT, mean)
                pe.wait_ge(loads["gm"], 64 * (i + 1))
                o = banks.open("v")
                if banks.due:
                    pe.wait_ge(*banks.due)
                for g in range(4):
                    ins = nc.tensor.transpose(o[:, g * P:(g + 1) * P], WS_RAW[:, g, :], ident)
                ins.then_inc(banks.filled, 1)
                pe.wait_ge(h_ready.sem, h_ready.nth("pe"))
                gemm_T(1, H, qtok)
                gemm_N(1, H, qtiles)
                pe.wait_ge(ln_ready.sem, ln_ready.nth("pe"))
                for g in range(4):
                    o = banks.open("v")
                    if banks.due:
                        pe.wait_ge(*banks.due)
                    for t in range(qtiles):
                        ins = mm(o[:, t * P:(t + 1) * P], VG[:, t, g * P:(g + 1) * P], WST[:, g, :], start=True, stop=True)
                    ins.then_inc(banks.filled, 1)
                pe.wait_ge(y_ready.sem, y_ready.nth("pe"))
                gemm_T(1, H, 2 * S)
                gemm_N(1, H, 4)
                gemm_T(1, H, qtok)
                pe.wait_ge(qkv_ready.sem, qkv_ready.nth("pe"))
                items = [(h, t) for h in range(NA_HEADS) for t in range(qtiles)]

                def keys(t):
                    return (0, 4) if t < ST else (ST, 4)

                def na_scores(n):
                    h, t = items[n]
                    r, (k0, k1) = DH * (h % 2), keys(t)
                    o = banks.open("v")
                    if banks.due:
                        pe.wait_ge(*banks.due)
                    mm(o[:, k0 * P:k1 * P], QT2[r:r + DH, h // 2, t * P:(t + 1) * P],
                                   KT2[r:r + DH, h // 2, k0 * P:k1 * P], start=True, stop=True).then_inc(banks.filled, 1)

                def na_out(n):
                    h, t = items[n]
                    r, (k0, k1) = DH * (h % 2), keys(t)
                    pe.wait_ge(p_ready.sem, p_ready.nth("pe"))
                    o = banks.open("a")
                    if banks.due:
                        pe.wait_ge(*banks.due)
                    for k in range(k0, k1):
                        ins = nc.tensor.transpose(o[:, k * P:(k + 1) * P], S2[n % 2][:, 0, k * P:(k + 1) * P], ident)
                    ins.then_inc(banks.filled, 1)
                    pe.wait_ge(pt_ready.sem, pt_ready.nth("pe"))
                    o = banks.open("v")
                    if banks.due:
                        pe.wait_ge(*banks.due)
                    for k in range(k0, k1):
                        ins = mm(o[r:r + DH, 0:P], V2[:, k, h * DH:(h + 1) * DH], PT2[n % 2][:, k, :],
                                 start=k == k0, stop=k == k1 - 1)
                    ins.then_inc(banks.filled, 1)

                skewed(len(items), na_scores, na_out)
                gemm_T(1, H, 2 * S)
                gemm_N(1, H, 4)
                gemm_T(1, H, qtok)
                pe.wait_ge(qkv_ready.sem, qkv_ready.nth("pe"))
                for T in (KT2, QT2):
                    for c in range(4):
                        o = banks.open("v")
                        if banks.due:
                            pe.wait_ge(*banks.due)
                        mm(o[:, 0:S], rot, T[:, c, 0:S], start=True, stop=True).then_inc(banks.filled, 1)
                pe.wait_ge(rope_ready.sem, rope_ready.nth("pe"))
                items = [(h, t) for h in range(DA_HEADS) for t in range(qtiles)]

                def da_scores(n):
                    h, t = items[n]
                    k0, k1 = keys(t)
                    for c in range(2):
                        o = banks.open("v", "a")
                        if banks.due:
                            pe.wait_ge(*banks.due)
                        r = DH * c
                        mm(o[:, k0 * P:k1 * P], QT2[r:r + DH, h, t * P:(t + 1) * P],
                                       KT2[r:r + DH, h, k0 * P:k1 * P], start=True, stop=True).then_inc(banks.filled, 1)

                def da_out(n):
                    h, t = items[n]
                    k0, k1 = keys(t)
                    pe.wait_ge(p_ready.sem, p_ready.nth("pe"))
                    o = banks.open("a")
                    if banks.due:
                        pe.wait_ge(*banks.due)
                    for k in range(k0, k1):
                        ins = nc.tensor.transpose(o[:, k * P:(k + 1) * P], S2[n % 2][:, 0, k * P:(k + 1) * P], ident)
                    ins.then_inc(banks.filled, 1)
                    pe.wait_ge(pt_ready.sem, pt_ready.nth("pe"))
                    o = banks.open("v")
                    if banks.due:
                        pe.wait_ge(*banks.due)
                    for k in range(k0, k1):
                        ins = mm(o[:, 0:P], V2[:, k, h * P:(h + 1) * P], PT2[n % 2][:, k, :], start=k == k0, stop=k == k1 - 1)
                    ins.then_inc(banks.filled, 1)

                skewed(len(items), da_scores, da_out)
                pe.wait_ge(sq_ready.sem, sq_ready.nth("pe"))
                for h in range(DA_HEADS):
                    o = banks.open("a")
                    if banks.due:
                        pe.wait_ge(*banks.due)
                    mm(o[:, 0:qtok], mean_head, Y2[1][:, h, 0:qtok], start=True, stop=True).then_inc(banks.filled, 1)
                pe.wait_ge(y_ready.sem, y_ready.nth("pe"))
                for b in range(3):
                    for half in range(2):
                        gemm_T(1, H, qtok, readers=("a",))
                        gemm_T(1, Y2[b], qtok, 4)
                pe.wait_ge(merged_ready.sem, merged_ready.nth("pe"))
                gemm_T(2, MB, qtok)
                mean_square(H, qtok, KT, mean)

                pe.wait_ge(h_ready.sem, h_ready.nth("pe"))
                pe.wait_ge(loads["router"], 16 * (i + 1))
                o = banks.open("v", "a")
                if banks.due:
                    pe.wait_ge(*banks.due)
                for t in range(qtiles):
                    for k in range(KT):
                        ins = mm(o[:, t * N_EXPERTS:(t + 1) * N_EXPERTS], H[:, k, t * P:(t + 1) * P], WR[:, k, :],
                                 start=k == 0, stop=k == KT - 1)
                ins.then_inc(banks.filled, 1)
                for t in range(qtiles):
                    for half in range(2):
                        o = banks.open("a")
                        if banks.due:
                            pe.wait_ge(*banks.due)
                        for f in range(4):
                            ins = nc.tensor.transpose(o[:, f * P:(f + 1) * P], H[:, 4 * half + f, t * P:(t + 1) * P], ident)
                        ins.then_inc(banks.filled, 1)
                rows = qtiles // 2 * N_EXPERTS
                pe.wait_ge(aff_ready.sem, aff_ready.nth("pe"))
                o = banks.open("v")
                if banks.due:
                    pe.wait_ge(*banks.due)
                for j in range(ST):
                    ins = nc.tensor.transpose(o[0:rows, j * P:(j + 1) * P],
                                              aff[:, j, 0:qtiles // 2, :].rearrange("p q e -> p (q e)"), ident)
                ins.then_inc(banks.filled, 1)
                pe.wait_ge(pos_ready.sem, pos_ready.nth("pe"))
                o = banks.open("v")
                if banks.due:
                    pe.wait_ge(*banks.due)
                for j in range(ST):
                    ins = nc.tensor.transpose(o[:, j * 32:j * 32 + rows], AW[0:rows, j * P:(j + 1) * P], ident[0:rows, 0:rows])
                ins.then_inc(banks.filled, 1)
                pe.wait_ge(P_ready.sem, P_ready.nth("pe"))
                pe.wait_ge(tok_ready.sem, tok_ready.nth("pe"))
                for k in range(KT):
                    for q in range(qtiles // 2):
                        o = banks.open("v")
                        if banks.due:
                            pe.wait_ge(*banks.due)
                        for j in range(ST):
                            ins = mm(o, HT[:, ST * q + j, k * P:(k + 1) * P],
                                     SEL[:, j, q * N_EXPERTS:(q + 1) * N_EXPERTS, :].rearrange("p e s -> p (e s)"),
                                     start=j == 0, stop=j == ST - 1)
                        ins.then_inc(banks.filled, 1)
                pe.wait_ge(G_ready.sem, G_ready.nth("pe"))
                for q in range(qtiles // 2):
                    for half in range(2):
                        o = banks.open("a")
                        if banks.due:
                            pe.wait_ge(*banks.due)
                        for n, (pk, j) in enumerate((pk, j) for pk in (2 * half, 2 * half + 1) for j in range(ST)):
                            e0 = q * N_EXPERTS + 4 * pk
                            ins = nc.tensor.transpose(o[:, n * P:(n + 1) * P],
                                                      GSEL[:, j, e0:e0 + 4, :].rearrange("p e s -> p (e s)"), ident)
                        ins.then_inc(banks.filled, 1)
                pe.wait_ge(xin_ready.sem, xin_ready.nth("pe"))
                w = qtiles // 2 * CAP
                for e in range(N_EXPERTS):
                    for which in range(2):
                        o = banks.open(*(("a", "v") if which == 0 else ("v",)))
                        if banks.due:
                            pe.wait_ge(*banks.due)
                        for half in range(2):
                            slots = []
                            for slot, loaded, count in next_chunks(2):
                                pe.wait_ge(loaded, count)
                                slots.append(slot.rearrange("p (k n) -> p k n", k=4))
                            for f in range(4):
                                for k in range(KT):
                                    c = (4 * half + f) * w
                                    ins = mm(o[:, c:c + w], slots[k // 4][:, k % 4, f * P:(f + 1) * P], XIN[:, k, e, 0:w],
                                             start=k == 0, stop=k == KT - 1)
                            if half == 0:
                                ins.then_inc(chunk_used, 1)
                                used[0] += 1
                                freed_at.extend([-used[0]] * 2)
                        ins.then_inc(banks.filled, 1)
                        chunks_done(2)
                    pe.wait_ge(hidden_ready.sem, hidden_ready.nth("pe"))
                    for half in range(2):
                        slots = []
                        for slot, loaded, count in next_chunks(2):
                            pe.wait_ge(loaded, count)
                            slots.append(slot.rearrange("p (k n) -> p k n", k=4))
                        o = banks.open("a")
                        if banks.due:
                            pe.wait_ge(*banks.due)
                        for k in range(KT):
                            ins = mm(o[0:w, :], HE[0][:, k, 0:w], slots[k // 4][:, k % 4, :], start=k == 0, stop=k == KT - 1)
                        ins.then_inc(banks.filled, 1)
                        chunks_done(2)
                pe.wait_ge(ye_ready.sem, ye_ready.nth("pe"))
                for f in range(KT):
                    o = banks.open("v")
                    if banks.due:
                        pe.wait_ge(*banks.due)
                    for q in range(qtiles // 2):
                        for pk in range(4):
                            ins = mm(o[:, q * S:(q + 1) * S], YE[q][:, pk, f * P:(f + 1) * P], PGT[:, q, pk, :],
                                     start=pk == 0, stop=pk == 3)
                    ins.then_inc(banks.filled, 1)

            mean_square(H, S, KT, mean)
            pe.wait_ge(h_ready.sem, h_ready.nth("pe"))
            for t in range(ST):
                for half in range(2):
                    o = banks.open("a")
                    if banks.due:
                        pe.wait_ge(*banks.due)
                    for f in range(4):
                        ins = nc.tensor.transpose(o[:, f * P:(f + 1) * P], H[:, 4 * half + f, t * P:(t + 1) * P], ident)
                    ins.then_inc(banks.filled, 1)
            assert state["chunk"] == len(chunks) == len(freed_at)

        @block.sync
        def _(sp):
            sp.dma_start(Cb[:, :], a["const_table"]).then_inc(loads["consts"], 16)
            stage = view(ROW_STAGE, 5, P)
            taken = {}
            for name, r, b, r0 in ROWS:
                src = a[name]
                src = src.rearrange(" ".join("abcd"[:len(src.shape)]) + " -> (" + " ".join("abcd"[:len(src.shape)]) + ")")
                src = src.rearrange("(r n) -> r n", n=P)
                s0 = taken.get(name, 0)
                taken[name] = s0 + r
                sp.dma_start(stage[r0:r0 + r, b, :], src[s0:s0 + r, :]).then_inc(loads["rows"], 16)
            sp.dma_start(view(X_STAGE, ST, D), a["x"][0].rearrange("(t p) d -> p t d", p=P)).then_inc(loads["x"], 16)
            sp.dma_start(view(C_STAGE, ST, D), a["ctx_2"][0].rearrange("(t p) d -> p t d", p=P)).then_inc(loads["ctx"], 16)
            sp.dma_start(arena[0:N_BUCKETS, RELB:RELB + 24], a["rel_bias"]).then_inc(loads["relb"], 16)
            sp.dma_start(arena[0:33, BUCKET:BUCKET + 1152], a["bucket_table"]).then_inc(loads["bucket"], 16)
            for n, pieces in enumerate(chunks):
                if n >= NSLOT:
                    at = freed_at[n - NSLOT]
                    if at > 0:
                        sp.wait_ge(banks.filled, at)
                    else:
                        sp.wait_ge(chunk_used, -at)
                slot = ring[:, (n % NSLOT) * SLOT:(n % NSLOT + 1) * SLOT]
                for src, c0, k, w, _ in pieces:
                    dst = slot.rearrange("p (k n) -> p k n", k=k)[:, :, c0:c0 + w]
                    sp.dma_start(dst, src).then_inc(slot_loaded[n % NSLOT], 16)
            sp.wait_ge(final_ready.sem, final_ready.nth("sp"))
            sp.dma_start(out[0].rearrange("(t p) d -> p t d", p=P), OUTT).then_inc(loads["out"], 16)
            sp.wait_ge(loads["out"], 16)

        @block.vector
        def _(v):
            ve = nc.vector


            stamps = [0]


            def stamp():
                stamps[0] += 1
                at = 976 + stamps[0] % 24
                return ve.tensor_copy(small[:, at:at + 1], eps)




            ve.memset(eps, EPS).then_inc(v_step.sem, v_step.up())
            v.wait_ge(v_step.sem, v_step.made)
            ve.memset(arena[32:33, RELB:RELB + 24], 1.0).then_inc(zero_ready.sem, zero_ready.up())
            for b, r in enumerate(ROW_BLOCKS):
                o = banks.take("v")
                v.wait_ge(banks.filled, banks.at["v"])
                ve.tensor_copy(colsb[:, b * P:b * P + r], o[:, 0:r]).then_inc(banks.freed["v"], banks.free("v"))
            for k in range(KT):
                o = banks.take("v")
                v.wait_ge(banks.filled, banks.at["v"])
                ve.tensor_copy(X[:, k, :], o).then_inc(banks.freed["v"], banks.free("v"))
            v.wait_ge(banks.freed["v"], banks.frees["v"])
            ve.tensor_copy(sc16[:, :, 0], col_c[:, 0:8]).then_inc(src_ready.sem, src_ready.up())
            for g in range(3):
                o = banks.take("v")
                v.wait_ge(banks.filled, banks.at["v"])
                ins = ve.tensor_copy(arena[0:DIL_HEADS, DROW + 384 * g:DROW + 384 * (g + 1)], o[0:DIL_HEADS, 0:384])
                ins.then_inc(banks.freed["v"], banks.free("v"))
            v.wait_ge(banks.freed["v"], banks.frees["v"])
            ve.tensor_copy(sc16[:, :, 1], col_c[:, 8:16]).then_inc(bias_rows.sem, bias_rows.up())

            def pre_norm(src, gain, n=S):
                v.wait_ge(rstd_ready.sem, rstd_ready.nth("v"))
                for k in range(KT):
                    ins = ve.scalar_tensor_tensor(H[:, k, 0:n], src[:, k, 0:n], gain[:, k:k + 1], rstd[:, 0:n], ALU.mult, ALU.mult)
                ins.then_inc(h_ready.sem, h_ready.up())

            def gain_of(i, j):
                return gains[:, (i * 4 + j) * KT:(i * 4 + j + 1) * KT]

            def post_norm_add(m, gain):
                v.wait_ge(rstd_ready.sem, rstd_ready.nth("v"))
                for k in range(KT):
                    ins = ve.scalar_tensor_tensor(m[:, k, :], m[:, k, :], gain[:, k:k + 1], rstd[:, 0:S], ALU.mult, ALU.mult)
                ins.then_inc(v_step.sem, v_step.up())
                v.wait_ge(v_step.sem, v_step.made)
                ve.tensor_tensor(X[:, :, 0:S], X[:, :, 0:S], m, ALU.add).then_inc(src_ready.sem, src_ready.up())
                v.wait_ge(src_ready.sem, src_ready.made)

            def evac(dst, n):
                o = banks.take("v")
                v.wait_ge(banks.filled, banks.at["v"])
                ve.tensor_copy(dst, o[:, 0:n]).then_inc(banks.freed["v"], banks.free("v"))

            def mixer_out(m, gain):
                for f in range(KT):
                    evac(m[:, f, :], S)
                v.wait_ge(banks.freed["v"], banks.frees["v"])
                stamp().then_inc(src_ready.sem, src_ready.up())
                post_norm_add(m, gain)

            def ffn(i):
                pre_norm(X, gain_of(i, 2))
                cw = conv_w[:, i * CONV_W * 2 * FT:(i + 1) * CONV_W * 2 * FT]
                cb = conv_b[:, i * 2 * FT:(i + 1) * 2 * FT]

                def tap(w, f):
                    return cw[:, w * 2 * FT + f:w * 2 * FT + f + 1]

                def conv(j):
                    gu = GU[j % 2]
                    fs = (2 * j, 2 * j + 1, FT + 2 * j, FT + 2 * j + 1)
                    os = []
                    for n, f in enumerate(fs):
                        o = banks.take("v")
                        v.wait_ge(banks.filled, banks.at["v"])
                        os.append(o)
                        ins = ve.tensor_scalar(gu[:, n, :], o[:, 0:S], tap(2, f), cb[:, f:f + 1], ALU.mult, ALU.add)
                    ins.then_inc(v_step.sem, v_step.up())
                    v.wait_ge(v_step.sem, v_step.made)
                    for n, f in enumerate(fs):
                        ins = ve.scalar_tensor_tensor(gu[:, n, 1:S], os[n][:, 0:S - 1], tap(1, f), gu[:, n, 1:S], ALU.mult, ALU.add)
                    ins.then_inc(v_step.sem, v_step.up())
                    v.wait_ge(v_step.sem, v_step.made)
                    for n, f in enumerate(fs):
                        ve.scalar_tensor_tensor(gu[:, n, 2:S], os[n][:, 0:S - 2], tap(0, f), gu[:, n, 2:S], ALU.mult, ALU.add).then_inc(banks.freed["v"], banks.free("v"))
                    v.wait_ge(banks.freed["v"], banks.frees["v"])
                    stamp().then_inc(gate_ready.sem, gate_ready.up())

                def glu(j):
                    gu, ge = GU[j % 2], GE[j % 2]
                    v.wait_ge(gate_exp.sem, gate_exp.nth("v"))
                    ve.scalar_tensor_tensor(ge, ge, 1.0, gu[:, 0:2, :], ALU.add, ALU.mult).then_inc(v_step.sem, v_step.up())
                    v.wait_ge(v_step.sem, v_step.made)
                    ve.scalar_tensor_tensor(HID[:, 2 * j:2 * j + 2, :], ge, 0.5, gu[:, 2:4, :], ALU.mult, ALU.mult
                                            ).then_inc(hidden_ready.sem, hidden_ready.up())
                    v.wait_ge(hidden_ready.sem, hidden_ready.made)

                conv(0)
                for j in range(FT // 2):
                    if j + 1 < FT // 2:
                        conv(j + 1)
                    glu(j)
                mixer_out(SM, gain_of(i, 3))

            pre_norm(X, gain_of(0, 0))
            for t in range(8):
                evac(SQT[:, t, :], S)
            for t in range(8):
                evac(SKT[:, t, :], S)
            for c in range(2):
                for t in range(ST):
                    evac(SV[:, t, c * BRANCH:(c + 1) * BRANCH], BRANCH)
            v.wait_ge(banks.freed["v"], banks.frees["v"])
            stamp().then_inc(qkv_ready.sem, qkv_ready.up())

            def bc4(x):
                return x.unsqueeze(1).broadcast_to([P, 4, 384])

            def sb_abs(b):
                z, e, L, p = SBUFS[4 * (b % 2):4 * (b % 2) + 4]
                v.wait_ge(z_copied.sem, z_copied.nth("v"))
                ve.scalar_tensor_tensor(e, z, -1.0, z, ALU.mult, ALU.min).then_inc(z_abs.sem, z_abs.up())

            def sb_rest(b):
                z, e, L, p = SBUFS[4 * (b % 2):4 * (b % 2) + 4]
                v.wait_ge(l_ready.sem, l_ready.nth("v"))
                ve.scalar_tensor_tensor(L, z, 0.0, e, ALU.max, ALU.add).then_inc(v_step.sem, v_step.up())
                v.wait_ge(v_step.sem, v_step.made)
                ve.tensor_tensor(L, L, bc4(cst("sb_keep")), ALU.mult).then_inc(L_ready.sem, L_ready.up())
                ve.tensor_tensor(z, z, bc4(cst("sb_neg")), ALU.add).then_inc(v_step.sem, v_step.up())
                v.wait_ge(v_step.sem, v_step.made)
                for j in range(4):
                    o = banks.take("v")
                    v.wait_ge(banks.filled, banks.at["v"])
                    ve.tensor_tensor(z[:, j, :], o[:, 0:384], z[:, j, :], ALU.add).then_inc(banks.freed["v"], banks.free("v"))
                v.wait_ge(banks.freed["v"], banks.frees["v"])
                stamp().then_inc(t_ready.sem, t_ready.up())
                for j in range(2):
                    evac(SOT[:, 2 * b + j, :], S)

            sb_abs(0)
            for b in range(SB_HEADS // 4):
                if b + 1 < SB_HEADS // 4:
                    sb_abs(b + 1)
                sb_rest(b)
            v.wait_ge(banks.freed["v"], banks.frees["v"])
            stamp().then_inc(o_ready.sem, o_ready.up())
            mixer_out(SM, gain_of(0, 1))
            ffn(0)

            pre_norm(X, gain_of(1, 0))
            for t in range(12):
                evac(DQT[:, t, :], S)
            for t in range(12):
                evac(DKT[:, t, :], S)
            for g in range(3):
                for t in range(ST):
                    evac(DV[:, t, g * BRANCH:(g + 1) * BRANCH], BRANCH)
            v.wait_ge(banks.freed["v"], banks.frees["v"])
            stamp().then_inc(qkv_ready.sem, qkv_ready.up())
            items = [(h, t) for h in range(DIL_HEADS) for t in range(ST)]
            v.wait_ge(loads["bias_in"], 16)

            def normalise(n, s):
                v.wait_ge(exp_ready.sem, exp_ready.nth("v"))
                ve.reciprocal(rsum[:, n % 2, 0:1], ssum[:, n % 2, 0:1]).then_inc(v_step.sem, v_step.up())
                v.wait_ge(v_step.sem, v_step.made)
                ve.tensor_scalar(s, s, rsum[:, n % 2, 0:1], None, ALU.mult).then_inc(p_ready.sem, p_ready.up())

            def dil_soft(n):
                h, t = items[n]
                k = (t + 1) * P
                s = DS[n % 2][:, :, 0:k]
                for g in range(3):
                    o = banks.take("v")
                    v.wait_ge(banks.filled, banks.at["v"])
                    ve.scalar_tensor_tensor(s[:, g, :], o[:, 0:k], SCALE, DB[:, g * DIL_HEADS + h, S - k:S], ALU.mult, ALU.add).then_inc(banks.freed["v"], banks.free("v"))
                v.wait_ge(banks.freed["v"], banks.frees["v"])
                ve.tensor_reduce(nmax[:, n % 2, 0:1], s, AX.XY, ALU.max, negate=True).then_inc(max_ready.sem, max_ready.up())

            def dil_rest(n):
                h, t = items[n]
                normalise(n, DS[n % 2][:, :, 0:(t + 1) * P])
                o = banks.take("v")
                v.wait_ge(banks.filled, banks.at["v"])
                r = DH * (h % 2)
                ve.tensor_copy(DOT[r:r + DH, h // 2, t * P:(t + 1) * P], o[r:r + DH, 0:P]).then_inc(banks.freed["v"], banks.free("v"))

            def skewed(n, first, second):
                first(0)
                for i in range(n):
                    if i + 1 < n:
                        first(i + 1)
                    second(i)

            skewed(len(items), dil_soft, dil_rest)
            v.wait_ge(banks.freed["v"], banks.frees["v"])
            stamp().then_inc(o_ready.sem, o_ready.up())
            mixer_out(SM, gain_of(1, 1))
            ffn(1)

            stamp().then_inc(dma_free.sem, dma_free.up())
            stamp().then_inc(gate_ready.sem, gate_ready.up())
            v.wait_ge(gate_exp.sem, gate_exp.nth("v"))
            ve.scalar_tensor_tensor(silu_c, silu_c, 1.0, sc16, ALU.add, ALU.mult).then_inc(v_step.sem, v_step.up())
            v.wait_ge(v_step.sem, v_step.made)
            ve.tensor_scalar(silu_c, silu_c, 0.5, None, ALU.mult).then_inc(sc_ready.sem, sc_ready.up())

            def modulated_norm(i, which, ns):
                sh, sc = mod[:, 24 * which:24 * which + 8, :], mod[:, 24 * which + 8:24 * which + 16, :]
                g = g_norm[which][:, i * KT:(i + 1) * KT]
                for s in range(ns):
                    ins = ve.scalar_tensor_tensor(ampl[:, :, s], sc[:, :, s], 1.0, g, ALU.add, ALU.mult)
                ins.then_inc(v_step.sem, v_step.up())
                v.wait_ge(v_step.sem, v_step.made)
                v.wait_ge(rstd_ready.sem, rstd_ready.nth("v"))
                for s in range(ns):
                    for k in range(KT):
                        t = slice(s * S, (s + 1) * S)
                        ins = ve.scalar_tensor_tensor(H[:, k, t], X[:, k, t], ampl[:, k, s:s + 1], rstd[:, t], ALU.mult, ALU.mult)
                ins.then_inc(v_step.sem, v_step.up())
                v.wait_ge(v_step.sem, v_step.made)
                for s in range(ns):
                    for k in range(KT):
                        t = slice(s * S, (s + 1) * S)
                        ins = ve.tensor_scalar(H[:, k, t], H[:, k, t], sh[:, k, s:s + 1], None, ALU.add)
                ins.then_inc(h_ready.sem, h_ready.up())

            def add_gated(which, ns):
                gt = mod[:, 24 * which + 16:24 * which + 24, :]
                for f in range(KT):
                    o = banks.take("v")
                    v.wait_ge(banks.filled, banks.at["v"])
                    for s in range(ns):
                        t = slice(s * S, (s + 1) * S)
                        ins = ve.scalar_tensor_tensor(X[:, f, t], o[:, t], gt[:, f, s:s + 1], X[:, f, t], ALU.mult, ALU.add)
                    ins.then_inc(banks.freed["v"], banks.free("v"))
                v.wait_ge(banks.freed["v"], banks.frees["v"])
                stamp().then_inc(src_ready.sem, src_ready.up())

            for i in range(DEPTH):
                last = i == DEPTH - 1
                ns = 1 if last else 2
                qtok, qtiles = ns * S, ns * ST
                bada = b_ada[:, i * N_MOD * KT:(i + 1) * N_MOD * KT]
                for c in range(N_MOD * D // BRANCH):
                    o = banks.take("v")
                    v.wait_ge(banks.filled, banks.at["v"])
                    ve.tensor_tensor(mod[:, 4 * c:4 * c + 4, :], o[:, 0:8].rearrange("p (f s) -> p f s", s=2),
                                          bada[:, 4 * c:4 * c + 4].unsqueeze(2).broadcast_to([P, 4, 2]), ALU.add).then_inc(banks.freed["v"], banks.free("v"))
                v.wait_ge(banks.freed["v"], banks.frees["v"])
                ve.tensor_scalar(mod[:, 16:24, :], mod[:, 16:24, :], 0.5, None, ALU.mult).then_inc(v_step.sem, v_step.up())
                v.wait_ge(v_step.sem, v_step.made)
                v.wait_ge(loads["lam"], 64 * (i + 1))
                ve.tensor_tensor(LAMV[:, 0, :], LAMV[:, 0, :], LAMV[:, 1, :], ALU.mult).then_inc(v_step.sem, v_step.up())
                v.wait_ge(v_step.sem, v_step.made)
                ve.tensor_tensor(LAMV[:, 2, :], LAMV[:, 2, :], LAMV[:, 3, :], ALU.mult).then_inc(v_step.sem, v_step.up())
                v.wait_ge(v_step.sem, v_step.made)
                ve.tensor_reduce(lam2[:, 0:1], LAMV[:, 0, :], AX.X, ALU.add).then_inc(v_step.sem, v_step.up())
                v.wait_ge(v_step.sem, v_step.made)
                ve.tensor_reduce(lam2[:, 1:2], LAMV[:, 2, :], AX.X, ALU.add).then_inc(lam_ready.sem, lam_ready.up())
                v.wait_ge(lam_exp.sem, lam_exp.nth("v"))
                lam_init = 0.8 - 0.6 * math.exp(-0.3 * i)
                ve.tensor_tensor(neg_lam, lam2[:, 1:2], lam2[:, 0:1], ALU.subtract).then_inc(v_step.sem, v_step.up())
                v.wait_ge(v_step.sem, v_step.made)
                ve.tensor_scalar(neg_lam, neg_lam, -lam_init, None, ALU.add).then_inc(v_step.sem, v_step.up())
                v.wait_ge(v_step.sem, v_step.made)
                ve.tensor_scalar(g_head, subln[:, i:i + 1], 1.0 - lam_init, None, ALU.mult).then_inc(v_step.sem, v_step.up())
                v.wait_ge(v_step.sem, v_step.made)
                ws = banks.take("v")
                v.wait_ge(banks.filled, banks.at["v"])
                ve.tensor_copy(WST.rearrange("p g c -> p (g c)"), ws).then_inc(banks.freed["v"], banks.free("v"))
                v.wait_ge(banks.freed["v"], banks.frees["v"])
                modulated_norm(i, 0, 2)

                for g in range(4):
                    evac(UT[:, g, 0:qtok], qtok)
                for t in range(qtiles):
                    evac(VG[:, t, :], 512)
                v.wait_ge(banks.freed["v"], banks.frees["v"])

                def gelu(x, t):
                    ve.tensor_tensor(t, x, x, ALU.mult).then_inc(v_step.sem, v_step.up())
                    v.wait_ge(v_step.sem, v_step.made)
                    ve.tensor_scalar(t, t, 0.044715, 1.0, ALU.mult, ALU.add).then_inc(v_step.sem, v_step.up())
                    v.wait_ge(v_step.sem, v_step.made)
                    ve.tensor_tensor(t, t, x, ALU.mult).then_inc(gate_ready.sem, gate_ready.up())
                    v.wait_ge(gate_exp.sem, gate_exp.nth("v"))
                    ve.scalar_tensor_tensor(x, t, 1.0, x, ALU.add, ALU.mult).then_inc(v_step.sem, v_step.up())
                    v.wait_ge(v_step.sem, v_step.made)

                gelu(VG[:, 0:qtiles, :], TG[:, 0:qtiles, :])
                vg = VG[:, 0:qtiles, :]

                def rows(x):
                    return x.unsqueeze(2).broadcast_to([P, qtiles, 512])

                def all_tiles(x):
                    return x.unsqueeze(1).broadcast_to([P, qtiles, 512])

                m, var, rs = (stat[:, j, 0:qtiles] for j in range(3))
                ve.tensor_reduce(m, vg, AX.X, ALU.add).then_inc(v_step.sem, v_step.up())
                v.wait_ge(v_step.sem, v_step.made)
                ve.tensor_scalar(m, m, -0.5 / BRANCH, None, ALU.mult).then_inc(v_step.sem, v_step.up())
                v.wait_ge(v_step.sem, v_step.made)
                ve.scalar_tensor_tensor(vg, vg, 0.5, rows(m), ALU.mult, ALU.add).then_inc(v_step.sem, v_step.up())
                v.wait_ge(v_step.sem, v_step.made)
                ve.tensor_tensor(TG[:, 0:qtiles, :], vg, vg, ALU.mult).then_inc(v_step.sem, v_step.up())
                v.wait_ge(v_step.sem, v_step.made)
                ve.tensor_reduce(var, TG[:, 0:qtiles, :], AX.X, ALU.add).then_inc(ln_rstd.sem, ln_rstd.up())
                v.wait_ge(rstd_ready.sem, rstd_ready.nth("v"))
                ve.tensor_tensor(vg, vg, rows(rs), ALU.mult).then_inc(v_step.sem, v_step.up())
                v.wait_ge(v_step.sem, v_step.made)
                v.wait_ge(loads["gm"], 64 * (i + 1))
                ve.tensor_tensor(vg, vg, all_tiles(GMR[:, 0, :]), ALU.mult).then_inc(v_step.sem, v_step.up())
                v.wait_ge(v_step.sem, v_step.made)
                ve.tensor_tensor(vg, vg, all_tiles(GMR[:, 1, :]), ALU.add).then_inc(ln_ready.sem, ln_ready.up())
                gelu(UT[:, :, 0:qtok], TG[:, :, 0:qtok])
                for g in range(4):
                    o = banks.take("v")
                    v.wait_ge(banks.filled, banks.at["v"])
                    ve.tensor_tensor(YCU[:, g, 0:qtok].rearrange("p (t q) -> p t q", q=P),
                                          o[:, 0:qtok].rearrange("p (t q) -> p t q", q=P),
                                          GMR[:, 2, g * P:(g + 1) * P].unsqueeze(1).broadcast_to([P, qtiles, P]), ALU.add).then_inc(banks.freed["v"], banks.free("v"))
                v.wait_ge(banks.freed["v"], banks.frees["v"])
                ve.scalar_tensor_tensor(YCU[:, :, 0:qtok], YCU[:, :, 0:qtok], 0.5, UT[:, :, 0:qtok], ALU.mult, ALU.mult).then_inc(y_ready.sem, y_ready.up())
                v.wait_ge(y_ready.sem, y_ready.made)

                for c in range(4):
                    evac(KT2[:, c, :], 2 * S)
                for t in range(4):
                    evac(V2[:, t, :], 512)
                for c in range(4):
                    evac(QT2[:, c, 0:qtok], qtok)
                v.wait_ge(banks.freed["v"], banks.frees["v"])
                stamp().then_inc(qkv_ready.sem, qkv_ready.up())
                v.wait_ge(loads["rpb_in"], 256 * (i + 1))
                ve.tensor_tensor(BN.rearrange("p h r c -> p (h r) c"), BN.rearrange("p h r c -> p (h r) c"),
                                                cst("col_neg").unsqueeze(1).broadcast_to([P, NA_HEADS * NA_DR, GRID_W]), ALU.add).then_inc(bias_tile.sem, bias_tile.up())
                v.wait_ge(bias_tile.sem, bias_tile.made)
                items = [(h, t) for h in range(NA_HEADS) for t in range(qtiles)]

                def na_soft(n):
                    h, t = items[n]
                    s = S2[n % 2][:, 0, :]
                    o = banks.take("v")
                    v.wait_ge(banks.filled, banks.at["v"])
                    if t < ST:
                        ve.scalar_tensor_tensor(s[:, 0:S].rearrange("p (r c) -> p r c", c=GRID_W),
                                                     o[:, 0:S].rearrange("p (r c) -> p r c", c=GRID_W), SCALE,
                                                     BN[:, h, 2 - 2 * t:6 - 2 * t, :], ALU.mult, ALU.add).then_inc(v_step.sem, v_step.up())
                    ve.tensor_scalar(s[:, S:2 * S], o[:, S:2 * S], SCALE, None, ALU.mult).then_inc(banks.freed["v"], banks.free("v"))
                    v.wait_ge(banks.freed["v"], banks.frees["v"])
                    if t >= ST:
                        s = s[:, S:2 * S]
                    ve.tensor_reduce(nmax[:, n % 2, 0:1], s, AX.X, ALU.max, negate=True).then_inc(max_ready.sem, max_ready.up())

                def na_rest(n):
                    h, t = items[n]
                    k0 = 0 if t < ST else S
                    normalise(n, S2[n % 2][:, 0, k0:2 * S])
                    o = banks.take("v")
                    v.wait_ge(banks.filled, banks.at["v"])
                    r = DH * (h % 2)
                    ve.tensor_copy(Y2[0][r:r + DH, h // 2, t * P:(t + 1) * P], o[r:r + DH, 0:P]).then_inc(banks.freed["v"], banks.free("v"))

                skewed(len(items), na_soft, na_rest)

                for c in range(4):
                    evac(KT2[:, c, :], 2 * S)
                for t in range(4):
                    evac(V2[:, t, :], 512)
                for c in range(4):
                    evac(QT2[:, c, 0:qtok], qtok)
                v.wait_ge(banks.freed["v"], banks.frees["v"])
                stamp().then_inc(qkv_ready.sem, qkv_ready.up())
                for T in (KT2, QT2):
                    for c in range(4):
                        o = banks.take("v")
                        v.wait_ge(banks.filled, banks.at["v"])
                        ve.tensor_tensor(ROPE_T, o[:, 0:S], cst("sin"), ALU.mult).then_inc(banks.freed["v"], banks.free("v"))
                        v.wait_ge(banks.freed["v"], banks.frees["v"])
                        ve.tensor_tensor(T[:, c, 0:S], T[:, c, 0:S], cst("cos"), ALU.mult).then_inc(v_step.sem, v_step.up())
                        v.wait_ge(v_step.sem, v_step.made)
                        ve.tensor_tensor(T[:, c, 0:S], T[:, c, 0:S], ROPE_T, ALU.add).then_inc(v_step.sem, v_step.up())
                        v.wait_ge(v_step.sem, v_step.made)
                stamp().then_inc(rope_ready.sem, rope_ready.up())
                items = [(h, t) for h in range(DA_HEADS) for t in range(qtiles)]

                def da_soft(n):
                    h, t = items[n]
                    k0 = 0 if t < ST else S
                    for c in range(2):
                        o = banks.take("v")
                        v.wait_ge(banks.filled, banks.at["v"])
                        ve.tensor_reduce(nmax[:, n % 2, c:c + 1], o[:, k0:2 * S], AX.X, ALU.max, negate=True).then_inc(v_step.sem, v_step.up())
                        v.wait_ge(v_step.sem, v_step.made)
                    ve.tensor_scalar(nmax[:, n % 2, 0:2], nmax[:, n % 2, 0:2], SCALE, None, ALU.mult).then_inc(max_ready.sem, max_ready.up())

                def da_rest(n):
                    h, t = items[n]
                    k0 = 0 if t < ST else S
                    e0, e1 = S2[n % 2][:, 0, k0:2 * S], S2[n % 2][:, 1, k0:2 * S]
                    v.wait_ge(exp_ready.sem, exp_ready.nth("v"))
                    ve.reciprocal(rsum[:, n % 2, 0:2], ssum[:, n % 2, 0:2]).then_inc(v_step.sem, v_step.up())
                    v.wait_ge(v_step.sem, v_step.made)
                    ve.tensor_tensor(rsum[:, n % 2, 1:2], rsum[:, n % 2, 1:2], neg_lam, ALU.mult).then_inc(v_step.sem, v_step.up())
                    v.wait_ge(v_step.sem, v_step.made)
                    ve.tensor_scalar(e0, e0, rsum[:, n % 2, 0:1], None, ALU.mult).then_inc(v_step.sem, v_step.up())
                    v.wait_ge(v_step.sem, v_step.made)
                    ve.scalar_tensor_tensor(e0, e1, rsum[:, n % 2, 1:2], e0, ALU.mult, ALU.add).then_inc(p_ready.sem, p_ready.up())
                    o = banks.take("v")
                    v.wait_ge(banks.filled, banks.at["v"])
                    ve.tensor_copy(O2[:, h, t * P:(t + 1) * P], o[:, 0:P]).then_inc(banks.freed["v"], banks.free("v"))

                skewed(len(items), da_soft, da_rest)
                v.wait_ge(banks.freed["v"], banks.frees["v"])
                ve.tensor_tensor(Y2[1][:, :, 0:qtok], O2[:, :, 0:qtok], O2[:, :, 0:qtok], ALU.mult).then_inc(sq_ready.sem, sq_ready.up())
                for h in range(DA_HEADS):
                    v.wait_ge(rstd_ready.sem, rstd_ready.nth("v"))
                    ins = ve.scalar_tensor_tensor(Y2[1][:, h, 0:qtok], O2[:, h, 0:qtok], g_head, S2[h // 2][:, h % 2, 0:qtok],
                                                  ALU.mult, ALU.mult)
                ins.then_inc(y_ready.sem, y_ready.up())
                v.wait_ge(y_ready.sem, y_ready.made)

                for b in range(3):
                    for half in range(2):
                        n = 2 * b + half
                        g = GS[n % 2][:, :, 0:qtok]
                        v.wait_ge(gate_exp.sem, gate_exp.nth("v"))
                        for f in range(4):
                            o = banks.take("v")
                            v.wait_ge(banks.filled, banks.at["v"])
                            ve.scalar_tensor_tensor(MB[:, 4 * half + f, 0:qtok] if b == 0 else g[:, f, :], g[:, f, :], 1.0,
                                                    o[:, 0:qtok], ALU.add, ALU.mult
                                                    ).then_inc(banks.freed["v"], banks.free("v"))
                        v.wait_ge(banks.freed["v"], banks.frees["v"])
                        m = MB[:, 4 * half:4 * half + 4, 0:qtok]
                        if b:
                            ve.tensor_tensor(m, m, g, ALU.add).then_inc(gate_used.sem, gate_used.up())
                            v.wait_ge(gate_used.sem, gate_used.made)
                        else:
                            stamp().then_inc(gate_used.sem, gate_used.up())
                stamp().then_inc(merged_ready.sem, merged_ready.up())
                add_gated(0, ns)

                modulated_norm(i, 1, ns)
                o = banks.take("v")
                v.wait_ge(banks.filled, banks.at["v"])
                lg = o[:, 0:qtiles * N_EXPERTS].rearrange("p (t e) -> p t e", e=N_EXPERTS)
                ve.tensor_reduce(mx4[:, 0:qtiles], lg, AX.X, ALU.max, negate=True).then_inc(v_step.sem, v_step.up())
                v.wait_ge(v_step.sem, v_step.made)
                stamp().then_inc(max_ready.sem, max_ready.up())
                v.wait_ge(exp_ready.sem, exp_ready.nth("v"))
                ve.reciprocal(rden[:, 0:qtiles], den4[:, 0:qtiles]).then_inc(v_step.sem, v_step.up())
                v.wait_ge(v_step.sem, v_step.made)
                for t in range(qtiles):
                    af = aff[:, t % 2, t // 2, :]
                    ins = ve.tensor_scalar(af, af, rden[:, t:t + 1], None, ALU.mult)
                    if t < qtiles - 1:
                        ins.then_inc(v_step.sem, v_step.up())
                ins.then_inc(aff_ready.sem, aff_ready.up())
                nr = ns * N_EXPERTS
                o = banks.take("v")
                v.wait_ge(banks.filled, banks.at["v"])
                at, aw, sc, keep = AT[0:nr, 0, :], AW[0:nr, :], AT[0:nr, 1, :], AT[0:nr, 0, :]
                ve.tensor_copy(aw, o[0:nr, 0:S]).then_inc(banks.freed["v"], banks.free("v"))
                v.wait_ge(banks.freed["v"], banks.frees["v"])
                for _ in range(CAP // 8):
                    ve.max(top8[0:nr], aw).then_inc(v_step.sem, v_step.up())
                    v.wait_ge(v_step.sem, v_step.made)
                    ve.match_replace(aw, top8[0:nr], aw, -1.0).then_inc(v_step.sem, v_step.up())
                    v.wait_ge(v_step.sem, v_step.made)
                ve.tensor_scalar(keep, aw, 0.0, None, ALU.is_lt).then_inc(v_step.sem, v_step.up())
                v.wait_ge(v_step.sem, v_step.made)
                for j in range(ST):
                    t = slice(j * P, (j + 1) * P)
                    ve.tensor_tensor_scan(sc[:, t], ones[0:nr, :], keep[:, t], sc[:, P - 1:P] if j else 0.0,
                                               ALU.mult, ALU.add).then_inc(v_step.sem, v_step.up())
                    v.wait_ge(v_step.sem, v_step.made)
                ve.tensor_tensor(sc, sc, keep, ALU.mult).then_inc(v_step.sem, v_step.up())
                v.wait_ge(v_step.sem, v_step.made)
                ve.tensor_scalar(aw, sc, -1.0, None, ALU.add).then_inc(pos_ready.sem, pos_ready.up())
                o = banks.take("v")
                v.wait_ge(banks.filled, banks.at["v"])
                ve.tensor_copy(pos[:, :, 0:nr], o[:, 0:64].rearrange("p (j r) -> p j r", j=ST)[:, :, 0:nr]).then_inc(banks.freed["v"], banks.free("v"))
                v.wait_ge(banks.freed["v"], banks.frees["v"])
                for j in range(ST):
                    ins = ve.tensor_tensor(SEL[:, j, 0:nr, :], pos[:, j, 0:nr].unsqueeze(2).broadcast_to([P, nr, CAP]),
                                           cst("iota").unsqueeze(1).broadcast_to([P, nr, CAP]), ALU.is_equal)
                    if j == 0:
                        ins.then_inc(v_step.sem, v_step.up())
                ins.then_inc(P_ready.sem, P_ready.up())
                v.wait_ge(P_ready.sem, P_ready.made)
                for j in range(ST):
                    ins = ve.tensor_tensor(GSEL[:, j, 0:nr, :], SEL[:, j, 0:nr, :],
                                           aff[:, j, 0:ns, :].rearrange("p q e -> p (q e)").unsqueeze(2).broadcast_to([P, nr, CAP]), ALU.mult)
                    if j == 0:
                        ins.then_inc(v_step.sem, v_step.up())
                ins.then_inc(G_ready.sem, G_ready.up())
                for k in range(KT):
                    for q in range(ns):
                        o = banks.take("v")
                        v.wait_ge(banks.filled, banks.at["v"])
                        ve.tensor_copy(XIN[:, k, :, q * CAP:(q + 1) * CAP], o.rearrange("p (e s) -> p e s", s=CAP)).then_inc(banks.freed["v"], banks.free("v"))
                v.wait_ge(banks.freed["v"], banks.frees["v"])
                stamp().then_inc(xin_ready.sem, xin_ready.up())
                w = ns * CAP
                for e in range(N_EXPERTS):
                    he, ge = HE[0][:, :, 0:w], HE[1][:, :, 0:w]
                    o1 = banks.take("v")[:, 0:8 * w].rearrange("p (f s) -> p f s", s=w)
                    v.wait_ge(banks.filled, banks.at["v"])
                    v.wait_ge(gate_exp.sem, gate_exp.nth("v"))
                    ve.scalar_tensor_tensor(ge, ge, 1.0, o1, ALU.add, ALU.mult).then_inc(banks.freed["v"], banks.free("v"))
                    v.wait_ge(banks.freed["v"], banks.frees["v"])
                    o = banks.take("v")
                    v.wait_ge(banks.filled, banks.at["v"])
                    o3 = o[:, 0:8 * w].rearrange("p (f s) -> p f s", s=w)
                    ve.scalar_tensor_tensor(he, ge, 0.5, o3, ALU.mult, ALU.mult).then_inc(banks.freed["v"], banks.free("v"))
                    v.wait_ge(banks.freed["v"], banks.frees["v"])
                    stamp().then_inc(hidden_ready.sem, hidden_ready.up())
                    v.wait_ge(hidden_ready.sem, hidden_ready.made)
                add_gated(1, ns)
                if not last:
                    stamp().then_inc(dma_free.sem, dma_free.up())

            pre_norm(X, g_final)

        @block.scalar
        def _(sc):
            se = nc.scalar
            stamps = [0]

            def stamp():
                stamps[0] += 1
                at = 1000 + stamps[0] % 24
                return se.activation(small[:, at:at + 1], eps, ACT.Copy)




            def inverse_root(dst, src, n, scale=1.0):
                se.activation(dst, src, ACT.Ln, bias=eps).then_inc(banks.freed["a"], banks.free("a"))
                sc.wait_ge(banks.freed["a"], banks.frees["a"])
                se.activation(dst, dst, ACT.Exp, scale=-0.5).then_inc(rstd_ready.sem, rstd_ready.up())

            def norm(src, n):
                sc.wait_ge(src_ready.sem, src_ready.nth("a"))
                se.activation(H[:, :, 0:n], src[:, :, 0:n], ACT.Square).then_inc(sq_ready.sem, sq_ready.up())
                o = banks.take("a")
                sc.wait_ge(banks.filled, banks.at["a"])
                inverse_root(rstd[:, 0:n], o[:, 0:n], n)

            def gate(x, src=None, scale=0.5):
                sc.wait_ge(gate_ready.sem, gate_ready.nth("a"))
                se.activation(x, x if src is None else src, ACT.Tanh, scale=scale).then_inc(gate_exp.sem, gate_exp.up())

            def ffn():
                norm(X, S)
                for j in range(FT // 2):
                    gate(GE[j % 2], GU[j % 2][:, 0:2, :])
                norm(SM, S)

            norm(X, S)

            def sb_first(b):
                z, e, L, p = SBUFS[4 * (b % 2):4 * (b % 2) + 4]
                for j in range(4):
                    o = banks.take("a")
                    sc.wait_ge(banks.filled, banks.at["a"])
                    se.activation(z[:, j, :], o[:, 0:384], ACT.Copy, scale=SCALE).then_inc(banks.freed["a"], banks.free("a"))
                sc.wait_ge(banks.freed["a"], banks.frees["a"])
                stamp().then_inc(z_copied.sem, z_copied.up())
                sc.wait_ge(z_abs.sem, z_abs.nth("a"))
                se.activation(e, e, ACT.Exp).then_inc(a_step.sem, a_step.up())
                sc.wait_ge(a_step.sem, a_step.made)
                se.activation(e, e, ACT.Ln, bias=1.0).then_inc(l_ready.sem, l_ready.up())

            def sb_second(b):
                z, e, L, p = SBUFS[4 * (b % 2):4 * (b % 2) + 4]
                sc.wait_ge(t_ready.sem, t_ready.nth("a"))
                se.activation(p, z, ACT.Exp).then_inc(sb_p_ready.sem, sb_p_ready.up())

            sb_first(0)
            for b in range(SB_HEADS // 4):
                if b + 1 < SB_HEADS // 4:
                    sb_first(b + 1)
                sb_second(b)
            norm(SM, S)
            ffn()

            norm(X, S)
            items = [(h, t) for h in range(DIL_HEADS) for t in range(ST)]

            def row_exp(n, s, k=0, src=None, scale=1.0):
                return se.activation(s, s if src is None else src, ACT.Exp, bias=nmax[:, n % 2, k:k + 1], scale=scale,
                                     accum_out=ssum[:, n % 2, k:k + 1])

            def dil_exp(n):
                h, t = items[n]
                sc.wait_ge(max_ready.sem, max_ready.nth("a"))
                row_exp(n, DS[n % 2][:, :, 0:(t + 1) * P]).then_inc(exp_ready.sem, exp_ready.up())

            def dil_pt(n):
                h, t = items[n]
                tiles = 3 * (t + 1)
                for n0 in range(0, tiles, 4):
                    m = min(4, tiles - n0)
                    o = banks.take("a")
                    sc.wait_ge(banks.filled, banks.at["a"])
                    se.activation(DPT[n % 2][:, n0:n0 + m, :].rearrange("p a b -> p (a b)"), o[:, 0:m * P], ACT.Copy).then_inc(banks.freed["a"], banks.free("a"))
                sc.wait_ge(banks.freed["a"], banks.frees["a"])
                stamp().then_inc(pt_ready.sem, pt_ready.up())

            def skewed(n, first, second):
                first(0)
                for i in range(n):
                    if i + 1 < n:
                        first(i + 1)
                    second(i)

            skewed(len(items), dil_exp, dil_pt)
            norm(SM, S)
            ffn()
            gate(silu_c, sc16)

            for i in range(DEPTH):
                last = i == DEPTH - 1
                ns = 1 if last else 2
                qtok, qtiles = ns * S, ns * ST
                sc.wait_ge(lam_ready.sem, lam_ready.nth("a"))
                se.activation(lam2, lam2, ACT.Exp).then_inc(lam_exp.sem, lam_exp.up())
                norm(X, 2 * S)
                gelu_scale = math.sqrt(2.0 / math.pi)
                gates_before = 6 * i
                gate(TG[:, 0:qtiles, :], scale=gelu_scale)
                sc.wait_ge(ln_rstd.sem, ln_rstd.nth("a"))
                se.activation(stat[:, 2, 0:qtiles], stat[:, 1, 0:qtiles], ACT.Ln, bias=eps, scale=1.0 / BRANCH).then_inc(a_step.sem, a_step.up())
                sc.wait_ge(a_step.sem, a_step.made)
                se.activation(stat[:, 2, 0:qtiles], stat[:, 2, 0:qtiles], ACT.Exp, scale=-0.5).then_inc(rstd_ready.sem, rstd_ready.up())
                gate(TG[:, :, 0:qtok], scale=gelu_scale)
                items = [(h, t) for h in range(NA_HEADS) for t in range(qtiles)]

                def pt_copy(n, t):
                    k0 = 0 if t < ST else ST
                    o = banks.take("a")
                    sc.wait_ge(banks.filled, banks.at["a"])
                    se.activation(PT2[n % 2].rearrange("p a b -> p (a b)")[:, k0 * P:512], o[:, k0 * P:512], ACT.Copy).then_inc(banks.freed["a"], banks.free("a"))
                    sc.wait_ge(banks.freed["a"], banks.frees["a"])
                    stamp().then_inc(pt_ready.sem, pt_ready.up())

                def na_exp(n):
                    h, t = items[n]
                    sc.wait_ge(max_ready.sem, max_ready.nth("a"))
                    row_exp(n, S2[n % 2][:, 0, (0 if t < ST else S):2 * S]).then_inc(exp_ready.sem, exp_ready.up())

                skewed(len(items), na_exp, lambda n: pt_copy(n, items[n][1]))
                items = [(h, t) for h in range(DA_HEADS) for t in range(qtiles)]

                def da_exp(n):
                    h, t = items[n]
                    k0 = 0 if t < ST else S
                    sc.wait_ge(max_ready.sem, max_ready.nth("a"))
                    for c in range(2):
                        o = banks.take("a")
                        sc.wait_ge(banks.filled, banks.at["a"])
                        row_exp(n, S2[n % 2][:, c, k0:2 * S], c, o[:, k0:2 * S], SCALE).then_inc(banks.freed["a"], banks.free("a"))
                    sc.wait_ge(banks.freed["a"], banks.frees["a"])
                    stamp().then_inc(exp_ready.sem, exp_ready.up())

                skewed(len(items), da_exp, lambda n: pt_copy(n, items[n][1]))
                for h in range(DA_HEADS):
                    o = banks.take("a")
                    sc.wait_ge(banks.filled, banks.at["a"])
                    inverse_root(S2[h // 2][:, h % 2, 0:qtok], o[:, 0:qtok], qtok)
                for n in range(6):
                    if n >= 2:
                        sc.wait_ge(gate_used.sem, gates_before + n - 1)
                    for f in range(4):
                        o = banks.take("a")
                        sc.wait_ge(banks.filled, banks.at["a"])
                        se.activation(GS[n % 2][:, f, 0:qtok], o[:, 0:qtok], ACT.Tanh, scale=0.5
                                      ).then_inc(banks.freed["a"], banks.free("a"))
                    sc.wait_ge(banks.freed["a"], banks.frees["a"])
                    stamp().then_inc(gate_exp.sem, gate_exp.up())
                norm(X, qtok)

                o = banks.take("a")
                sc.wait_ge(banks.filled, banks.at["a"])
                sc.wait_ge(max_ready.sem, max_ready.nth("a"))
                for t in range(qtiles):
                    ins = se.activation(aff[:, t % 2, t // 2, :], o[:, t * N_EXPERTS:(t + 1) * N_EXPERTS], ACT.Exp,
                                        bias=mx4[:, t:t + 1], accum_out=den4[:, t:t + 1])
                ins.then_inc(banks.freed["a"], banks.free("a"))
                sc.wait_ge(banks.freed["a"], banks.frees["a"])
                stamp().then_inc(exp_ready.sem, exp_ready.up())
                for t in range(qtiles):
                    for half in range(2):
                        o = banks.take("a")
                        sc.wait_ge(banks.filled, banks.at["a"])
                        se.activation(HT[:, t, half * 512:(half + 1) * 512], o, ACT.Copy).then_inc(banks.freed["a"], banks.free("a"))
                sc.wait_ge(banks.freed["a"], banks.frees["a"])
                stamp().then_inc(tok_ready.sem, tok_ready.up())
                for q in range(ns):
                    for half in range(2):
                        o = banks.take("a")
                        sc.wait_ge(banks.filled, banks.at["a"])
                        se.activation(PGT[:, q, 2 * half:2 * half + 2, :].rearrange("p k t -> p (k t)"), o, ACT.Copy).then_inc(banks.freed["a"], banks.free("a"))
                for e in range(N_EXPERTS):
                    o = banks.take("a")
                    sc.wait_ge(banks.filled, banks.at["a"])
                    se.activation(HE[1][:, :, 0:ns * CAP], o[:, 0:8 * ns * CAP].rearrange("p (f s) -> p f s", f=8), ACT.Tanh,
                                  scale=0.5).then_inc(gate_exp.sem, gate_exp.up())
                    for half in range(2):
                        o = banks.take("a")
                        sc.wait_ge(banks.filled, banks.at["a"])
                        for q in range(ns):
                            r = CAP * (e % 4)
                            ins = se.activation(YE[q][r:r + CAP, e // 4, half * 512:(half + 1) * 512],
                                                o[q * CAP:(q + 1) * CAP, :], ACT.Copy)
                        ins.then_inc(banks.freed["a"], banks.free("a"))
                sc.wait_ge(banks.freed["a"], banks.frees["a"])
                stamp().then_inc(ye_ready.sem, ye_ready.up())
            norm(X, S)
            for t in range(ST):
                for half in range(2):
                    o = banks.take("a")
                    sc.wait_ge(banks.filled, banks.at["a"])
                    se.activation(OUTT[:, t, half * 512:(half + 1) * 512], o, ACT.Copy).then_inc(banks.freed["a"], banks.free("a"))
            sc.wait_ge(banks.freed["a"], banks.frees["a"])
            stamp().then_inc(final_ready.sem, final_ready.up())

        @block.gpsimd
        def _(gp):
            def dram(ap, offset, dims):
                return bass.AP(tensor=ap.tensor, offset=offset, ap=dims)

            gp.wait_ge(bias_rows.sem, bias_rows.nth("gp"))
            gp.dma_start(bias_scratch.rearrange("(g h) n -> h g n", g=3),
                         view(DROW, 3, 384)[0:DIL_HEADS]).then_inc(loads["bias_out"], 16)
            gp.wait_ge(loads["bias_out"], 16)
            gp.dma_start(dram(bias_shear, 0, [[P * 386, 3 * DIL_HEADS], [385, P], [1, 384]]),
                         dram(bias_scratch, 0, [[384, 3 * DIL_HEADS], [0, P], [1, 384]])).then_inc(loads["bias_shear"], 16)
            gp.wait_ge(loads["bias_shear"], 16)
            gp.wait_ge(o_ready.sem, 1)
            gp.dma_start(DB, dram(bias_shear, P - 1, [[384, P], [P * 386, 3 * DIL_HEADS], [1, S]])).then_inc(loads["bias_in"], 16)
            gp.dma_start(rpb_scratch, a["zero_table"]).then_inc(loads["rpb_out"], 16)
            gp.wait_ge(loads["rpb_out"], 16)
            for i in range(DEPTH):
                gp.wait_ge(dma_free.sem, dma_free.nth("gp"))
                for n, name in enumerate(("da_lam_q1_2", "da_lam_k1_2", "da_lam_q2_2", "da_lam_k2_2")):
                    gp.dma_start(LAMV[:, n, :], dram(a[name], i * DH, [[0, P], [1, DH]])).then_inc(loads["lam"], 16)
                gp.dma_start(WS_RAW, a["gm_w_s_2"][i].rearrange("g p q -> p g q")).then_inc(loads["gm"], 16)
                for n, name in enumerate(("gm_ln_g_2", "gm_ln_b_2", "gm_b_s_2")):
                    gp.dma_start(GMR[:, n, :], dram(a[name], i * BRANCH, [[0, P], [1, BRANCH]])).then_inc(loads["gm"], 16)
                gp.dma_start(WR, a["w_router_2"][i].rearrange("(k p) e -> p k e", p=P)).then_inc(loads["router"], 16)
                gp.dma_start(rpb_scratch[:, :, 48:48 + 2 * NA_WIN_C - 1], a["na_rpb_2"][i]).then_inc(loads["rpb_out"], 16)
                gp.wait_ge(loads["rpb_out"], 16 * (i + 2))
                for h in range(NA_HEADS):
                    gp.dma_start(dram(rpb_shear, h * (NA_DR + 1) * GRID_W * 130, [[GRID_W * 130, NA_DR + 1], [129, GRID_W], [1, P]]),
                                 dram(rpb_scratch, (h * 15 + 4) * P, [[P, NA_DR + 1], [0, GRID_W], [1, P]])
                                 ).then_inc(loads["rpb_shear"], 16)
                gp.wait_ge(loads["rpb_shear"], 16 * NA_HEADS * (i + 1))
                for hh in range(2):
                    for h in range(NA_HEADS):
                        gp.dma_start(BN[hh * GRID_W:(hh + 1) * GRID_W, h, :, :],
                                     dram(rpb_shear, (h * (NA_DR + 1) + 1 - hh) * GRID_W * 130 + GRID_W - 1,
                                          [[P, GRID_W], [GRID_W * 130, NA_DR], [1, GRID_W]])).then_inc(loads["rpb_in"], 16)
                gp.wait_ge(loads["rpb_in"], 256 * (i + 1))


_INS = ['x', 'rel_bias', 'norm_gains', 'sb_w_qkv', 'sb_w_o', 'dil_w_qkv', 'dil_w_o', 'ffn_w_up', 'ffn_conv_w',
        'ffn_conv_b', 'ffn_w_down', 'c_2', 'ctx_2', 'c_ctx_2', 'w_ada_2', 'b_ada_2', 'g_norm1_2', 'g_norm2_2',
        'w_in_2', 'na_rpb_2', 'da_lam_q1_2', 'da_lam_k1_2', 'da_lam_q2_2', 'da_lam_k2_2', 'da_subln_g_2',
        'gm_ln_g_2', 'gm_ln_b_2', 'gm_w_s_2', 'gm_b_s_2', 'w_branch_2', 'w_out_2', 'w_router_2', 'w_e1_2',
        'w_e3_2', 'w_e2_2', 'g_final_2']


def kernel(**inputs):
    import concourse.bacc as bacc
    from concourse.bass_utils import run_bass_kernel_spmd as run

    nc = bacc.Bacc("TRN2", target_bir_lowering=False, num_devices=1)
    arrays, args = {}, {}
    given = {n: np.ascontiguousarray(inputs[n]) for n in _INS}
    given["const_table"] = constant_table()
    given["bucket_table"] = bucket_table()
    given["zero_table"] = np.zeros((NA_HEADS, 2 * NA_WIN_R - 1, P), np.float32)
    for name, v in given.items():
        arrays[f"in_{name}"] = v
        args[name] = nc.dram_tensor(f"in_{name}", v.shape, F32, kind="ExternalInput").ap()
    out = nc.dram_tensor("out", (1, S, D), F32, kind="ExternalOutput").ap()
    build(nc, args, out)
    r = run(nc, [arrays], core_ids=[0])
    return r.results[0]["out"]
```

```python
import math

import numpy as np
import concourse.bass as bass
from concourse import mybir
from concourse.alu_op_type import AluOpType as ALU

ACT = mybir.ActivationFunctionType
AX = mybir.AxisListType
F32 = mybir.dt.float32

P = 128
D = 1024
KT = D // P
S = 256
ST = S // P
DEPTH = 2
DH = 64
SCALE = DH ** -0.5
EPS = 1e-6
NEG = -1e30
SB_HEADS = 16
DIL = ((128, 1), (512, 4), (2048, 16))
DIL_HEADS = 8
N_BUCKETS, BUCKET_MAX_DIST = 32, 2048
D_FF = 2816
FT = D_FF // P
CONV_W = 3
GRID_W = 64
NA_HEADS, NA_WIN_R, NA_WIN_C = 8, 8, 16
NA_DR = 6
DA_HEADS = 4
BRANCH = 512
BT = BRANCH // P
GM_GROUPS = 4
N_EXPERTS, CAP = 16, 32
PROJ = 7168
N_MOD = 6
SLOT = 4 * BRANCH
SB_HALF = SB_HEADS // 4
LAG = 2
NSLOT = 7
NBANK = 8
MERGE_ORDER = (0, 2, 1)
GRP = 2
ADA_GAP = 3

C_AT, C_N = {}, 0
for _name, _w in (("ident", P), ("mean", P), ("mean_head", P), ("ones", P), ("suffix", P), ("rot", P),
                  ("cos", S), ("sin", S), ("sb_keep", 384), ("sb_neg", 384), ("iota", CAP), ("col_neg", GRID_W),
                  ("fold64", P), ("fold32", P)):
    C_AT[_name] = (C_N, C_N + _w)
    C_N += _w

ROWS = (("norm_gains", DEPTH * 4 * KT, 0, 0), ("c_2", KT, 0, 64), ("c_ctx_2", KT, 0, 72), ("g_final_2", KT, 0, 80),
        ("g_norm1_2", DEPTH * KT, 0, 88), ("g_norm2_2", DEPTH * KT, 0, 104), ("da_subln_g_2", DEPTH, 0, 120),
        ("ffn_conv_w", P, 1, 0), ("ffn_conv_w", P, 2, 0), ("ffn_conv_w", 8, 3, 0),
        ("ffn_conv_b", DEPTH * 2 * FT, 3, 8), ("b_ada_2", DEPTH * N_MOD * KT, 4, 0))
ROW_BLOCKS = (122, 128, 128, 96, 96)


def constant_table():
    t = np.zeros((P, C_N), np.float32)

    def put(name, v):
        t[:, slice(*C_AT[name])] = v

    k = np.arange(P)
    put("ident", np.eye(P))
    put("mean", 1.0 / D)
    put("mean_head", 1.0 / P)
    put("ones", 1.0)
    put("suffix", k[:, None] >= k[None, :])
    rot = np.zeros((P, P))
    for m in range(P):
        if m % 32 < 16:
            rot[m + 16, m] = -1.0
        else:
            rot[m - 16, m] = 1.0
    put("rot", rot)
    inv = 10000.0 ** (-np.arange(0, 32, 2, dtype=np.float32) / 32)
    tok = np.arange(S)
    at = np.where((k % 64 < 32)[:, None], (tok // GRID_W)[None], (tok % GRID_W)[None]).astype(np.float32)
    ang = at * inv.astype(np.float32)[k % 16][:, None]
    put("cos", np.cos(ang))
    put("sin", np.sin(ang))
    tri = (k[:, None] < k[None, :]).astype(np.float32)
    keep = np.concatenate([tri, np.ones((P, P)), tri], 1)
    put("sb_keep", -keep)
    put("sb_neg", np.where(keep > 0, 0.0, NEG))
    put("iota", np.arange(CAP)[None])
    col = np.arange(GRID_W)
    first = np.clip(col - NA_WIN_C // 2, 0, GRID_W - NA_WIN_C)
    inside = (col[None] >= first[:, None]) & (col[None] < first[:, None] + NA_WIN_C)
    put("col_neg", np.tile(np.where(inside, 0.0, NEG), (2, 1)))
    for w in (64, 32):
        put(f"fold{w}", (k[:, None] % w == k[None, :]) & (k[None, :] < w))
    return t


def bucket_table():
    t = np.zeros((N_BUCKETS + 1, 3 * 384), np.float32)
    exact = N_BUCKETS // 2
    for g, (window, r) in enumerate(DIL):
        for i in range(383):
            d = 255 - i
            if d < 0 or d % r or d // r > window // r:
                t[N_BUCKETS, g * 384 + i] = NEG
                continue
            x = np.float32(max(d, 1))
            large = exact + int(np.float32(np.log(x / np.float32(exact)) / np.float32(math.log(BUCKET_MAX_DIST / exact))
                                           * np.float32(N_BUCKETS - exact)))
            t[d if d < exact else min(large, N_BUCKETS - 1), g * 384 + i] = 1.0
    return t


class Signal:

    def __init__(self, sem):
        self.sem, self.made, self.taken = sem, 0, {}

    def up(self):
        self.made += 1
        return 1

    def nth(self, who):
        self.taken[who] = self.taken.get(who, 0) + 1
        return self.taken[who]


class Banks:

    def __init__(self, ps, filled, freed):
        self.ps, self.filled, self.freed = ps, filled, freed
        self.uses, self.at, self.frees, self.due = [], {}, {}, None

    def open(self, *readers):
        u = len(self.uses)
        last = self.uses[u - NBANK][-1] if u >= NBANK else None
        self.due = last and (self.freed[last], sum(r[-1] == last for r in self.uses[:u - NBANK + 1]))
        self.uses.append(readers)
        return self.ps[:, u % NBANK, :]

    def take(self, who):
        u = self.at.get(who, 0)
        while who not in self.uses[u]:
            u += 1
        self.at[who] = u + 1
        return self.ps[:, u % NBANK, :]

    def free(self, who):
        self.frees[who] = self.frees.get(who, 0) + 1
        return 1


def weight_chunks(a):
    out = []

    def cols(w, k0, c0):
        out.append([(w[k0:k0 + 4 * P, c0:c0 + BRANCH].rearrange("(k p) n -> p k n", p=P), 0, 4, BRANCH, 0)])

    def panel(w, c0, rows=D):
        for k0 in range(0, rows, 4 * P):
            cols(w, k0, c0)

    def ffn(i):
        up, down = a["ffn_w_up"][i], a["ffn_w_down"][i]
        for j in range(FT // 2):
            for k0 in (0, 4 * P):
                out.append([(up[k0:k0 + 4 * P, half * D_FF + j * S:half * D_FF + (j + 1) * S]
                             .rearrange("(k p) n -> p k n", p=P), half * S, 4, S, 0) for half in (0, 1)])
        for j in range(FT // 2):
            out.append([(down[j * S:(j + 1) * S, :].rearrange("(k p) n -> p k n", p=P), 0, 2, D, 1)])

    ada = [(i, c0) for i in range(DEPTH) for c0 in range(0, N_MOD * D, BRANCH)]

    def ada_gap(n):
        for _ in range(n * ADA_GAP):
            i, c0 = ada.pop(0)
            panel(a["w_ada_2"][i], c0)

    ada_gap(1)
    for i in range(2):
        w = a["sb_w_qkv"][0] if i == 0 else a["dil_w_qkv"][0]
        for c in (0, 2, 4, 5, 1, 3) if i == 0 else range(w.shape[1] // BRANCH):
            panel(w, c * BRANCH)
        w = a["sb_w_o"][0] if i == 0 else a["dil_w_o"][0]
        for c0 in range(0, D, BRANCH):
            panel(w, c0, w.shape[0])
        ada_gap(2)
        ffn(i)
        ada_gap(2 - i)
    for i in range(DEPTH):
        w = a["w_in_2"][i]
        for c0 in (6, 7, 0, 1, 4, 2, 3, 5):
            panel(w, c0 * BRANCH)
        for b in MERGE_ORDER:
            for half in range(2):
                panel(w, 8 * BRANCH + b * D + half * BRANCH)
                panel(a["w_branch_2"][i][b], half * BRANCH, BRANCH)
        for half in range(2):
            panel(a["w_out_2"][i], half * BRANCH)
        for e in range(N_EXPERTS + 1):
            for w, of in (("w_e1_2", e), ("w_e3_2", e), ("w_e2_2", e - 1)):
                for half in range(2):
                    if 0 <= of < N_EXPERTS:
                        panel(a[w][i][of], half * BRANCH)
    return out


def build(nc, a, out, dump=None, stop=None):
    from contextlib import ExitStack
    ctx = ExitStack()
    with ctx:
        def sb(name, words):
            return ctx.enter_context(nc.sbuf_tensor(name, [P, words], F32))

        ring = sb("ring", NSLOT * SLOT)
        Xb = sb("residual", KT * 2 * S)
        Hb = sb("normed", KT * 2 * S)
        Cb = sb("constants", C_N)
        colsb = sb("param_cols", 5 * P)
        small = sb("small", 1640)
        ARENA = 25600
        arena = sb("arena", ARENA)
        ps = ctx.enter_context(nc.psum_tensor("ps", [P, NBANK, 512], F32))

        X = Xb[:, :].rearrange("p (k t) -> p k t", k=KT)
        H = Hb[:, :].rearrange("p (k t) -> p k t", k=KT)

        def cst(name):
            return Cb[:, slice(*C_AT[name])]

        ident, mean, mean_head, ones, suffix, rot = (cst(n) for n in ("ident", "mean", "mean_head", "ones", "suffix", "rot"))

        def view(off, *dims):
            n = int(np.prod(dims))
            assert off + n <= ARENA
            v = arena[:, off:off + n]
            if len(dims) == 2:
                v = v.rearrange("p (a b) -> p a b", b=dims[1])
            if len(dims) == 3:
                v = v.rearrange("p (a b c) -> p a b c", b=dims[1], c=dims[2])
            if len(dims) == 4:
                v = v.rearrange("p (a b c d) -> p a b c d", b=dims[1], c=dims[2], d=dims[3])
            return v

        def tiny(off, n):
            return small[:, off:off + n]

        gains = colsb[:, 0:64]
        col_c = colsb[:, 64:80]
        g_final = colsb[:, 80:88]
        g_norm = (colsb[:, 88:104], colsb[:, 104:120])
        subln = colsb[:, 120:122]
        conv_w = colsb[:, P:P + DEPTH * CONV_W * 2 * FT]
        conv_b = colsb[:, 3 * P + 8:3 * P + 8 + DEPTH * 2 * FT]
        b_ada = colsb[:, 4 * P:4 * P + DEPTH * N_MOD * KT]

        rstd = small[:, 0:512]
        mods = [small[:, o:o + 96].rearrange("p (t s) -> p t s", s=2) for o in (512, 1280)]
        silu_pad = small[:, 1024:1280].rearrange("p (k s) -> p k s", s=32)
        ampl = small[:, 608:624].rearrange("p (k s) -> p k s", s=2)
        silu_c = small[:, 624:640].rearrange("p (k s) -> p k s", s=2)
        nmax, ssum, rsum = (small[:, 640 + 8 * i:648 + 8 * i].rearrange("p (b c) -> p b c", b=2) for i in range(3))
        neg_lam = small[:, 664:665]
        lam2 = small[:, 665:667]
        g_head = small[:, 667:668]
        eps = small[:, 668:669]
        sc16 = small[:, 670:686].rearrange("p (k s) -> p k s", s=2)
        stat = small[:, 686:698].rearrange("p (a b) -> p a b", b=4)
        rden = small[:, 698:702]
        top8 = small[:, 704:712]
        aff = small[:, 712:776].rearrange("p (j q e) -> p j q e", j=ST, q=2)
        pos = small[:, 776:840].rearrange("p (j r) -> p j r", j=ST)
        den4 = small[:, 840:844]
        mx4 = small[:, 844:848]

        bias_scratch = nc.dram_tensor("dil_bias_scratch", [3 * DIL_HEADS, 384], F32, kind="Internal").ap()
        rpb_scratch = nc.dram_tensor("na_bias_scratch", [NA_HEADS, 15, P], F32, kind="Internal").ap()

        bias_shear = nc.dram_tensor("dil_bias_shear", [3 * DIL_HEADS, P * 386], F32, kind="Internal").ap()
        rpb_shear = nc.dram_tensor("na_bias_shear", [NA_HEADS, NA_DR + 1, GRID_W * 130], F32, kind="Internal").ap()

        def sem(name):
            return ctx.enter_context(nc.semaphore(name))

        def sig(name):
            return Signal(sem(name))

        banks = Banks(ps, sem("psum_filled"), {"v": sem("psum_freed_by_vector"), "a": sem("psum_freed_by_scalar")})
        slot_loaded = [sem(f"slot_loaded{i}") for i in range(NSLOT)]
        chunk_used = sem("chunk_used")
        loads = {n: sem(f"load_{n}") for n in ("consts", "rows", "x", "ctx", "bucket", "router", "out", "relb", "gm",
                                               "lam", "bias_out", "bias_shear", "bias_in", "rpb_out", "rpb_shear", "rpb_in")}
        load_count = {n: 0 for n in loads}
        consts_ready, cols_ready, x_ready, zero_ready = sig("consts_ready"), sig("cols_ready"), sig("x_ready"), sig("zero_ready")
        sq_ready, rstd_ready, h_ready = sig("squares_ready"), sig("rstd_ready"), sig("normed_ready")
        src_ready = sig("norm_source_ready")
        xn_ready = sig("x_times_rstd_ready")
        v_step, a_step = sig("vector_step"), sig("scalar_step")
        qkv_ready = sig("qkv_ready")
        z_copied, z_abs, l_ready, L_ready, t_ready, sb_p_ready, o_ready = (
            sig(n) for n in ("z_copied", "neg_abs_ready", "log1p_ready", "lognot_ready", "stick_arg_ready",
                             "stick_probs_ready", "attn_out_ready"))
        gate_ready, gate_exp, hidden_ready = sig("gate_ready"), sig("gate_exp_ready"), sig("hidden_ready")
        max_ready, exp_ready, p_ready, pt_ready = (sig(n) for n in ("row_max_ready", "exp_ready", "probs_ready", "probsT_ready"))
        bias_rows, bias_tile = sig("bias_rows_ready"), sig("bias_tile_ready")
        sc_ready = sig("silu_c_ready")
        dma_free = sig("arena_free_for_loads")
        rope_ready = sig("rope_ready")
        ln_ready, ln_rstd = sig("ln_var_ready"), sig("ln_rstd_ready")
        y_ready = sig("branch_out_ready")
        merged_ready = sig("merged_ready")
        tok_ready, aff_ready, pos_ready, P_ready, G_ready = (
            sig(n) for n in ("token_major_ready", "affinity_ready", "slot_pos_ready", "select_ready", "gated_select_ready"))
        xin_ready, pgt_ready, ye_ready = sig("expert_in_ready"), sig("scatter_ready"), sig("expert_out_ready")
        affT_ready = sig("affinityT_ready")
        lam_ready, lam_exp = sig("lambda_dot_ready"), sig("lambda_exp_ready")
        wst_ready, final_ready, mod_ready = sig("spatialT_ready"), sig("final_ready"), sig("mod_ready")
        gate_used = sig("gate_used")
        router_part = sig("router_part_copied")

        chunks = weight_chunks(a)
        freed_at = []
        state = {"chunk": 0}

        X_STAGE, C_STAGE, ROW_STAGE, RELB, BUCKET, DROW = 0, 2048, 4096, 4800, 4832, 8192
        SQT, SKT, SV, SOT = view(0, 8, S), view(2048, 8, S), view(4096, ST, D), view(6144, 8, S)
        SM = view(22000, 8, S)
        SBUFS = [view(8192 + 768 * i, 2, 384) for i in range(16)]
        DQT, DKT, DV = view(0, 12, S), view(3072, 12, S), view(6144, ST, 1536)
        DB = view(9216, 24, S)
        DOT = view(15360, 4, S)
        DS = [view(o, 3, S) for o in (16384, 17152, 19456)]
        DPT = [view(17920 + 768 * i, 6, P) for i in range(2)]
        HID = view(0, FT, S)
        GU = [view(5632 + 1024 * i, 4, S) for i in range(2)]
        GE = [view(7680 + 512 * i, 2, S) for i in range(2)]
        ADA = [view(20976 + 512 * i, 512) for i in range(2)]
        KT2, QT2, V2 = view(0, 4, 512), view(2048, 4, 512), view(4096, 4, 512)
        Y2 = [view(6144 + 2048 * i, 4, 512) for i in range(3)]
        BN = view(12288, NA_HEADS, NA_DR, GRID_W)
        S2 = [view(o, 2, 512) for o in (15360, 16384, 14336)]
        NAS = [view(15360 + 512 * i, 512) for i in range(4)]
        PT2 = [view(17408 + 512 * i, 4, P) for i in range(2)]
        WST = view(18432, 4, P)
        GMR = view(18944, 3, 512)
        LAMV = view(20480, 4, DH)
        WS_RAW = view(20736, 4, P)
        ROPE_T = view(21248, S)
        O2 = view(4096, 4, 512)
        UT, VG, TG = view(8192, 4, 512), view(21504, 4, 512), view(23552, 4, 512)
        KT3, QT3, V3 = UT, VG, TG
        YCU = Y2[2]
        MB = view(0, 8, 512)
        GS = [view(o, 4, 512) for o in (12288, 18432)]
        HT = view(0, 4, D)
        SEL = view(4096, ST, 2 * N_EXPERTS, CAP)
        GSEL = view(6144, ST, 2 * N_EXPERTS, CAP)
        XIN = view(8192, KT, N_EXPERTS, 2 * CAP)
        PGT = view(16384, 2, 4, S)
        HE = [view(18432 + 512 * i, 8, 2 * CAP) for i in range(2)]
        HG = [view(19456 + 512 * i, 8, 2 * CAP) for i in range(2)]
        HR = [view(21504 + 1024 * i, D) for i in range(2)]
        AT = view(20480, 2, S)[0:2 * N_EXPERTS]
        AW = view(20992, S)[0:2 * N_EXPERTS]
        WR = small[:, 1380:1636].rearrange("p (k e) -> p k e", e=32)
        RPART = view(21504, 512)
        YE = (Hb[:, :].rearrange("p (k d) -> p k d", k=4), arena[:, 0:4096].rearrange("p (k d) -> p k d", k=4))
        OUTT = view(0, ST, D)

        src_written = []

        block = ctx.enter_context(nc.Block())

        @block.tensor
        def _(pe):
            mm = nc.tensor.matmul

            def chunk(n):
                return (ring[:, (n % NSLOT) * SLOT:(n % NSLOT + 1) * SLOT], slot_loaded[n % NSLOT],
                        16 * sum(len(chunks[m]) for m in range(n % NSLOT, n + 1, NSLOT)))

            def next_chunks(k):
                state["chunk"] += k
                return [chunk(n) for n in range(state["chunk"] - k, state["chunk"])]

            used = [0]

            def chunks_done(k, banked=False):
                for _ in range(k):
                    freed_at.append(len(banks.uses))

            def tiles_T(src, n, kts=KT, readers=("v",), fresh=False):
                slots = []

                def tile(f):
                    if f == 0:
                        for slot, loaded, count in next_chunks(kts // 4):
                            pe.wait_ge(loaded, count)
                            slots.append(slot.rearrange("p (k n) -> p k n", k=4))
                    o = banks.open(*readers)
                    if banks.due:
                        pe.wait_ge(*banks.due)
                    for k in range(kts):
                        if fresh and f == 0 and k % GRP == 0:
                            pe.wait_ge(h_ready.sem, h_ready.nth("pe"))
                        ins = mm(o[:, 0:n], slots[k // 4][:, k % 4, f * P:(f + 1) * P], src[:, k, 0:n],
                                 start=k == 0, stop=k == kts - 1)
                    ins.then_inc(banks.filled, 1)
                    if f == 3:
                        chunks_done(kts // 4)

                return [lambda f=f: tile(f) for f in range(4)]

            def tiles_N(src, tiles):
                slots = []

                def tile(t):
                    if t == 0:
                        for slot, loaded, count in next_chunks(2):
                            pe.wait_ge(loaded, count)
                            slots.append(slot.rearrange("p (k n) -> p k n", k=4))
                    o = banks.open("v")
                    if banks.due:
                        pe.wait_ge(*banks.due)
                    for k in range(KT):
                        ins = mm(o, src[:, k, t * P:(t + 1) * P], slots[k // 4][:, k % 4, :],
                                 start=k == 0, stop=k == KT - 1)
                    ins.then_inc(banks.filled, 1)
                    if t == tiles - 1:
                        chunks_done(2)

                return [lambda t=t: tile(t) for t in range(tiles)]

            def gemm_T(panels, src, n, kts=KT, readers=("v",), fresh=False):
                for c in range(panels):
                    for step in tiles_T(src, n, kts, readers, fresh and c == 0):
                        step()

            def gemm_N(panels, src, tiles):
                for _ in range(panels):
                    for step in tiles_N(src, tiles):
                        step()

            def mean_square(src, n, tiles, m):
                o = banks.open("a")
                if banks.due:
                    pe.wait_ge(*banks.due)
                for k in range(tiles):
                    if k % GRP == 0:
                        pe.wait_ge(sq_ready.sem, sq_ready.nth("pe"))
                    ins = mm(o[:, 0:n], m, src[:, k, 0:n], start=k == 0, stop=k == tiles - 1)
                ins.then_inc(banks.filled, 1)

            pe.wait_ge(loads["consts"], 16)
            pe.wait_ge(loads["rows"], 16 * len(ROWS))
            for b, r in enumerate(ROW_BLOCKS):
                o = banks.open("v")
                if banks.due:
                    pe.wait_ge(*banks.due)
                nc.tensor.transpose(o[:, 0:r], view(ROW_STAGE, 5, P)[0:r, b, :], ident[0:r, 0:r]).then_inc(banks.filled, 1)
            pe.wait_ge(loads["x"], 16)
            pe.wait_ge(loads["ctx"], 16)
            for k in range(KT):
                o = banks.open("v")
                if banks.due:
                    pe.wait_ge(*banks.due)
                for t in range(4):
                    src = view((X_STAGE, C_STAGE)[t // 2], ST, D)
                    ins = nc.tensor.transpose(o[:, t * P:(t + 1) * P], src[:, t % 2, k * P:(k + 1) * P], ident)
                ins.then_inc(banks.filled, 1)
            pe.wait_ge(loads["relb"], 16)
            pe.wait_ge(loads["bucket"], 16)
            pe.wait_ge(zero_ready.sem, zero_ready.nth("pe"))
            for g in range(3):
                o = banks.open("v")
                if banks.due:
                    pe.wait_ge(*banks.due)
                mm(o[0:DIL_HEADS, 0:384], arena[0:33, RELB + g * DIL_HEADS:RELB + (g + 1) * DIL_HEADS],
                               arena[0:33, BUCKET + g * 384:BUCKET + (g + 1) * 384], start=True, stop=True).then_inc(banks.filled, 1)

            ada = {"part": 0, "fold": 0, "read": {}}

            def ada_part():
                slots = []
                for slot, loaded, count in next_chunks(2):
                    pe.wait_ge(loaded, count)
                    slots.append(slot.rearrange("p (k n) -> p k n", k=4))
                o = banks.open("a")
                pe.wait_ge(*banks.due)
                for k in range(KT):
                    ins = mm(o[32 * (k % 4):32 * (k % 4) + 32, :], silu_pad[:, k, :], slots[k // 4][:, k % 4, :],
                             start=k < 4, stop=k >= 4)
                ins.then_inc(banks.filled, 1)
                chunks_done(2)
                ada["read"][ada["part"]] = sum(r[-1] == "a" for r in banks.uses)
                ada["part"] += 1

            def ada_fold():
                n = ada["fold"]
                ada["fold"] += 1
                pe.wait_ge(banks.freed["a"], ada["read"][n])
                o = banks.open("v")
                pe.wait_ge(*banks.due)
                for f in range(4):
                    ins = mm(o[:, f * P:(f + 1) * P], ADA[n % 2][:, f * P:(f + 1) * P], cst("fold32"), start=True, stop=True)
                ins.then_inc(banks.filled, 1)

            def ada_gap():
                for n in range(ADA_GAP):
                    ada_part()
                    if n:
                        ada_fold()
                ada_fold()

            def ffn():
                mean_square(H, S, KT, mean)
                ada_gap()
                gemm_T(FT // 2, H, S, fresh=True)
                outs = []
                for _ in range(8):
                    outs.append(banks.open("v"))
                    pe.wait_ge(*banks.due)
                for j in range(FT // 2):
                    pe.wait_ge(hidden_ready.sem, hidden_ready.nth("pe"))
                    (slot, loaded, count), = next_chunks(1)
                    pe.wait_ge(loaded, count)
                    slot = slot.rearrange("p (k n) -> p k n", k=2)
                    for f in range(8):
                        for k in range(2):
                            ins = mm(outs[f][:, 0:S], slot[:, k, f * P:(f + 1) * P], HID[:, 2 * j + k, :],
                                     start=j == 0 and k == 0, stop=j == FT // 2 - 1 and k == 1)
                        if j == FT // 2 - 1:
                            ins.then_inc(banks.filled, 1)
                    if j < FT // 2 - 1:
                        ins.then_inc(chunk_used, 1)
                        used[0] += 1
                        freed_at.append(-used[0])
                    else:
                        chunks_done(1)
                mean_square(H, S, KT, mean)
                ada_gap()

            pe.wait_ge(sc_ready.sem, sc_ready.nth("pe"))
            mean_square(H, S, KT, mean)
            ada_gap()
            gemm_T(2, H, S, fresh=True)
            gemm_N(2, H, ST)
            pe.wait_ge(qkv_ready.sem, qkv_ready.nth("pe"))

            def staged(n, *stages, fill=(), over=None):
                steps = n + 2 * LAG
                over = over or steps
                for step in range(steps):
                    for lag, stage in stages:
                        if 0 <= step - lag < n:
                            stage(step - lag)
                    for work in fill[len(fill) * step // over:len(fill) * (step + 1) // over]:
                        work()

            def sb_scores(b):
                if b == SB_HALF:
                    pe.wait_ge(qkv_ready.sem, qkv_ready.nth("pe"))
                for h in (2 * b, 2 * b + 1):
                    r, t = DH * (h % 2), h // 2
                    o = banks.open("a")
                    if banks.due:
                        pe.wait_ge(*banks.due)
                    mm(o[:, 0:S], SKT[r:r + DH, t, 0:P], SQT[r:r + DH, t, :], start=True, stop=True)
                    mm(o[:, S:384], SKT[r:r + DH, t, P:S], SQT[r:r + DH, t, P:S], start=True, stop=True).then_inc(banks.filled, 1)

            def sb_sums(b):
                L = SBUFS[4 * (b % 4) + 2]
                pe.wait_ge(L_ready.sem, L_ready.nth("pe"))
                for j in range(2):
                    o = banks.open("v")
                    if banks.due:
                        pe.wait_ge(*banks.due)
                    mm(o[:, 0:384], suffix, L[:, j, :], start=True, stop=False)
                    mm(o[:, P:S], ones, L[:, j, S:384], start=False, stop=True).then_inc(banks.filled, 1)

            def sb_out(b):
                Pr = SBUFS[4 * (b % 4) + 3]
                pe.wait_ge(sb_p_ready.sem, sb_p_ready.nth("pe"))
                o = banks.open("v")
                if banks.due:
                    pe.wait_ge(*banks.due)
                for i in range(2):
                    h = 2 * b + i
                    v0 = SV[:, 0, h * DH:(h + 1) * DH]
                    v1 = SV[:, 1, h * DH:(h + 1) * DH]
                    dst = o[DH * i:DH * (i + 1)]
                    mm(dst[:, 0:S], v0, Pr[:, i, 0:S], start=True, stop=False)
                    ins = mm(dst[:, P:S], v1, Pr[:, i, S:384], start=False, stop=True)
                ins.then_inc(banks.filled, 1)

            staged(2 * SB_HALF, (0, sb_scores), (2, sb_sums), (3, sb_out), fill=tiles_T(H, S) + tiles_T(H, S), over=SB_HALF)
            pe.wait_ge(o_ready.sem, o_ready.nth("pe"))
            gemm_T(2, SOT, S)
            mean_square(H, S, KT, mean)
            ada_gap()
            ffn()

            mean_square(H, S, KT, mean)
            ada_gap()
            gemm_T(6, H, S, fresh=True)
            gemm_N(3, H, ST)
            pe.wait_ge(qkv_ready.sem, qkv_ready.nth("pe"))
            items = [(h, t) for h in range(DIL_HEADS) for t in range(ST)]

            def dil_scores(i):
                h, t = items[i]
                r = DH * (h % 2)
                for g in range(3):
                    o = banks.open("v")
                    if banks.due:
                        pe.wait_ge(*banks.due)
                    c = g * 4 + h // 2
                    mm(o[:, 0:(t + 1) * P], DQT[r:r + DH, c, t * P:(t + 1) * P],
                                   DKT[r:r + DH, c, 0:(t + 1) * P], start=True, stop=True).then_inc(banks.filled, 1)

            def dil_turn(i):
                h, t = items[i]
                pe.wait_ge(p_ready.sem, p_ready.nth("pe"))
                tiles = [(g, k) for g in range(3) for k in range(t + 1)]
                for n0 in range(0, len(tiles), 4):
                    o = banks.open("a")
                    if banks.due:
                        pe.wait_ge(*banks.due)
                    for n, (g, k) in enumerate(tiles[n0:n0 + 4]):
                        ins = nc.tensor.transpose(o[:, n * P:(n + 1) * P], DS[i % 3][:, g, k * P:(k + 1) * P], ident)
                    ins.then_inc(banks.filled, 1)

            def dil_pv(i):
                h, t = items[i]
                tiles = [(g, k) for g in range(3) for k in range(t + 1)]
                pe.wait_ge(pt_ready.sem, pt_ready.nth("pe"))
                o = banks.open("v")
                if banks.due:
                    pe.wait_ge(*banks.due)
                r = DH * (h % 2)
                for n, (g, k) in enumerate(tiles):
                    ins = mm(o[r:r + DH, 0:P], DV[:, k, g * BRANCH + h * DH:g * BRANCH + (h + 1) * DH],
                             DPT[i % 2][:, n, :], start=n == 0, stop=n == len(tiles) - 1)
                ins.then_inc(banks.filled, 1)

            staged(len(items), (0, dil_scores), (2 * LAG, dil_pv), (LAG, dil_turn))
            pe.wait_ge(o_ready.sem, o_ready.nth("pe"))
            gemm_T(2, DOT, S, 4)
            mean_square(H, S, KT, mean)
            ada_gap()
            ffn()

            for i in range(DEPTH):
                last = i == DEPTH - 1
                qtok, qtiles = (S, ST) if last else (2 * S, 2 * ST)
                mean_square(H, 2 * S, KT, mean)
                gemm_T(1, H, qtok, fresh=True)
                gemm_N(1, H, qtiles)
                pe.wait_ge(loads["gm"], 64 * (i + 1))
                o = banks.open("v")
                if banks.due:
                    pe.wait_ge(*banks.due)
                for g in range(4):
                    ins = nc.tensor.transpose(o[:, g * P:(g + 1) * P], WS_RAW[:, g, :], ident)
                ins.then_inc(banks.filled, 1)
                gemm_T(1, H, 2 * S)
                gemm_N(1, H, 4)
                gemm_T(1, H, qtok)
                pe.wait_ge(ln_ready.sem, ln_ready.nth("pe"))
                for g in range(4):
                    o = banks.open("v")
                    if banks.due:
                        pe.wait_ge(*banks.due)
                    for t in range(qtiles):
                        ins = mm(o[:, t * P:(t + 1) * P], VG[:, t, g * P:(g + 1) * P], WST[:, g, :], start=True, stop=True)
                    ins.then_inc(banks.filled, 1)
                pe.wait_ge(qkv_ready.sem, qkv_ready.nth("pe"))
                items = [(h, t) for h in range(NA_HEADS) for t in range(qtiles)]

                def keys(t):
                    return (0, 4) if t < ST else (ST, 4)

                def na_scores(n):
                    h, t = items[n]
                    r, (k0, k1) = DH * (h % 2), keys(t)
                    o = banks.open("v")
                    if banks.due:
                        pe.wait_ge(*banks.due)
                    mm(o[:, k0 * P:k1 * P], QT2[r:r + DH, h // 2, t * P:(t + 1) * P],
                                   KT2[r:r + DH, h // 2, k0 * P:k1 * P], start=True, stop=True).then_inc(banks.filled, 1)

                def na_turn(n):
                    h, t = items[n]
                    r, (k0, k1) = DH * (h % 2), keys(t)
                    pe.wait_ge(p_ready.sem, p_ready.nth("pe"))
                    o = banks.open("a")
                    if banks.due:
                        pe.wait_ge(*banks.due)
                    for k in range(k0, k1):
                        ins = nc.tensor.transpose(o[:, k * P:(k + 1) * P], NAS[n % 4][:, k * P:(k + 1) * P], ident)
                    ins.then_inc(banks.filled, 1)

                def na_pv(n):
                    h, t = items[n]
                    r, (k0, k1) = DH * (h % 2), keys(t)
                    pe.wait_ge(pt_ready.sem, pt_ready.nth("pe"))
                    o = banks.open("v")
                    if banks.due:
                        pe.wait_ge(*banks.due)
                    for k in range(k0, k1):
                        ins = mm(o[r:r + DH, 0:P], V2[:, k, h * DH:(h + 1) * DH], PT2[n % 2][:, k, :],
                                 start=k == k0, stop=k == k1 - 1)
                    ins.then_inc(banks.filled, 1)

                staged(len(items), (0, na_scores), (2 * LAG, na_pv), (LAG, na_turn),
                       fill=tiles_T(H, 2 * S) + tiles_N(H, 4) + tiles_T(H, qtok))
                pe.wait_ge(y_ready.sem, y_ready.nth("pe"))
                pe.wait_ge(qkv_ready.sem, qkv_ready.nth("pe"))
                for T in (KT3, QT3):
                    for c in range(4):
                        o = banks.open("v")
                        if banks.due:
                            pe.wait_ge(*banks.due)
                        mm(o[:, 0:S], rot, T[:, c, 0:S], start=True, stop=True).then_inc(banks.filled, 1)
                merge_tiles = []
                for b in MERGE_ORDER[0:2]:
                    for _ in range(2):
                        merge_tiles += tiles_T(H, qtok, readers=("a",)) + tiles_T(Y2[b], qtok, 4)
                for step in merge_tiles[0:4]:
                    step()
                pe.wait_ge(rope_ready.sem, rope_ready.nth("pe"))
                items = [(h, t) for h in range(DA_HEADS) for t in range(qtiles)]

                def da_scores(n):
                    h, t = items[n]
                    k0, k1 = keys(t)
                    for c in range(2):
                        o = banks.open("v", "a")
                        if banks.due:
                            pe.wait_ge(*banks.due)
                        r = DH * c
                        mm(o[:, k0 * P:k1 * P], QT3[r:r + DH, h, t * P:(t + 1) * P],
                                       KT3[r:r + DH, h, k0 * P:k1 * P], start=True, stop=True).then_inc(banks.filled, 1)

                def da_turn(n):
                    h, t = items[n]
                    k0, k1 = keys(t)
                    pe.wait_ge(p_ready.sem, p_ready.nth("pe"))
                    o = banks.open("a")
                    if banks.due:
                        pe.wait_ge(*banks.due)
                    for k in range(k0, k1):
                        ins = nc.tensor.transpose(o[:, k * P:(k + 1) * P], S2[n % 3][:, 0, k * P:(k + 1) * P], ident)
                    ins.then_inc(banks.filled, 1)

                def da_pv(n):
                    h, t = items[n]
                    r, (k0, k1) = DH * (h % 2), keys(t)
                    pe.wait_ge(pt_ready.sem, pt_ready.nth("pe"))
                    o = banks.open("v")
                    if banks.due:
                        pe.wait_ge(*banks.due)
                    for k in range(k0, k1):
                        ins = mm(o[:, 0:P], V3[:, k, h * P:(h + 1) * P], PT2[n % 2][:, k, :], start=k == k0, stop=k == k1 - 1)
                    ins.then_inc(banks.filled, 1)

                staged(len(items), (0, da_scores), (2 * LAG, da_pv), (LAG, da_turn), fill=merge_tiles[4:])
                pe.wait_ge(sq_ready.sem, sq_ready.nth("pe"))
                for h in range(DA_HEADS):
                    o = banks.open("a")
                    if banks.due:
                        pe.wait_ge(*banks.due)
                    mm(o[:, 0:qtok], mean_head, Y2[1][:, h, 0:qtok], start=True, stop=True).then_inc(banks.filled, 1)
                gemm_T(1, H, qtok, readers=("a",))
                pe.wait_ge(y_ready.sem, y_ready.nth("pe"))
                gemm_T(1, Y2[MERGE_ORDER[2]], qtok, 4)
                gemm_T(1, H, qtok, readers=("a",))
                gemm_T(1, Y2[MERGE_ORDER[2]], qtok, 4)
                pe.wait_ge(merged_ready.sem, merged_ready.nth("pe"))
                gemm_T(2, MB, qtok)
                mean_square(H, qtok, KT, mean)

                pe.wait_ge(loads["router"], 16 * (i + 1))
                o = banks.open("a")
                if banks.due:
                    pe.wait_ge(*banks.due)
                for k in range(KT):
                    if k % GRP == 0:
                        pe.wait_ge(h_ready.sem, h_ready.nth("pe"))
                    ins = mm(o[32 * (k % 4):32 * (k % 4) + 32, 0:qtok], WR[:, k, :], H[:, k, 0:qtok], start=k < 4, stop=k >= 4)
                ins.then_inc(banks.filled, 1)
                for t in range(qtiles):
                    for half in range(2):
                        o = banks.open("a")
                        if banks.due:
                            pe.wait_ge(*banks.due)
                        for f in range(4):
                            ins = nc.tensor.transpose(o[:, f * P:(f + 1) * P], H[:, 4 * half + f, t * P:(t + 1) * P], ident)
                        ins.then_inc(banks.filled, 1)
                    if t == 0:
                        pe.wait_ge(router_part.sem, router_part.nth("pe"))
                        o = banks.open("v", "a")
                        if banks.due:
                            pe.wait_ge(*banks.due)
                        for u in range(qtiles):
                            ins = mm(o[:, u * N_EXPERTS:(u + 1) * N_EXPERTS], RPART[:, u * P:(u + 1) * P],
                                     cst("fold32")[:, 0:N_EXPERTS], start=True, stop=True)
                        ins.then_inc(banks.filled, 1)
                rows = qtiles // 2 * N_EXPERTS
                pe.wait_ge(aff_ready.sem, aff_ready.nth("pe"))
                o = banks.open("v")
                if banks.due:
                    pe.wait_ge(*banks.due)
                for j in range(ST):
                    ins = nc.tensor.transpose(o[0:rows, j * P:(j + 1) * P],
                                              aff[:, j, 0:qtiles // 2, :].rearrange("p q e -> p (q e)"), ident)
                ins.then_inc(banks.filled, 1)
                pe.wait_ge(pos_ready.sem, pos_ready.nth("pe"))
                o = banks.open("v")
                if banks.due:
                    pe.wait_ge(*banks.due)
                for j in range(ST):
                    ins = nc.tensor.transpose(o[:, j * 32:j * 32 + rows], AW[0:rows, j * P:(j + 1) * P], ident[0:rows, 0:rows])
                ins.then_inc(banks.filled, 1)
                pe.wait_ge(P_ready.sem, P_ready.nth("pe"))
                pe.wait_ge(tok_ready.sem, tok_ready.nth("pe"))
                for k in range(KT):
                    for q in range(qtiles // 2):
                        o = banks.open("v")
                        if banks.due:
                            pe.wait_ge(*banks.due)
                        for j in range(ST):
                            ins = mm(o, HT[:, ST * q + j, k * P:(k + 1) * P],
                                     SEL[:, j, q * N_EXPERTS:(q + 1) * N_EXPERTS, :].rearrange("p e s -> p (e s)"),
                                     start=j == 0, stop=j == ST - 1)
                        ins.then_inc(banks.filled, 1)
                pe.wait_ge(G_ready.sem, G_ready.nth("pe"))
                for q in range(qtiles // 2):
                    for half in range(2):
                        o = banks.open("a")
                        if banks.due:
                            pe.wait_ge(*banks.due)
                        for n, (pk, j) in enumerate((pk, j) for pk in (2 * half, 2 * half + 1) for j in range(ST)):
                            e0 = q * N_EXPERTS + 4 * pk
                            ins = nc.tensor.transpose(o[:, n * P:(n + 1) * P],
                                                      GSEL[:, j, e0:e0 + 4, :].rearrange("p e s -> p (e s)"), ident)
                        ins.then_inc(banks.filled, 1)
                pe.wait_ge(xin_ready.sem, xin_ready.nth("pe"))
                w = qtiles // 2 * CAP
                groups = P // w

                def expert_up(e):
                    for which in range(2):
                        for half in range(2):
                            slots = []
                            for slot, loaded, count in next_chunks(2):
                                pe.wait_ge(loaded, count)
                                slots.append(slot.rearrange("p (k n) -> p k n", k=4))
                            o = banks.open("av"[which])
                            pe.wait_ge(*banks.due)
                            for k in range(KT):
                                r = w * (k % groups)
                                ins = mm(o[r:r + w, :], XIN[:, k, e, 0:w], slots[k // 4][:, k % 4, :],
                                         start=k < groups, stop=k >= KT - groups)
                            ins.then_inc(banks.filled, 1)
                            chunks_done(2)
                    rows_read[e] = [sum(r[-1] == who for r in banks.uses) for who in "av"]

                def expert_fold(e):
                    for which in range(2):
                        pe.wait_ge(banks.freed["av"[which]], rows_read[e][which])
                        for half in range(2):
                            o = banks.open(*(("a", "v") if which == 0 else ("v",)))
                            pe.wait_ge(*banks.due)
                            for f in range(4):
                                ins = mm(o[:, f * P:(f + 1) * P], HR[which][:, (4 * half + f) * P:(4 * half + f + 1) * P],
                                         cst(f"fold{w}"), start=True, stop=True)
                            ins.then_inc(banks.filled, 1)

                def expert_down(e):
                    pe.wait_ge(hidden_ready.sem, hidden_ready.nth("pe"))
                    for half in range(2):
                        slots = []
                        for slot, loaded, count in next_chunks(2):
                            pe.wait_ge(loaded, count)
                            slots.append(slot.rearrange("p (k n) -> p k n", k=4))
                        o = banks.open("a")
                        pe.wait_ge(*banks.due)
                        for k in range(KT):
                            ins = mm(o[0:w, :], HE[e % 2][:, k, 0:w], slots[k // 4][:, k % 4, :], start=k == 0, stop=k == KT - 1)
                        ins.then_inc(banks.filled, 1)
                        chunks_done(2)

                rows_read = {}
                for e in range(N_EXPERTS + 1):
                    if e < N_EXPERTS:
                        expert_up(e)
                    if e:
                        expert_down(e - 1)
                    if e < N_EXPERTS:
                        expert_fold(e)
                pe.wait_ge(ye_ready.sem, ye_ready.nth("pe"))
                for f in range(KT):
                    o = banks.open("v")
                    if banks.due:
                        pe.wait_ge(*banks.due)
                    for q in range(qtiles // 2):
                        for pk in range(4):
                            ins = mm(o[:, q * S:(q + 1) * S], YE[q][:, pk, f * P:(f + 1) * P], PGT[:, q, pk, :],
                                     start=pk == 0, stop=pk == 3)
                    ins.then_inc(banks.filled, 1)

            mean_square(H, S, KT, mean)
            for _ in range(KT // GRP):
                pe.wait_ge(h_ready.sem, h_ready.nth("pe"))
            for t in range(ST):
                for half in range(2):
                    o = banks.open("a")
                    if banks.due:
                        pe.wait_ge(*banks.due)
                    for f in range(4):
                        ins = nc.tensor.transpose(o[:, f * P:(f + 1) * P], H[:, 4 * half + f, t * P:(t + 1) * P], ident)
                    ins.then_inc(banks.filled, 1)
            assert state["chunk"] == len(chunks) == len(freed_at)

        @block.sync
        def _(sp):
            sp.dma_start(Cb[:, :], a["const_table"]).then_inc(loads["consts"], 16)
            stage = view(ROW_STAGE, 5, P)
            taken = {}
            for name, r, b, r0 in ROWS:
                src = a[name]
                src = src.rearrange(" ".join("abcd"[:len(src.shape)]) + " -> (" + " ".join("abcd"[:len(src.shape)]) + ")")
                src = src.rearrange("(r n) -> r n", n=P)
                s0 = taken.get(name, 0)
                taken[name] = s0 + r
                sp.dma_start(stage[r0:r0 + r, b, :], src[s0:s0 + r, :]).then_inc(loads["rows"], 16)
            sp.dma_start(view(X_STAGE, ST, D), a["x"][0].rearrange("(t p) d -> p t d", p=P)).then_inc(loads["x"], 16)
            sp.dma_start(view(C_STAGE, ST, D), a["ctx_2"][0].rearrange("(t p) d -> p t d", p=P)).then_inc(loads["ctx"], 16)
            sp.dma_start(arena[0:N_BUCKETS, RELB:RELB + 24], a["rel_bias"]).then_inc(loads["relb"], 16)
            sp.dma_start(arena[0:33, BUCKET:BUCKET + 1152], a["bucket_table"]).then_inc(loads["bucket"], 16)
            for n, pieces in enumerate(chunks):
                if n >= NSLOT:
                    at = freed_at[n - NSLOT]
                    if at > 0:
                        sp.wait_ge(banks.filled, at)
                    else:
                        sp.wait_ge(chunk_used, -at)
                slot = ring[:, (n % NSLOT) * SLOT:(n % NSLOT + 1) * SLOT]
                for src, c0, k, w, _ in pieces:
                    dst = slot.rearrange("p (k n) -> p k n", k=k)[:, :, c0:c0 + w]
                    sp.dma_start(dst, src).then_inc(slot_loaded[n % NSLOT], 16)
            sp.wait_ge(final_ready.sem, final_ready.nth("sp"))
            sp.dma_start(out[0].rearrange("(t p) d -> p t d", p=P), OUTT).then_inc(loads["out"], 16)
            sp.wait_ge(loads["out"], 16)

        @block.vector
        def _(v):
            ve = nc.vector


            stamps = [0]


            def tile_written(k):
                if k % GRP == GRP - 1:
                    src_written.append((banks.freed["v"], banks.frees["v"]))

            def stamp():
                stamps[0] += 1
                at = 976 + stamps[0] % 24
                return ve.tensor_copy(small[:, at:at + 1], eps)




            ve.memset(eps, EPS).then_inc(v_step.sem, v_step.up())
            v.wait_ge(v_step.sem, v_step.made)
            ve.memset(arena[32:33, RELB:RELB + 24], 1.0).then_inc(zero_ready.sem, zero_ready.up())
            for b, r in enumerate(ROW_BLOCKS):
                o = banks.take("v")
                v.wait_ge(banks.filled, banks.at["v"])
                ve.tensor_copy(colsb[:, b * P:b * P + r], o[:, 0:r]).then_inc(banks.freed["v"], banks.free("v"))
            for k in range(KT):
                o = banks.take("v")
                v.wait_ge(banks.filled, banks.at["v"])
                ve.tensor_copy(X[:, k, :], o).then_inc(banks.freed["v"], banks.free("v"))
                tile_written(k)
            v.wait_ge(banks.freed["v"], banks.frees["v"])
            ve.tensor_copy(sc16[:, :, 0], col_c[:, 0:8]).then_inc(v_step.sem, v_step.up())
            for g in range(3):
                o = banks.take("v")
                v.wait_ge(banks.filled, banks.at["v"])
                ins = ve.tensor_copy(arena[0:DIL_HEADS, DROW + 384 * g:DROW + 384 * (g + 1)], o[0:DIL_HEADS, 0:384])
                ins.then_inc(banks.freed["v"], banks.free("v"))
            v.wait_ge(banks.freed["v"], banks.frees["v"])
            ve.tensor_copy(sc16[:, :, 1], col_c[:, 8:16]).then_inc(bias_rows.sem, bias_rows.up())

            ve.memset(silu_pad, 0.0).then_inc(v_step.sem, v_step.up())
            ve.memset(WR, 0.0).then_inc(v_step.sem, v_step.up())
            v.wait_ge(v_step.sem, v_step.made)
            stamp().then_inc(gate_ready.sem, gate_ready.up())
            v.wait_ge(gate_exp.sem, gate_exp.nth("v"))
            ve.scalar_tensor_tensor(silu_c, silu_c, 1.0, sc16, ALU.add, ALU.mult).then_inc(v_step.sem, v_step.up())
            v.wait_ge(v_step.sem, v_step.made)
            ve.tensor_scalar(silu_pad[:, :, 0:2], silu_c, 0.5, None, ALU.mult).then_inc(sc_ready.sem, sc_ready.up())

            def pre_norm(src, gain, n=S):
                v.wait_ge(rstd_ready.sem, rstd_ready.nth("v"))
                for k in range(KT):
                    ins = ve.scalar_tensor_tensor(H[:, k, 0:n], src[:, k, 0:n], gain[:, k:k + 1], rstd[:, 0:n], ALU.mult, ALU.mult)
                    if k % GRP == GRP - 1:
                        ins.then_inc(h_ready.sem, h_ready.up())

            def gain_of(i, j):
                return gains[:, (i * 4 + j) * KT:(i * 4 + j + 1) * KT]

            def post_norm_add(m, gain):
                v.wait_ge(rstd_ready.sem, rstd_ready.nth("v"))
                for k in range(KT):
                    ve.scalar_tensor_tensor(m[:, k, :], m[:, k, :], gain[:, k:k + 1], rstd[:, 0:S], ALU.mult, ALU.mult
                                            ).then_inc(v_step.sem, v_step.up())
                for k in range(0, KT, GRP):
                    v.wait_ge(v_step.sem, v_step.made - KT + k + GRP)
                    ve.tensor_tensor(X[:, k:k + GRP, 0:S], X[:, k:k + GRP, 0:S], m[:, k:k + GRP, :], ALU.add
                                     ).then_inc(src_ready.sem, src_ready.up())
                    src_written.append((src_ready.sem, src_ready.made))
                v.wait_ge(src_ready.sem, src_ready.made)

            def evac(dst, n):
                o = banks.take("v")
                v.wait_ge(banks.filled, banks.at["v"])
                ve.tensor_copy(dst, o[:, 0:n]).then_inc(banks.freed["v"], banks.free("v"))

            def mixer_out(m, gain):
                for f in range(KT):
                    evac(m[:, f, :], S)
                    tile_written(f)
                v.wait_ge(banks.freed["v"], banks.frees["v"])
                post_norm_add(m, gain)
                ada_columns()

            ada_done = [0]

            def ada_columns():
                for _ in range(ADA_GAP):
                    i, c = divmod(ada_done[0], N_MOD * D // BRANCH)
                    ada_done[0] += 1
                    o = banks.take("v")
                    v.wait_ge(banks.filled, banks.at["v"])
                    bada = b_ada[:, i * N_MOD * KT + 4 * c:i * N_MOD * KT + 4 * c + 4]
                    ve.tensor_tensor(mods[i][:, 4 * c:4 * c + 4, :], o.rearrange("p (f s) -> p f s", s=P)[:, :, 0:2],
                                     bada.unsqueeze(2).broadcast_to([P, 4, 2]), ALU.add
                                     ).then_inc(banks.freed["v"], banks.free("v"))

            def ffn(i):
                pre_norm(X, gain_of(i, 2))
                ada_columns()
                cw = conv_w[:, i * CONV_W * 2 * FT:(i + 1) * CONV_W * 2 * FT]
                cb = conv_b[:, i * 2 * FT:(i + 1) * 2 * FT]

                def tap(w, f):
                    return cw[:, w * 2 * FT + f:w * 2 * FT + f + 1]

                def conv(j):
                    gu = GU[j % 2]
                    fs = (2 * j, 2 * j + 1, FT + 2 * j, FT + 2 * j + 1)
                    os = []
                    for n, f in enumerate(fs):
                        o = banks.take("v")
                        v.wait_ge(banks.filled, banks.at["v"])
                        os.append(o)
                        ins = ve.tensor_scalar(gu[:, n, :], o[:, 0:S], tap(2, f), cb[:, f:f + 1], ALU.mult, ALU.add)
                    ins.then_inc(v_step.sem, v_step.up())
                    v.wait_ge(v_step.sem, v_step.made)
                    for n, f in enumerate(fs):
                        ins = ve.scalar_tensor_tensor(gu[:, n, 1:S], os[n][:, 0:S - 1], tap(1, f), gu[:, n, 1:S], ALU.mult, ALU.add)
                    ins.then_inc(v_step.sem, v_step.up())
                    v.wait_ge(v_step.sem, v_step.made)
                    for n, f in enumerate(fs):
                        ve.scalar_tensor_tensor(gu[:, n, 2:S], os[n][:, 0:S - 2], tap(0, f), gu[:, n, 2:S], ALU.mult, ALU.add).then_inc(banks.freed["v"], banks.free("v"))
                    v.wait_ge(banks.freed["v"], banks.frees["v"])
                    stamp().then_inc(gate_ready.sem, gate_ready.up())

                def glu(j):
                    gu, ge = GU[j % 2], GE[j % 2]
                    v.wait_ge(gate_exp.sem, gate_exp.nth("v"))
                    ve.scalar_tensor_tensor(ge, ge, 1.0, gu[:, 0:2, :], ALU.add, ALU.mult).then_inc(v_step.sem, v_step.up())
                    v.wait_ge(v_step.sem, v_step.made)
                    ve.scalar_tensor_tensor(HID[:, 2 * j:2 * j + 2, :], ge, 0.5, gu[:, 2:4, :], ALU.mult, ALU.mult
                                            ).then_inc(hidden_ready.sem, hidden_ready.up())
                    v.wait_ge(hidden_ready.sem, hidden_ready.made)

                conv(0)
                for j in range(FT // 2):
                    if j + 1 < FT // 2:
                        conv(j + 1)
                    glu(j)
                mixer_out(SM, gain_of(i, 3))

            pre_norm(X, gain_of(0, 0))
            ada_columns()
            for T in (SQT, SKT):
                for t in range(4):
                    evac(T[:, t, :], S)
            for c in range(2):
                for t in range(ST):
                    evac(SV[:, t, c * BRANCH:(c + 1) * BRANCH], BRANCH)
            v.wait_ge(banks.freed["v"], banks.frees["v"])
            stamp().then_inc(qkv_ready.sem, qkv_ready.up())

            def staged(n, *stages, fill=(), over=None):
                steps = n + 2 * LAG
                over = over or steps
                for step in range(steps):
                    for lag, stage in stages:
                        if 0 <= step - lag < n:
                            stage(step - lag)
                    for work in fill[len(fill) * step // over:len(fill) * (step + 1) // over]:
                        work()

            def bc2(x):
                return x.unsqueeze(1).broadcast_to([P, 2, 384])

            def sb_abs(b):
                z, e, L, p = SBUFS[4 * (b % 4):4 * (b % 4) + 4]
                v.wait_ge(z_copied.sem, z_copied.nth("v"))
                ve.scalar_tensor_tensor(e, z, -1.0, z, ALU.mult, ALU.min).then_inc(z_abs.sem, z_abs.up())

            def sb_logs(b):
                z, e, L, p = SBUFS[4 * (b % 4):4 * (b % 4) + 4]
                v.wait_ge(l_ready.sem, l_ready.nth("v"))
                ve.scalar_tensor_tensor(L, z, 0.0, e, ALU.max, ALU.add).then_inc(v_step.sem, v_step.up())
                v.wait_ge(v_step.sem, v_step.made)
                ve.tensor_tensor(L, L, bc2(cst("sb_keep")), ALU.mult).then_inc(L_ready.sem, L_ready.up())
                ve.tensor_tensor(z, z, bc2(cst("sb_neg")), ALU.add).then_inc(v_step.sem, v_step.up())
                v.wait_ge(v_step.sem, v_step.made)

            def sb_args(b):
                z = SBUFS[4 * (b % 4)]
                for j in range(2):
                    o = banks.take("v")
                    v.wait_ge(banks.filled, banks.at["v"])
                    ve.tensor_tensor(z[:, j, :], o[:, 0:384], z[:, j, :], ALU.add).then_inc(banks.freed["v"], banks.free("v"))
                v.wait_ge(banks.freed["v"], banks.frees["v"])
                stamp().then_inc(t_ready.sem, t_ready.up())

            def second_half():
                v.wait_ge(banks.freed["v"], banks.frees["v"])
                stamp().then_inc(qkv_ready.sem, qkv_ready.up())

            fill = [lambda T=T, t=t: evac(T[:, t, :], S) for T in (SQT, SKT) for t in range(4, 8)]
            fill[-1] = lambda: (evac(SKT[:, 7, :], S), second_half())
            staged(2 * SB_HALF, (0, sb_abs), (1, sb_logs), (2, sb_args), (3, lambda b: evac(SOT[:, b, :], S)),
                   fill=fill, over=SB_HALF)
            v.wait_ge(banks.freed["v"], banks.frees["v"])
            stamp().then_inc(o_ready.sem, o_ready.up())
            mixer_out(SM, gain_of(0, 1))
            ffn(0)

            pre_norm(X, gain_of(1, 0))
            ada_columns()
            for t in range(12):
                evac(DQT[:, t, :], S)
            for t in range(12):
                evac(DKT[:, t, :], S)
            for g in range(3):
                for t in range(ST):
                    evac(DV[:, t, g * BRANCH:(g + 1) * BRANCH], BRANCH)
            v.wait_ge(banks.freed["v"], banks.frees["v"])
            stamp().then_inc(qkv_ready.sem, qkv_ready.up())
            items = [(h, t) for h in range(DIL_HEADS) for t in range(ST)]
            v.wait_ge(loads["bias_in"], 16)

            def normalise(n, s):
                v.wait_ge(exp_ready.sem, exp_ready.nth("v"))
                ve.reciprocal(rsum[:, n % 2, 0:1], ssum[:, n % 2, 0:1]).then_inc(v_step.sem, v_step.up())
                v.wait_ge(v_step.sem, v_step.made)
                ve.tensor_scalar(s, s, rsum[:, n % 2, 0:1], None, ALU.mult).then_inc(p_ready.sem, p_ready.up())

            def dil_soft(n):
                h, t = items[n]
                k = (t + 1) * P
                s = DS[n % 3][:, :, 0:k]
                for g in range(3):
                    o = banks.take("v")
                    v.wait_ge(banks.filled, banks.at["v"])
                    ve.scalar_tensor_tensor(s[:, g, :], o[:, 0:k], SCALE, DB[:, g * DIL_HEADS + h, S - k:S], ALU.mult, ALU.add).then_inc(banks.freed["v"], banks.free("v"))
                v.wait_ge(banks.freed["v"], banks.frees["v"])
                ve.tensor_reduce(nmax[:, n % 2, 0:1], s, AX.XY, ALU.max, negate=True).then_inc(max_ready.sem, max_ready.up())

            def dil_norm(n):
                h, t = items[n]
                normalise(n, DS[n % 3][:, :, 0:(t + 1) * P])

            def dil_copy(n):
                h, t = items[n]
                o = banks.take("v")
                v.wait_ge(banks.filled, banks.at["v"])
                r = DH * (h % 2)
                ve.tensor_copy(DOT[r:r + DH, h // 2, t * P:(t + 1) * P], o[r:r + DH, 0:P]).then_inc(banks.freed["v"], banks.free("v"))

            staged(len(items), (0, dil_soft), (1, dil_norm), (2 * LAG, dil_copy))
            v.wait_ge(banks.freed["v"], banks.frees["v"])
            stamp().then_inc(o_ready.sem, o_ready.up())
            mixer_out(SM, gain_of(1, 1))
            ffn(1)

            stamp().then_inc(dma_free.sem, dma_free.up())
            def modulated_norm(i, which, ns):
                mod = mods[i]
                sc = mod[:, 24 * which + 8:24 * which + 16, :]
                g = g_norm[which][:, i * KT:(i + 1) * KT]
                for s in range(ns):
                    ins = ve.scalar_tensor_tensor(ampl[:, :, s], sc[:, :, s], 1.0, g, ALU.add, ALU.mult)
                ins.then_inc(v_step.sem, v_step.up())
                v.wait_ge(v_step.sem, v_step.made)
                v.wait_ge(rstd_ready.sem, rstd_ready.nth("v"))
                for k in range(0, KT, GRP):
                    ve.tensor_tensor(H[:, k:k + GRP, 0:ns * S], X[:, k:k + GRP, 0:ns * S],
                                     rstd[:, 0:ns * S].unsqueeze(1).broadcast_to([P, GRP, ns * S]), ALU.mult
                                     ).then_inc(xn_ready.sem, xn_ready.up())

            def add_gated(i, which, ns):
                gt = mods[i][:, 24 * which + 16:24 * which + 24, :]
                for f in range(KT):
                    o = banks.take("v")
                    v.wait_ge(banks.filled, banks.at["v"])
                    for s in range(ns):
                        t = slice(s * S, (s + 1) * S)
                        ins = ve.scalar_tensor_tensor(X[:, f, t], o[:, t], gt[:, f, s:s + 1], X[:, f, t], ALU.mult, ALU.add)
                    ins.then_inc(banks.freed["v"], banks.free("v"))
                    if which == 0:
                        tile_written(f)
                v.wait_ge(banks.freed["v"], banks.frees["v"])
                if which == 1:
                    src_written.extend([(banks.freed["v"], banks.frees["v"])] * (KT // GRP))

            for i in range(DEPTH):
                last = i == DEPTH - 1
                ns = 1 if last else 2
                qtok, qtiles = ns * S, ns * ST
                mod = mods[i]
                ve.tensor_scalar(mod[:, 16:24, :], mod[:, 16:24, :], 0.5, None, ALU.mult).then_inc(v_step.sem, v_step.up())
                v.wait_ge(v_step.sem, v_step.made)
                modulated_norm(i, 0, 2)
                v.wait_ge(loads["lam"], 64 * (i + 1))
                ve.tensor_tensor(LAMV[:, 0, :], LAMV[:, 0, :], LAMV[:, 1, :], ALU.mult).then_inc(v_step.sem, v_step.up())
                v.wait_ge(v_step.sem, v_step.made)
                ve.tensor_tensor(LAMV[:, 2, :], LAMV[:, 2, :], LAMV[:, 3, :], ALU.mult).then_inc(v_step.sem, v_step.up())
                v.wait_ge(v_step.sem, v_step.made)
                ve.tensor_reduce(lam2[:, 0:1], LAMV[:, 0, :], AX.X, ALU.add).then_inc(v_step.sem, v_step.up())
                v.wait_ge(v_step.sem, v_step.made)
                ve.tensor_reduce(lam2[:, 1:2], LAMV[:, 2, :], AX.X, ALU.add).then_inc(lam_ready.sem, lam_ready.up())
                v.wait_ge(lam_exp.sem, lam_exp.nth("v"))
                lam_init = 0.8 - 0.6 * math.exp(-0.3 * i)
                ve.tensor_tensor(neg_lam, lam2[:, 1:2], lam2[:, 0:1], ALU.subtract).then_inc(v_step.sem, v_step.up())
                v.wait_ge(v_step.sem, v_step.made)
                ve.tensor_scalar(neg_lam, neg_lam, -lam_init, None, ALU.add).then_inc(v_step.sem, v_step.up())
                v.wait_ge(v_step.sem, v_step.made)
                ve.tensor_scalar(g_head, subln[:, i:i + 1], 1.0 - lam_init, None, ALU.mult).then_inc(v_step.sem, v_step.up())
                v.wait_ge(v_step.sem, v_step.made)

                for g in range(4):
                    evac(UT[:, g, 0:qtok], qtok)
                for t in range(qtiles):
                    evac(VG[:, t, :], 512)
                ws = banks.take("v")
                v.wait_ge(banks.filled, banks.at["v"])
                ve.tensor_copy(WST.rearrange("p g c -> p (g c)"), ws).then_inc(banks.freed["v"], banks.free("v"))
                v.wait_ge(banks.freed["v"], banks.frees["v"])
                v.wait_ge(banks.freed["v"], banks.frees["v"])

                def gelu(x, t):
                    ve.tensor_tensor(t, x, x, ALU.mult).then_inc(v_step.sem, v_step.up())
                    v.wait_ge(v_step.sem, v_step.made)
                    ve.tensor_scalar(t, t, 0.044715, 1.0, ALU.mult, ALU.add).then_inc(v_step.sem, v_step.up())
                    v.wait_ge(v_step.sem, v_step.made)
                    ve.tensor_tensor(t, t, x, ALU.mult).then_inc(gate_ready.sem, gate_ready.up())
                    v.wait_ge(gate_exp.sem, gate_exp.nth("v"))
                    ve.scalar_tensor_tensor(x, t, 1.0, x, ALU.add, ALU.mult).then_inc(v_step.sem, v_step.up())
                    v.wait_ge(v_step.sem, v_step.made)

                gelu(VG[:, 0:qtiles, :], TG[:, 0:qtiles, :])
                vg = VG[:, 0:qtiles, :]

                def rows(x):
                    return x.unsqueeze(2).broadcast_to([P, qtiles, 512])

                def all_tiles(x):
                    return x.unsqueeze(1).broadcast_to([P, qtiles, 512])

                m, var, rs = (stat[:, j, 0:qtiles] for j in range(3))
                ve.tensor_reduce(m, vg, AX.X, ALU.add).then_inc(v_step.sem, v_step.up())
                v.wait_ge(v_step.sem, v_step.made)
                ve.tensor_scalar(m, m, -0.5 / BRANCH, None, ALU.mult).then_inc(v_step.sem, v_step.up())
                v.wait_ge(v_step.sem, v_step.made)
                ve.scalar_tensor_tensor(vg, vg, 0.5, rows(m), ALU.mult, ALU.add).then_inc(v_step.sem, v_step.up())
                v.wait_ge(v_step.sem, v_step.made)
                ve.tensor_tensor(TG[:, 0:qtiles, :], vg, vg, ALU.mult).then_inc(v_step.sem, v_step.up())
                v.wait_ge(v_step.sem, v_step.made)
                ve.tensor_reduce(var, TG[:, 0:qtiles, :], AX.X, ALU.add).then_inc(ln_rstd.sem, ln_rstd.up())
                v.wait_ge(rstd_ready.sem, rstd_ready.nth("v"))
                ve.tensor_tensor(vg, vg, rows(rs), ALU.mult).then_inc(v_step.sem, v_step.up())
                v.wait_ge(v_step.sem, v_step.made)
                v.wait_ge(loads["gm"], 64 * (i + 1))
                ve.tensor_tensor(vg, vg, all_tiles(GMR[:, 0, :]), ALU.mult).then_inc(v_step.sem, v_step.up())
                v.wait_ge(v_step.sem, v_step.made)
                ve.tensor_tensor(vg, vg, all_tiles(GMR[:, 1, :]), ALU.add).then_inc(ln_ready.sem, ln_ready.up())
                gelu(UT[:, :, 0:qtok], TG[:, :, 0:qtok])
                for c in range(4):
                    evac(KT2[:, c, :], 2 * S)
                for t in range(4):
                    evac(V2[:, t, :], 512)
                for c in range(4):
                    evac(QT2[:, c, 0:qtok], qtok)
                v.wait_ge(banks.freed["v"], banks.frees["v"])
                stamp().then_inc(qkv_ready.sem, qkv_ready.up())
                v.wait_ge(loads["rpb_in"], 256 * (i + 1))
                ve.tensor_tensor(BN.rearrange("p h r c -> p (h r) c"), BN.rearrange("p h r c -> p (h r) c"),
                                                cst("col_neg").unsqueeze(1).broadcast_to([P, NA_HEADS * NA_DR, GRID_W]), ALU.add).then_inc(bias_tile.sem, bias_tile.up())
                v.wait_ge(bias_tile.sem, bias_tile.made)
                for g in range(4):
                    o = banks.take("v")
                    v.wait_ge(banks.filled, banks.at["v"])
                    ve.tensor_tensor(YCU[:, g, 0:qtok].rearrange("p (t q) -> p t q", q=P),
                                          o[:, 0:qtok].rearrange("p (t q) -> p t q", q=P),
                                          GMR[:, 2, g * P:(g + 1) * P].unsqueeze(1).broadcast_to([P, qtiles, P]), ALU.add).then_inc(banks.freed["v"], banks.free("v"))
                v.wait_ge(banks.freed["v"], banks.frees["v"])
                ve.scalar_tensor_tensor(YCU[:, :, 0:qtok], YCU[:, :, 0:qtok], 0.5, UT[:, :, 0:qtok], ALU.mult, ALU.mult).then_inc(y_ready.sem, y_ready.up())
                v.wait_ge(y_ready.sem, y_ready.made)

                items = [(h, t) for h in range(NA_HEADS) for t in range(qtiles)]

                def na_soft(n):
                    h, t = items[n]
                    s = NAS[n % 4][:, :]
                    o = banks.take("v")
                    v.wait_ge(banks.filled, banks.at["v"])
                    if t < ST:
                        ve.scalar_tensor_tensor(s[:, 0:S].rearrange("p (r c) -> p r c", c=GRID_W),
                                                     o[:, 0:S].rearrange("p (r c) -> p r c", c=GRID_W), SCALE,
                                                     BN[:, h, 2 - 2 * t:6 - 2 * t, :], ALU.mult, ALU.add).then_inc(v_step.sem, v_step.up())
                    ve.tensor_scalar(s[:, S:2 * S], o[:, S:2 * S], SCALE, None, ALU.mult).then_inc(banks.freed["v"], banks.free("v"))
                    v.wait_ge(banks.freed["v"], banks.frees["v"])
                    if t >= ST:
                        s = s[:, S:2 * S]
                    ve.tensor_reduce(nmax[:, n % 2, 0:1], s, AX.X, ALU.max, negate=True).then_inc(max_ready.sem, max_ready.up())

                def na_norm(n):
                    h, t = items[n]
                    k0 = 0 if t < ST else S
                    normalise(n, NAS[n % 4][:, k0:2 * S])

                def na_copy(n):
                    h, t = items[n]
                    o = banks.take("v")
                    v.wait_ge(banks.filled, banks.at["v"])
                    r = DH * (h % 2)
                    ve.tensor_copy(Y2[0][r:r + DH, h // 2, t * P:(t + 1) * P], o[r:r + DH, 0:P]).then_inc(banks.freed["v"], banks.free("v"))

                staged(len(items), (0, na_soft), (1, na_norm), (2 * LAG, na_copy),
                       fill=[lambda c=c: evac(KT3[:, c, :], 2 * S) for c in range(4)]
                       + [lambda t=t: evac(V3[:, t, :], 512) for t in range(4)]
                       + [lambda c=c: evac(QT3[:, c, 0:qtok], qtok) for c in range(4)])

                v.wait_ge(banks.freed["v"], banks.frees["v"])
                stamp().then_inc(qkv_ready.sem, qkv_ready.up())
                for T in (KT3, QT3):
                    for c in range(4):
                        o = banks.take("v")
                        v.wait_ge(banks.filled, banks.at["v"])
                        ve.tensor_tensor(ROPE_T, o[:, 0:S], cst("sin"), ALU.mult).then_inc(banks.freed["v"], banks.free("v"))
                        v.wait_ge(banks.freed["v"], banks.frees["v"])
                        ve.tensor_tensor(T[:, c, 0:S], T[:, c, 0:S], cst("cos"), ALU.mult).then_inc(v_step.sem, v_step.up())
                        v.wait_ge(v_step.sem, v_step.made)
                        ve.tensor_tensor(T[:, c, 0:S], T[:, c, 0:S], ROPE_T, ALU.add).then_inc(v_step.sem, v_step.up())
                        v.wait_ge(v_step.sem, v_step.made)
                stamp().then_inc(rope_ready.sem, rope_ready.up())
                items = [(h, t) for h in range(DA_HEADS) for t in range(qtiles)]

                def da_soft(n):
                    h, t = items[n]
                    k0 = 0 if t < ST else S
                    for c in range(2):
                        o = banks.take("v")
                        v.wait_ge(banks.filled, banks.at["v"])
                        ve.tensor_reduce(nmax[:, n % 2, c:c + 1], o[:, k0:2 * S], AX.X, ALU.max, negate=True).then_inc(v_step.sem, v_step.up())
                        v.wait_ge(v_step.sem, v_step.made)
                    ve.tensor_scalar(nmax[:, n % 2, 0:2], nmax[:, n % 2, 0:2], SCALE, None, ALU.mult).then_inc(max_ready.sem, max_ready.up())

                def da_norm(n):
                    h, t = items[n]
                    k0 = 0 if t < ST else S
                    e0, e1 = S2[n % 3][:, 0, k0:2 * S], S2[n % 3][:, 1, k0:2 * S]
                    v.wait_ge(exp_ready.sem, exp_ready.nth("v"))
                    ve.reciprocal(rsum[:, n % 2, 0:2], ssum[:, n % 2, 0:2]).then_inc(v_step.sem, v_step.up())
                    v.wait_ge(v_step.sem, v_step.made)
                    ve.tensor_tensor(rsum[:, n % 2, 1:2], rsum[:, n % 2, 1:2], neg_lam, ALU.mult).then_inc(v_step.sem, v_step.up())
                    v.wait_ge(v_step.sem, v_step.made)
                    ve.tensor_scalar(e0, e0, rsum[:, n % 2, 0:1], None, ALU.mult).then_inc(v_step.sem, v_step.up())
                    v.wait_ge(v_step.sem, v_step.made)
                    ve.scalar_tensor_tensor(e0, e1, rsum[:, n % 2, 1:2], e0, ALU.mult, ALU.add).then_inc(p_ready.sem, p_ready.up())

                def da_copy(n):
                    h, t = items[n]
                    o = banks.take("v")
                    v.wait_ge(banks.filled, banks.at["v"])
                    ve.tensor_copy(O2[:, h, t * P:(t + 1) * P], o[:, 0:P]).then_inc(banks.freed["v"], banks.free("v"))

                def merge_tile(n, f):
                    g = GS[n % 2][:, :, 0:qtok]
                    if f == 0:
                        v.wait_ge(gate_exp.sem, gate_exp.nth("v"))
                    o = banks.take("v")
                    v.wait_ge(banks.filled, banks.at["v"])
                    ve.scalar_tensor_tensor(MB[:, 4 * (n % 2) + f, 0:qtok] if n < 2 else g[:, f, :], g[:, f, :], 1.0,
                                            o[:, 0:qtok], ALU.add, ALU.mult
                                            ).then_inc(banks.freed["v"], banks.free("v"))
                    if f < 3:
                        return
                    v.wait_ge(banks.freed["v"], banks.frees["v"])
                    m = MB[:, 4 * (n % 2):4 * (n % 2) + 4, 0:qtok]
                    if n < 2:
                        stamp().then_inc(gate_used.sem, gate_used.up())
                    else:
                        ve.tensor_tensor(m, m, g, ALU.add).then_inc(gate_used.sem, gate_used.up())
                        v.wait_ge(gate_used.sem, gate_used.made)

                gate_turn = [lambda: None] * 4
                fill = []
                for n in range(4):
                    fill += gate_turn + [lambda n=n, f=f: merge_tile(n, f) for f in range(4)]
                staged(len(items), (0, da_soft), (1, da_norm), (2 * LAG, da_copy), fill=fill[4:])
                v.wait_ge(banks.freed["v"], banks.frees["v"])
                ve.tensor_tensor(Y2[1][:, :, 0:qtok], O2[:, :, 0:qtok], O2[:, :, 0:qtok], ALU.mult).then_inc(sq_ready.sem, sq_ready.up())
                for h in range(DA_HEADS):
                    v.wait_ge(rstd_ready.sem, rstd_ready.nth("v"))
                    ins = ve.scalar_tensor_tensor(Y2[1][:, h, 0:qtok], O2[:, h, 0:qtok], g_head, S2[h // 2][:, h % 2, 0:qtok],
                                                  ALU.mult, ALU.mult)
                ins.then_inc(y_ready.sem, y_ready.up())
                v.wait_ge(y_ready.sem, y_ready.made)

                for half in range(2):
                    for f in range(4):
                        merge_tile(4 + half, f)
                stamp().then_inc(merged_ready.sem, merged_ready.up())
                add_gated(i, 0, ns)

                modulated_norm(i, 1, ns)
                o = banks.take("v")
                v.wait_ge(banks.filled, banks.at["v"])
                lg = o[:, 0:qtiles * N_EXPERTS].rearrange("p (t e) -> p t e", e=N_EXPERTS)
                ve.tensor_reduce(mx4[:, 0:qtiles], lg, AX.X, ALU.max, negate=True).then_inc(v_step.sem, v_step.up())
                v.wait_ge(v_step.sem, v_step.made)
                stamp().then_inc(max_ready.sem, max_ready.up())
                v.wait_ge(exp_ready.sem, exp_ready.nth("v"))
                ve.reciprocal(rden[:, 0:qtiles], den4[:, 0:qtiles]).then_inc(v_step.sem, v_step.up())
                v.wait_ge(v_step.sem, v_step.made)
                for t in range(qtiles):
                    af = aff[:, t % 2, t // 2, :]
                    ins = ve.tensor_scalar(af, af, rden[:, t:t + 1], None, ALU.mult)
                    if t < qtiles - 1:
                        ins.then_inc(v_step.sem, v_step.up())
                ins.then_inc(aff_ready.sem, aff_ready.up())
                nr = ns * N_EXPERTS
                o = banks.take("v")
                v.wait_ge(banks.filled, banks.at["v"])
                at, aw, sc, keep = AT[0:nr, 0, :], AW[0:nr, :], AT[0:nr, 1, :], AT[0:nr, 0, :]
                ve.tensor_copy(aw, o[0:nr, 0:S]).then_inc(banks.freed["v"], banks.free("v"))
                v.wait_ge(banks.freed["v"], banks.frees["v"])
                for _ in range(CAP // 8):
                    ve.max(top8[0:nr], aw).then_inc(v_step.sem, v_step.up())
                    v.wait_ge(v_step.sem, v_step.made)
                    ve.match_replace(aw, top8[0:nr], aw, -1.0).then_inc(v_step.sem, v_step.up())
                    v.wait_ge(v_step.sem, v_step.made)
                ve.tensor_scalar(keep, aw, 0.0, None, ALU.is_lt).then_inc(v_step.sem, v_step.up())
                v.wait_ge(v_step.sem, v_step.made)
                for j in range(ST):
                    t = slice(j * P, (j + 1) * P)
                    ve.tensor_tensor_scan(sc[:, t], ones[0:nr, :], keep[:, t], sc[:, P - 1:P] if j else 0.0,
                                               ALU.mult, ALU.add).then_inc(v_step.sem, v_step.up())
                    v.wait_ge(v_step.sem, v_step.made)
                ve.tensor_tensor(sc, sc, keep, ALU.mult).then_inc(v_step.sem, v_step.up())
                v.wait_ge(v_step.sem, v_step.made)
                ve.tensor_scalar(aw, sc, -1.0, None, ALU.add).then_inc(pos_ready.sem, pos_ready.up())
                o = banks.take("v")
                v.wait_ge(banks.filled, banks.at["v"])
                ve.tensor_copy(pos[:, :, 0:nr], o[:, 0:64].rearrange("p (j r) -> p j r", j=ST)[:, :, 0:nr]).then_inc(banks.freed["v"], banks.free("v"))
                v.wait_ge(banks.freed["v"], banks.frees["v"])
                for j in range(ST):
                    ins = ve.tensor_tensor(SEL[:, j, 0:nr, :], pos[:, j, 0:nr].unsqueeze(2).broadcast_to([P, nr, CAP]),
                                           cst("iota").unsqueeze(1).broadcast_to([P, nr, CAP]), ALU.is_equal)
                    if j == 0:
                        ins.then_inc(v_step.sem, v_step.up())
                ins.then_inc(P_ready.sem, P_ready.up())
                v.wait_ge(P_ready.sem, P_ready.made)
                for j in range(ST):
                    ins = ve.tensor_tensor(GSEL[:, j, 0:nr, :], SEL[:, j, 0:nr, :],
                                           aff[:, j, 0:ns, :].rearrange("p q e -> p (q e)").unsqueeze(2).broadcast_to([P, nr, CAP]), ALU.mult)
                    if j == 0:
                        ins.then_inc(v_step.sem, v_step.up())
                ins.then_inc(G_ready.sem, G_ready.up())
                for k in range(KT):
                    for q in range(ns):
                        o = banks.take("v")
                        v.wait_ge(banks.filled, banks.at["v"])
                        ve.tensor_copy(XIN[:, k, :, q * CAP:(q + 1) * CAP], o.rearrange("p (e s) -> p e s", s=CAP)).then_inc(banks.freed["v"], banks.free("v"))
                v.wait_ge(banks.freed["v"], banks.frees["v"])
                stamp().then_inc(xin_ready.sem, xin_ready.up())
                w = ns * CAP
                for e in range(N_EXPERTS):
                    for half in range(2):
                        evac(HR[1][:, half * 512:(half + 1) * 512], 512)
                    he, ge = HE[e % 2], HG[e % 2]
                    v.wait_ge(gate_exp.sem, gate_exp.nth("v"))
                    for half in range(2):
                        o = banks.take("v").rearrange("p (f s) -> p f s", s=P)
                        v.wait_ge(banks.filled, banks.at["v"])
                        f = slice(4 * half, 4 * half + 4)
                        ve.scalar_tensor_tensor(ge[:, f, 0:w], ge[:, f, 0:w], 1.0, o[:, :, 0:w], ALU.add, ALU.mult
                                                ).then_inc(banks.freed["v"], banks.free("v"))
                    v.wait_ge(banks.freed["v"], banks.frees["v"])
                    for half in range(2):
                        o = banks.take("v").rearrange("p (f s) -> p f s", s=P)
                        v.wait_ge(banks.filled, banks.at["v"])
                        f = slice(4 * half, 4 * half + 4)
                        ve.scalar_tensor_tensor(he[:, f, 0:w], ge[:, f, 0:w], 0.5, o[:, :, 0:w], ALU.mult, ALU.mult
                                                ).then_inc(banks.freed["v"], banks.free("v"))
                    v.wait_ge(banks.freed["v"], banks.frees["v"])
                    stamp().then_inc(hidden_ready.sem, hidden_ready.up())
                    v.wait_ge(hidden_ready.sem, hidden_ready.made)
                add_gated(i, 1, ns)
                if not last:
                    stamp().then_inc(dma_free.sem, dma_free.up())

            pre_norm(X, g_final)

        @block.scalar
        def _(sc):
            se = nc.scalar
            stamps = [0]

            def stamp():
                stamps[0] += 1
                at = 1000 + stamps[0] % 24
                return se.activation(small[:, at:at + 1], eps, ACT.Copy)




            def inverse_root(dst, src, n, scale=1.0):
                se.activation(dst, src, ACT.Ln, bias=eps).then_inc(banks.freed["a"], banks.free("a"))
                sc.wait_ge(banks.freed["a"], banks.frees["a"])
                se.activation(dst, dst, ACT.Exp, scale=-0.5).then_inc(rstd_ready.sem, rstd_ready.up())

            def norm(src, n):
                for k in range(0, KT, GRP):
                    sc.wait_ge(*src_written.pop(0))
                    se.activation(H[:, k:k + GRP, 0:n], src[:, k:k + GRP, 0:n], ACT.Square).then_inc(sq_ready.sem, sq_ready.up())
                o = banks.take("a")
                sc.wait_ge(banks.filled, banks.at["a"])
                inverse_root(rstd[:, 0:n], o[:, 0:n], n)

            def scale_shift(i, which, ns):
                sh = mods[i][:, 24 * which:24 * which + 8, :]
                for k in range(0, KT, GRP):
                    sc.wait_ge(xn_ready.sem, xn_ready.nth("a"))
                    for n, s in ((n, s) for n in range(k, k + GRP) for s in range(ns)):
                        t = slice(s * S, (s + 1) * S)
                        ins = se.activation(H[:, n, t], H[:, n, t], ACT.Identity, bias=sh[:, n, s:s + 1], scale=ampl[:, n, s:s + 1])
                    ins.then_inc(h_ready.sem, h_ready.up())

            def gate(x, src=None, scale=0.5):
                sc.wait_ge(gate_ready.sem, gate_ready.nth("a"))
                se.activation(x, x if src is None else src, ACT.Tanh, scale=scale).then_inc(gate_exp.sem, gate_exp.up())

            ada_copied = [0]

            def ada_copies():
                for _ in range(ADA_GAP):
                    o = banks.take("a")
                    sc.wait_ge(banks.filled, banks.at["a"])
                    se.activation(ADA[ada_copied[0] % 2], o, ACT.Copy).then_inc(banks.freed["a"], banks.free("a"))
                    ada_copied[0] += 1

            def ffn():
                norm(X, S)
                ada_copies()
                for j in range(FT // 2):
                    gate(GE[j % 2], GU[j % 2][:, 0:2, :])
                norm(SM, S)
                ada_copies()

            gate(silu_c, sc16)
            norm(X, S)
            ada_copies()
            sc.wait_ge(loads["bias_out"], 16)

            def staged(n, *stages, fill=(), over=None):
                steps = n + 2 * LAG
                over = over or steps
                for step in range(steps):
                    for lag, stage in stages:
                        if 0 <= step - lag < n:
                            stage(step - lag)
                    for work in fill[len(fill) * step // over:len(fill) * (step + 1) // over]:
                        work()

            def sb_first(b):
                z, e, L, p = SBUFS[4 * (b % 4):4 * (b % 4) + 4]
                for j in range(2):
                    o = banks.take("a")
                    sc.wait_ge(banks.filled, banks.at["a"])
                    se.activation(z[:, j, :], o[:, 0:384], ACT.Copy, scale=SCALE).then_inc(banks.freed["a"], banks.free("a"))
                sc.wait_ge(banks.freed["a"], banks.frees["a"])
                stamp().then_inc(z_copied.sem, z_copied.up())
                sc.wait_ge(z_abs.sem, z_abs.nth("a"))
                se.activation(e, e, ACT.Exp).then_inc(a_step.sem, a_step.up())
                sc.wait_ge(a_step.sem, a_step.made)
                se.activation(e, e, ACT.Ln, bias=1.0).then_inc(l_ready.sem, l_ready.up())

            def sb_second(b):
                z, e, L, p = SBUFS[4 * (b % 4):4 * (b % 4) + 4]
                sc.wait_ge(t_ready.sem, t_ready.nth("a"))
                se.activation(p, z, ACT.Exp).then_inc(sb_p_ready.sem, sb_p_ready.up())

            staged(2 * SB_HALF, (0, sb_first), (2, sb_second))
            norm(SM, S)
            ada_copies()
            ffn()

            norm(X, S)
            ada_copies()
            items = [(h, t) for h in range(DIL_HEADS) for t in range(ST)]

            def row_exp(n, s, k=0, src=None, scale=1.0):
                return se.activation(s, s if src is None else src, ACT.Exp, bias=nmax[:, n % 2, k:k + 1], scale=scale,
                                     accum_out=ssum[:, n % 2, k:k + 1])

            def dil_exp(n):
                h, t = items[n]
                sc.wait_ge(max_ready.sem, max_ready.nth("a"))
                row_exp(n, DS[n % 3][:, :, 0:(t + 1) * P]).then_inc(exp_ready.sem, exp_ready.up())

            def dil_pt(n):
                h, t = items[n]
                tiles = 3 * (t + 1)
                for n0 in range(0, tiles, 4):
                    m = min(4, tiles - n0)
                    o = banks.take("a")
                    sc.wait_ge(banks.filled, banks.at["a"])
                    se.activation(DPT[n % 2][:, n0:n0 + m, :].rearrange("p a b -> p (a b)"), o[:, 0:m * P], ACT.Copy).then_inc(banks.freed["a"], banks.free("a"))
                sc.wait_ge(banks.freed["a"], banks.frees["a"])
                stamp().then_inc(pt_ready.sem, pt_ready.up())

            staged(len(items), (0, dil_exp), (LAG, dil_pt))
            norm(SM, S)
            ada_copies()
            ffn()

            for i in range(DEPTH):
                last = i == DEPTH - 1
                ns = 1 if last else 2
                qtok, qtiles = ns * S, ns * ST
                norm(X, 2 * S)
                scale_shift(i, 0, 2)
                sc.wait_ge(lam_ready.sem, lam_ready.nth("a"))
                se.activation(lam2, lam2, ACT.Exp).then_inc(lam_exp.sem, lam_exp.up())
                gelu_scale = math.sqrt(2.0 / math.pi)
                gates_before = 6 * i
                gate(TG[:, 0:qtiles, :], scale=gelu_scale)
                sc.wait_ge(ln_rstd.sem, ln_rstd.nth("a"))
                se.activation(stat[:, 2, 0:qtiles], stat[:, 1, 0:qtiles], ACT.Ln, bias=eps, scale=1.0 / BRANCH).then_inc(a_step.sem, a_step.up())
                sc.wait_ge(a_step.sem, a_step.made)
                se.activation(stat[:, 2, 0:qtiles], stat[:, 2, 0:qtiles], ACT.Exp, scale=-0.5).then_inc(rstd_ready.sem, rstd_ready.up())
                gate(TG[:, :, 0:qtok], scale=gelu_scale)
                items = [(h, t) for h in range(NA_HEADS) for t in range(qtiles)]

                def pt_copy(n, t):
                    k0 = 0 if t < ST else ST
                    o = banks.take("a")
                    sc.wait_ge(banks.filled, banks.at["a"])
                    se.activation(PT2[n % 2].rearrange("p a b -> p (a b)")[:, k0 * P:512], o[:, k0 * P:512], ACT.Copy).then_inc(banks.freed["a"], banks.free("a"))
                    sc.wait_ge(banks.freed["a"], banks.frees["a"])
                    stamp().then_inc(pt_ready.sem, pt_ready.up())

                def na_exp(n):
                    h, t = items[n]
                    sc.wait_ge(max_ready.sem, max_ready.nth("a"))
                    row_exp(n, NAS[n % 4][:, (0 if t < ST else S):2 * S]).then_inc(exp_ready.sem, exp_ready.up())

                staged(len(items), (0, na_exp), (LAG, lambda n: pt_copy(n, items[n][1])))
                items = [(h, t) for h in range(DA_HEADS) for t in range(qtiles)]

                def da_exp(n):
                    h, t = items[n]
                    k0 = 0 if t < ST else S
                    sc.wait_ge(max_ready.sem, max_ready.nth("a"))
                    for c in range(2):
                        o = banks.take("a")
                        sc.wait_ge(banks.filled, banks.at["a"])
                        row_exp(n, S2[n % 3][:, c, k0:2 * S], c, o[:, k0:2 * S], SCALE).then_inc(banks.freed["a"], banks.free("a"))
                    sc.wait_ge(banks.freed["a"], banks.frees["a"])
                    stamp().then_inc(exp_ready.sem, exp_ready.up())

                def gate_tile(n, f):
                    if f == 0 and n >= 2:
                        sc.wait_ge(gate_used.sem, gates_before + n - 1)
                    o = banks.take("a")
                    sc.wait_ge(banks.filled, banks.at["a"])
                    se.activation(GS[n % 2][:, f, 0:qtok], o[:, 0:qtok], ACT.Tanh, scale=0.5
                                  ).then_inc(banks.freed["a"], banks.free("a"))
                    if f == 3:
                        sc.wait_ge(banks.freed["a"], banks.frees["a"])
                        stamp().then_inc(gate_exp.sem, gate_exp.up())

                product_turn = [lambda: None] * 4
                fill = []
                for n in range(4):
                    fill += [lambda n=n, f=f: gate_tile(n, f) for f in range(4)] + product_turn
                for step in fill[0:4]:
                    step()
                staged(len(items), (0, da_exp), (LAG, lambda n: pt_copy(n, items[n][1])), fill=fill[4:])
                for h in range(DA_HEADS):
                    o = banks.take("a")
                    sc.wait_ge(banks.filled, banks.at["a"])
                    inverse_root(S2[h // 2][:, h % 2, 0:qtok], o[:, 0:qtok], qtok)
                for n in range(4, 6):
                    for f in range(4):
                        gate_tile(n, f)
                norm(X, qtok)
                scale_shift(i, 1, ns)

                o = banks.take("a")
                sc.wait_ge(banks.filled, banks.at["a"])
                se.activation(RPART[:, 0:qtok], o[:, 0:qtok], ACT.Copy).then_inc(banks.freed["a"], banks.free("a"))
                sc.wait_ge(banks.freed["a"], banks.frees["a"])
                stamp().then_inc(router_part.sem, router_part.up())
                for t in range(qtiles):
                    for half in range(2):
                        o = banks.take("a")
                        sc.wait_ge(banks.filled, banks.at["a"])
                        se.activation(HT[:, t, half * 512:(half + 1) * 512], o, ACT.Copy).then_inc(banks.freed["a"], banks.free("a"))
                    if t == 0:
                        o = banks.take("a")
                        sc.wait_ge(banks.filled, banks.at["a"])
                        sc.wait_ge(max_ready.sem, max_ready.nth("a"))
                        for u in range(qtiles):
                            ins = se.activation(aff[:, u % 2, u // 2, :], o[:, u * N_EXPERTS:(u + 1) * N_EXPERTS], ACT.Exp,
                                                bias=mx4[:, u:u + 1], accum_out=den4[:, u:u + 1])
                        ins.then_inc(banks.freed["a"], banks.free("a"))
                        sc.wait_ge(banks.freed["a"], banks.frees["a"])
                        stamp().then_inc(exp_ready.sem, exp_ready.up())
                sc.wait_ge(banks.freed["a"], banks.frees["a"])
                stamp().then_inc(tok_ready.sem, tok_ready.up())
                for q in range(ns):
                    for half in range(2):
                        o = banks.take("a")
                        sc.wait_ge(banks.filled, banks.at["a"])
                        se.activation(PGT[:, q, 2 * half:2 * half + 2, :].rearrange("p k t -> p (k t)"), o, ACT.Copy).then_inc(banks.freed["a"], banks.free("a"))
                w = ns * CAP
                for e in range(N_EXPERTS + 1):
                    if e < N_EXPERTS:
                        for half in range(2):
                            o = banks.take("a")
                            sc.wait_ge(banks.filled, banks.at["a"])
                            se.activation(HR[0][:, half * 512:(half + 1) * 512], o, ACT.Copy
                                          ).then_inc(banks.freed["a"], banks.free("a"))
                    if e:
                        r = CAP * ((e - 1) % 4)
                        for half in range(2):
                            o = banks.take("a")
                            sc.wait_ge(banks.filled, banks.at["a"])
                            for q in range(ns):
                                ins = se.activation(YE[q][r:r + CAP, (e - 1) // 4, half * 512:(half + 1) * 512],
                                                    o[q * CAP:(q + 1) * CAP, :], ACT.Copy)
                            ins.then_inc(banks.freed["a"], banks.free("a"))
                    if e < N_EXPERTS:
                        for half in range(2):
                            o = banks.take("a").rearrange("p (f s) -> p f s", s=P)
                            sc.wait_ge(banks.filled, banks.at["a"])
                            ins = se.activation(HG[e % 2][:, 4 * half:4 * half + 4, 0:w], o[:, :, 0:w], ACT.Tanh, scale=0.5)
                            if half == 0:
                                ins.then_inc(a_step.sem, a_step.up())
                        ins.then_inc(gate_exp.sem, gate_exp.up())
                sc.wait_ge(banks.freed["a"], banks.frees["a"])
                stamp().then_inc(ye_ready.sem, ye_ready.up())
            norm(X, S)
            for t in range(ST):
                for half in range(2):
                    o = banks.take("a")
                    sc.wait_ge(banks.filled, banks.at["a"])
                    se.activation(OUTT[:, t, half * 512:(half + 1) * 512], o, ACT.Copy).then_inc(banks.freed["a"], banks.free("a"))
            sc.wait_ge(banks.freed["a"], banks.frees["a"])
            stamp().then_inc(final_ready.sem, final_ready.up())

        @block.gpsimd
        def _(gp):
            def dram(ap, offset, dims):
                return bass.AP(tensor=ap.tensor, offset=offset, ap=dims)

            gp.wait_ge(bias_rows.sem, bias_rows.nth("gp"))
            gp.dma_start(bias_scratch.rearrange("(g h) n -> h g n", g=3),
                         view(DROW, 3, 384)[0:DIL_HEADS]).then_inc(loads["bias_out"], 16)
            gp.wait_ge(loads["bias_out"], 16)
            gp.dma_start(dram(bias_shear, 0, [[P * 386, 3 * DIL_HEADS], [385, P], [1, 384]]),
                         dram(bias_scratch, 0, [[384, 3 * DIL_HEADS], [0, P], [1, 384]])).then_inc(loads["bias_shear"], 16)
            gp.wait_ge(loads["bias_shear"], 16)
            gp.wait_ge(o_ready.sem, 1)
            gp.dma_start(DB, dram(bias_shear, P - 1, [[384, P], [P * 386, 3 * DIL_HEADS], [1, S]])).then_inc(loads["bias_in"], 16)
            gp.dma_start(rpb_scratch, a["zero_table"]).then_inc(loads["rpb_out"], 16)
            gp.wait_ge(loads["rpb_out"], 16)
            for i in range(DEPTH):
                gp.wait_ge(dma_free.sem, dma_free.nth("gp"))
                for n, name in enumerate(("da_lam_q1_2", "da_lam_k1_2", "da_lam_q2_2", "da_lam_k2_2")):
                    gp.dma_start(LAMV[:, n, :], dram(a[name], i * DH, [[0, P], [1, DH]])).then_inc(loads["lam"], 16)
                gp.dma_start(WS_RAW, a["gm_w_s_2"][i].rearrange("g p q -> p g q")).then_inc(loads["gm"], 16)
                for n, name in enumerate(("gm_ln_g_2", "gm_ln_b_2", "gm_b_s_2")):
                    gp.dma_start(GMR[:, n, :], dram(a[name], i * BRANCH, [[0, P], [1, BRANCH]])).then_inc(loads["gm"], 16)
                gp.dma_start(WR[:, :, 0:N_EXPERTS], a["w_router_2"][i].rearrange("(k p) e -> p k e", p=P)).then_inc(loads["router"], 16)
                gp.dma_start(rpb_scratch[:, :, 48:48 + 2 * NA_WIN_C - 1], a["na_rpb_2"][i]).then_inc(loads["rpb_out"], 16)
                gp.wait_ge(loads["rpb_out"], 16 * (i + 2))
                for h in range(NA_HEADS):
                    gp.dma_start(dram(rpb_shear, h * (NA_DR + 1) * GRID_W * 130, [[GRID_W * 130, NA_DR + 1], [129, GRID_W], [1, P]]),
                                 dram(rpb_scratch, (h * 15 + 4) * P, [[P, NA_DR + 1], [0, GRID_W], [1, P]])
                                 ).then_inc(loads["rpb_shear"], 16)
                gp.wait_ge(loads["rpb_shear"], 16 * NA_HEADS * (i + 1))
                for hh in range(2):
                    for h in range(NA_HEADS):
                        gp.dma_start(BN[hh * GRID_W:(hh + 1) * GRID_W, h, :, :],
                                     dram(rpb_shear, (h * (NA_DR + 1) + 1 - hh) * GRID_W * 130 + GRID_W - 1,
                                          [[P, GRID_W], [GRID_W * 130, NA_DR], [1, GRID_W]])).then_inc(loads["rpb_in"], 16)
                gp.wait_ge(loads["rpb_in"], 256 * (i + 1))


_INS = ['x', 'rel_bias', 'norm_gains', 'sb_w_qkv', 'sb_w_o', 'dil_w_qkv', 'dil_w_o', 'ffn_w_up', 'ffn_conv_w',
        'ffn_conv_b', 'ffn_w_down', 'c_2', 'ctx_2', 'c_ctx_2', 'w_ada_2', 'b_ada_2', 'g_norm1_2', 'g_norm2_2',
        'w_in_2', 'na_rpb_2', 'da_lam_q1_2', 'da_lam_k1_2', 'da_lam_q2_2', 'da_lam_k2_2', 'da_subln_g_2',
        'gm_ln_g_2', 'gm_ln_b_2', 'gm_w_s_2', 'gm_b_s_2', 'w_branch_2', 'w_out_2', 'w_router_2', 'w_e1_2',
        'w_e3_2', 'w_e2_2', 'g_final_2']


def kernel(**inputs):
    import concourse.bacc as bacc
    from concourse.bass_utils import run_bass_kernel_spmd as run

    nc = bacc.Bacc("TRN2", target_bir_lowering=False, num_devices=1)
    arrays, args = {}, {}
    given = {n: np.ascontiguousarray(inputs[n]) for n in _INS}
    given["const_table"] = constant_table()
    given["bucket_table"] = bucket_table()
    given["zero_table"] = np.zeros((NA_HEADS, 2 * NA_WIN_R - 1, P), np.float32)
    for name, v in given.items():
        arrays[f"in_{name}"] = v
        args[name] = nc.dram_tensor(f"in_{name}", v.shape, F32, kind="ExternalInput").ap()
    out = nc.dram_tensor("out", (1, S, D), F32, kind="ExternalOutput").ap()
    build(nc, args, out)
    r = run(nc, [arrays], core_ids=[0])
    return r.results[0]["out"]
```
